# Optimizing a Trainium2 kernel written in Bass

```python
import jax, jax.numpy as jnp
from jax import lax
import numpy as np

'''One inference step of a conditioned hybrid decoder trunk, for a prompt group and a sample group
that share the same weights.

Layer math (per layer, a single mixer sub-layer):
  shift, scale, gate = split(silu(c) @ w_ada + b_ada)                 (adaLN from conditioning c)
  h = RMSNorm(x) * (1 + scale) + shift
  z = h @ w_in   (ONE combined input projection; columns partitioned into
                  MLA q down-projection | MLA kv down-projection (latent + decoupled rotary key) |
                  dilated-attention q/k/v for 3 head groups | SiLU gate path A | SiLU gate path B |
                  merge gate A | merge gate B)
  branch A: multi-head latent attention (RMSNorm'd low-rank latent, QK-norm, decoupled rotary key)
  branch B: dilated sliding-window attention, head groups (128,1), (512,4), (2048,16) with QK-norm and
            full-head rotary, groups combined per position by their softmax denominators
  y_b = (branch_b * silu(gate_path_b)) @ w_p{a,b}                      (each branch to D_MODEL)
  x_out = x + gate * ((sigmoid(merge_a) * y_a + sigmoid(merge_b) * y_b) @ w_out)

Inputs:
  x_prompt (BATCH, SEQ, D_MODEL), positions 0..SEQ-1
  x_sample (DEC_BATCH, DEC_SEQ, D_MODEL), positions PAST_LEN..PAST_LEN+DEC_SEQ-1
  cache_mla (DEPTH, N_PHYS, PAGE_SIZE, MLA_KV_RANK + MLA_ROPE): paged pool of [latent c_kv | rotary key k_pe] rows
  cache_win{g} (DEPTH, DEC_BATCH, min(W_g, PAST_LEN), 2, DIL_HEADS, DIL_HEAD_DIM): last [k | v] rows of dilation group g
  page_table (DEC_BATCH, PAST_LEN // PAGE_SIZE) int32: logical page -> physical page of cache_mla
  c_prompt (BATCH, D_MODEL), c_sample (DEC_BATCH, D_MODEL); weights carry a leading DEPTH axis.
Returns the tuple
  (y_prompt      (BATCH, SEQ, D_MODEL),
   y_sample      (DEC_BATCH, DEC_SEQ, D_MODEL),
   mla_rows_prompt (DEPTH, BATCH, SEQ, MLA_KV_RANK + MLA_ROPE)            latent/rotary-key rows of every prompt token,
   win0_prompt   (DEPTH, BATCH, min(128, SEQ), 2, DIL_HEADS, DIL_HEAD_DIM)   final window buffers of the prompt,
   win1_prompt   (DEPTH, BATCH, min(512, SEQ), 2, DIL_HEADS, DIL_HEAD_DIM),
   win2_prompt   (DEPTH, BATCH, min(2048, SEQ), 2, DIL_HEADS, DIL_HEAD_DIM),
   mla_rows_sample (DEPTH, DEC_BATCH, DEC_SEQ, MLA_KV_RANK + MLA_ROPE)    rows to write into the paged pool,
   win0_sample   (DEPTH, DEC_BATCH, DEC_SEQ, 2, DIL_HEADS, DIL_HEAD_DIM)   new rows appended to each window buffer,
   win1_sample   (DEPTH, DEC_BATCH, DEC_SEQ, 2, DIL_HEADS, DIL_HEAD_DIM),
   win2_sample   (DEPTH, DEC_BATCH, DEC_SEQ, 2, DIL_HEADS, DIL_HEAD_DIM))
'''

D_MODEL = 1024
BATCH = 1
SEQ = 512
DEPTH = 1
DEC_BATCH = 8
DEC_SEQ = 1
PAST_LEN = 4096
PAGE_SIZE = 128

MLA_HEADS = 8
MLA_NOPE = 64
MLA_ROPE = 32
MLA_V = 64
MLA_Q_RANK = 384
MLA_KV_RANK = 256
MLA_QK = MLA_NOPE + MLA_ROPE
MLA_CACHE_W = MLA_KV_RANK + MLA_ROPE
MLA_SCALE = MLA_QK ** -0.5
DIL_PATTERNS = ((128, 1), (512, 4), (2048, 16))
N_DIL = len(DIL_PATTERNS)
DIL_HEADS = 4
DIL_HEAD_DIM = 64
DIL_SCALE = DIL_HEAD_DIM ** -0.5
A_WIDTH = MLA_HEADS * MLA_V
B_WIDTH = DIL_HEADS * DIL_HEAD_DIM
IN_SPLITS = (MLA_Q_RANK, MLA_CACHE_W, N_DIL * 3 * B_WIDTH, A_WIDTH, B_WIDTH, D_MODEL, D_MODEL)
IN_WIDTH = sum(IN_SPLITS)
ROPE_THETA = 10000.0
EPS = 1e-6
Q_BLOCK = 128

kernel_name = 'mla_dilated_gated_hybrid_step'

def _rms(x, g):
    xf = x.astype(jnp.float32)
    y = xf * lax.rsqrt(jnp.mean(xf * xf, axis=-1, keepdims=True) + EPS)
    return (y * g.astype(jnp.float32)).astype(x.dtype)

def _rope(x, pos):
    half = x.shape[-1] // 2
    inv = ROPE_THETA ** (-jnp.arange(half, dtype=jnp.float32) / half)
    ang = pos.astype(jnp.float32)[:, None] * inv[None, :]
    shape = (pos.shape[0],) + (1,) * (x.ndim - 3) + (half,)
    cos = jnp.cos(ang).reshape(shape)
    sin = jnp.sin(ang).reshape(shape)
    xf = x.astype(jnp.float32)
    x1, x2 = xf[..., :half], xf[..., half:]
    return jnp.concatenate([x1 * cos - x2 * sin, x2 * cos + x1 * sin], axis=-1).astype(x.dtype)

def _project(x, c, pos, norm_w, w_ada, b_ada, w_in, qa_norm, w_qb, kv_norm, qn_g, qr_g, kr_g, dq_g, dk_g):
    B, S, _ = x.shape
    shift, scale, res_gate = jnp.split(jax.nn.silu(c) @ w_ada + b_ada, 3, axis=-1)
    h = _rms(x, norm_w) * (1 + scale[:, None]) + shift[:, None]
    zq, zkv, zd, ga, gb, ma, mb = jnp.split(h @ w_in, np.cumsum(IN_SPLITS)[:-1].tolist(), axis=-1)
    q = (_rms(zq, qa_norm) @ w_qb).reshape(B, S, MLA_HEADS, MLA_QK)
    q_nope = _rms(q[..., :MLA_NOPE], qn_g)
    q_pe = _rope(_rms(q[..., MLA_NOPE:], qr_g), pos)
    rows = jnp.concatenate([_rms(zkv[..., :MLA_KV_RANK], kv_norm),
                            _rope(_rms(zkv[..., MLA_KV_RANK:], kr_g), pos)], axis=-1)
    zd = zd.reshape(B, S, N_DIL, 3, DIL_HEADS, DIL_HEAD_DIM)
    dq = _rope(_rms(zd[:, :, :, 0], dq_g[:, None]), pos)
    dk = _rope(_rms(zd[:, :, :, 1], dk_g[:, None]), pos)
    dv = zd[:, :, :, 2]
    return q_nope, q_pe, rows, dq, dk, dv, (ga, gb, ma, mb, res_gate)

def _mla_prompt(q_nope, q_pe, rows, w_uk, w_uv, kn_g):
    B, S, H, _ = q_nope.shape
    ckv = rows[..., :MLA_KV_RANK].astype(jnp.float32)
    kpe = rows[..., MLA_KV_RANK:].astype(jnp.float32)
    k_nope = _rms(jnp.einsum('bsr,rhe->bshe', ckv, w_uk.astype(jnp.float32)), kn_g)
    v = jnp.einsum('bsr,rhe->bshe', ckv, w_uv.astype(jnp.float32))
    nq = S // Q_BLOCK
    qn = q_nope.astype(jnp.float32).reshape(B, nq, Q_BLOCK, H, MLA_NOPE).transpose(1, 0, 2, 3, 4)
    qp = q_pe.astype(jnp.float32).reshape(B, nq, Q_BLOCK, H, MLA_ROPE).transpose(1, 0, 2, 3, 4)
    kpos = jnp.arange(S)

    def block(args):
        qn_b, qp_b, i = args
        s = (jnp.einsum('bqhe,bkhe->bhqk', qn_b, k_nope)
             + jnp.einsum('bqhe,bke->bhqk', qp_b, kpe)) * MLA_SCALE
        qpos = i * Q_BLOCK + jnp.arange(Q_BLOCK)
        s = jnp.where(kpos[None, :] <= qpos[:, None], s, -jnp.inf)
        return jnp.einsum('bhqk,bkhe->bqhe', jax.nn.softmax(s, axis=-1), v)

    o = lax.map(block, (qn, qp, jnp.arange(nq)))
    return o.transpose(1, 0, 2, 3, 4).reshape(B, S, H * MLA_V)

def _mla_sample(q_nope, q_pe, rows_new, pool, page_table, w_uk, w_uv, kn_g):
    Bd, T, H, _ = q_nope.shape
    qn = q_nope.astype(jnp.float32)
    qp = q_pe.astype(jnp.float32)
    wuk = w_uk.astype(jnp.float32)

    def attend(rows, mask):
        ckv = rows[..., :MLA_KV_RANK].astype(jnp.float32)
        kpe = rows[..., MLA_KV_RANK:].astype(jnp.float32)
        k_nope = _rms(jnp.einsum('bsr,rhe->bshe', ckv, wuk), kn_g)
        s = (jnp.einsum('bthe,bshe->bhts', qn, k_nope)
             + jnp.einsum('bthe,bse->bhts', qp, kpe)) * MLA_SCALE
        if mask is not None:
            s = jnp.where(mask, s, -jnp.inf)
        m = s.max(axis=-1)
        e = jnp.exp(s - m[..., None])
        return m, e.sum(axis=-1), jnp.einsum('bhts,bsr->bhtr', e, ckv)

    m_p, l_p, acc_p = lax.map(lambda p: attend(pool[page_table[:, p]], None),
                              jnp.arange(page_table.shape[1]))
    m_n, l_n, acc_n = attend(rows_new, jnp.tril(jnp.ones((T, T), dtype=bool)))
    m_all = jnp.maximum(m_p.max(axis=0), m_n)
    w_p = jnp.exp(m_p - m_all)
    w_n = jnp.exp(m_n - m_all)
    num = jnp.einsum('pbht,pbhtr->bhtr', w_p, acc_p) + w_n[..., None] * acc_n
    den = (w_p * l_p).sum(axis=0) + w_n * l_n
    lat = num / den[..., None]
    return jnp.einsum('bhtr,rhe->bthe', lat, w_uv.astype(jnp.float32)).reshape(Bd, T, H * MLA_V)

def _dilated_prompt(q, k, v, dilation, n_off):
    B, S, H, Dh = q.shape
    L = S // dilation
    nb = -(-L // n_off)
    pad = nb * n_off - L

    def to_blocks(t):
        t = t.reshape(B, L, dilation, H, Dh).transpose(0, 2, 1, 3, 4)
        t = jnp.pad(t, ((0, 0), (0, 0), (0, pad), (0, 0), (0, 0)))
        return t.reshape(B, dilation, nb, n_off, H, Dh)

    def with_prev(t):
        prev = jnp.pad(t, ((0, 0), (0, 0), (1, 0), (0, 0), (0, 0), (0, 0)))[:, :, :nb]
        return jnp.concatenate([prev, t], axis=3)

    qb = to_blocks(q)
    kx = with_prev(to_blocks(k))
    vx = with_prev(to_blocks(v))
    s = jnp.einsum('bgnqhe,bgnkhe->bgnhqk', qb, kx) * DIL_SCALE
    qi = jnp.arange(n_off)[:, None]
    kj = jnp.arange(2 * n_off)[None, :]
    dist = n_off + qi - kj
    band = (dist >= 0) & (dist <= n_off)
    has_prev = (jnp.arange(nb)[:, None, None] > 0) | (kj[None] >= n_off)
    s = jnp.where((band[None] & has_prev)[:, None], s, -jnp.inf)
    m = s.max(axis=-1)
    e = jnp.exp(s - m[..., None])
    l = e.sum(axis=-1)
    acc = jnp.einsum('bgnhqk,bgnkhe->bgnqhe', e, vx)

    def from_blocks(t):
        t = t.reshape((B, dilation, nb * n_off) + t.shape[4:])[:, :, :L]
        return jnp.swapaxes(t, 1, 2).reshape((B, S) + t.shape[3:])

    return (from_blocks(jnp.swapaxes(m, 3, 4)), from_blocks(jnp.swapaxes(l, 3, 4)), from_blocks(acc))

def _dilated_sample(q, k, v, buf, dilation, n_off):
    Wb = buf.shape[1]
    T = q.shape[1]
    kc = jnp.concatenate([buf[:, :, 0].astype(jnp.float32), k], axis=1)
    vc = jnp.concatenate([buf[:, :, 1].astype(jnp.float32), v], axis=1)
    idx = Wb + jnp.arange(T)[:, None] - dilation * jnp.arange(n_off + 1)[None, :]
    valid = idx >= 0
    idx = jnp.maximum(idx, 0)
    kg = kc[:, idx]
    vg = vc[:, idx]
    s = jnp.einsum('bthe,btjhe->bthj', q, kg) * DIL_SCALE
    s = jnp.where(valid[None, :, None, :], s, -jnp.inf)
    m = s.max(axis=-1)
    e = jnp.exp(s - m[..., None])
    return m, e.sum(axis=-1), jnp.einsum('bthj,btjhe->bthe', e, vg)

def _combine(stats):
    m = jnp.stack([st[0] for st in stats])
    l = jnp.stack([st[1] for st in stats])
    acc = jnp.stack([st[2] for st in stats])
    w = jnp.exp(m - m.max(axis=0))
    return (w[..., None] * acc).sum(axis=0) / (w * l).sum(axis=0)[..., None]

def _merge(x, o_a, o_b, ga, gb, ma, mb, res_gate, w_pa, w_pb, w_out):
    dt = x.dtype
    ya = (o_a.astype(dt) * jax.nn.silu(ga)) @ w_pa
    yb = (o_b.astype(dt) * jax.nn.silu(gb)) @ w_pb
    merged = jax.nn.sigmoid(ma) * ya + jax.nn.sigmoid(mb) * yb
    return x + res_gate[:, None] * (merged @ w_out)

def _layer_prompt(x, c, proj_w, attn_w, out_w):
    B, S, _ = x.shape
    pos = jnp.arange(S, dtype=jnp.int32)
    q_nope, q_pe, rows, dq, dk, dv, gates = _project(x, c, pos, *proj_w)
    w_uk, w_uv, kn_g = attn_w
    o_a = _mla_prompt(q_nope, q_pe, rows, w_uk, w_uv, kn_g)
    stats = [_dilated_prompt(dq[:, :, g].astype(jnp.float32), dk[:, :, g].astype(jnp.float32),
                             dv[:, :, g].astype(jnp.float32), dil, win // dil)
             for g, (win, dil) in enumerate(DIL_PATTERNS)]
    o_b = _combine(stats).reshape(B, S, B_WIDTH)
    y = _merge(x, o_a, o_b, *gates, *out_w)
    bufs = [jnp.stack([dk[:, :, g], dv[:, :, g]], axis=2)[:, S - min(win, S):]
            for g, (win, _) in enumerate(DIL_PATTERNS)]
    return y, rows, bufs

def _layer_sample(x, c, pool, page_table, bufs, proj_w, attn_w, out_w):
    B, T, _ = x.shape
    pos = PAST_LEN + jnp.arange(T, dtype=jnp.int32)
    q_nope, q_pe, rows, dq, dk, dv, gates = _project(x, c, pos, *proj_w)
    w_uk, w_uv, kn_g = attn_w
    o_a = _mla_sample(q_nope, q_pe, rows, pool, page_table, w_uk, w_uv, kn_g)
    stats = [_dilated_sample(dq[:, :, g].astype(jnp.float32), dk[:, :, g].astype(jnp.float32),
                             dv[:, :, g].astype(jnp.float32), bufs[g], dil, win // dil)
             for g, (win, dil) in enumerate(DIL_PATTERNS)]
    o_b = _combine(stats).reshape(B, T, B_WIDTH)
    y = _merge(x, o_a, o_b, *gates, *out_w)
    new_rows = [jnp.stack([dk[:, :, g], dv[:, :, g]], axis=2) for g in range(N_DIL)]
    return y, rows, new_rows

def setup_inputs(seed: int = 0) -> dict:
    key = jax.random.key(seed)
    ks = jax.random.split(key, 32)
    f32 = jnp.float32
    L = DEPTH
    n_pages = PAST_LEN // PAGE_SIZE
    n_used = DEC_BATCH * n_pages
    n_phys = n_used + max(1, n_used // 4)

    def nrm(k, shape, scale):
        return jax.random.normal(k, shape, f32) * scale

    def gain(k, shape):
        return 1.0 + 0.05 * jax.random.normal(k, shape, f32)

    def win_buf(k, w):
        return nrm(k, (L, DEC_BATCH, min(w, PAST_LEN), 2, DIL_HEADS, DIL_HEAD_DIM), 1.0)

    page_table = jax.random.permutation(ks[6], n_phys)[:n_used].reshape(DEC_BATCH, n_pages).astype(jnp.int32)
    return {
        'x_prompt': nrm(ks[0], (BATCH, SEQ, D_MODEL), 1.0),
        'x_sample': nrm(ks[1], (DEC_BATCH, DEC_SEQ, D_MODEL), 1.0),
        'cache_mla': nrm(ks[2], (L, n_phys, PAGE_SIZE, MLA_CACHE_W), 1.0),
        'cache_win0': win_buf(ks[3], DIL_PATTERNS[0][0]),
        'cache_win1': win_buf(ks[4], DIL_PATTERNS[1][0]),
        'cache_win2': win_buf(ks[5], DIL_PATTERNS[2][0]),
        'page_table': page_table,
        'c_prompt': nrm(ks[7], (BATCH, D_MODEL), 1.0),
        'c_sample': nrm(ks[8], (DEC_BATCH, D_MODEL), 1.0),
        'norm_w': gain(ks[9], (L, D_MODEL)),
        'w_ada': nrm(ks[10], (L, D_MODEL, 3 * D_MODEL), D_MODEL ** -0.5),
        'b_ada': nrm(ks[11], (L, 3 * D_MODEL), 0.02),
        'w_in': nrm(ks[12], (L, D_MODEL, IN_WIDTH), D_MODEL ** -0.5),
        'mla_qa_norm': gain(ks[13], (L, MLA_Q_RANK)),
        'w_qb': nrm(ks[14], (L, MLA_Q_RANK, MLA_HEADS * MLA_QK), MLA_Q_RANK ** -0.5),
        'mla_kv_norm': gain(ks[15], (L, MLA_KV_RANK)),
        'w_uk': nrm(ks[16], (L, MLA_KV_RANK, MLA_HEADS, MLA_NOPE), MLA_KV_RANK ** -0.5),
        'w_uv': nrm(ks[17], (L, MLA_KV_RANK, MLA_HEADS, MLA_V), MLA_KV_RANK ** -0.5),
        'mla_qn_g': gain(ks[18], (L, MLA_NOPE)),
        'mla_qr_g': gain(ks[19], (L, MLA_ROPE)),
        'mla_kn_g': gain(ks[20], (L, MLA_NOPE)),
        'mla_kr_g': gain(ks[21], (L, MLA_ROPE)),
        'dil_q_g': gain(ks[22], (L, N_DIL, DIL_HEAD_DIM)),
        'dil_k_g': gain(ks[23], (L, N_DIL, DIL_HEAD_DIM)),
        'w_pa': nrm(ks[24], (L, A_WIDTH, D_MODEL), A_WIDTH ** -0.5),
        'w_pb': nrm(ks[25], (L, B_WIDTH, D_MODEL), B_WIDTH ** -0.5),
        'w_out': nrm(ks[26], (L, D_MODEL, D_MODEL), D_MODEL ** -0.5),
    }

def reference(x_prompt, x_sample, cache_mla, cache_win0, cache_win1, cache_win2, page_table, c_prompt, c_sample,
              norm_w, w_ada, b_ada, w_in, mla_qa_norm, w_qb, mla_kv_norm, w_uk, w_uv, mla_qn_g, mla_qr_g,
              mla_kn_g, mla_kr_g, dil_q_g, dil_k_g, w_pa, w_pb, w_out):
    h_p, h_s = x_prompt, x_sample
    rows_p, rows_s, win_p, win_s = [], [], [], []
    for l in range(DEPTH):
        proj_w = (norm_w[l], w_ada[l], b_ada[l], w_in[l], mla_qa_norm[l], w_qb[l], mla_kv_norm[l],
                  mla_qn_g[l], mla_qr_g[l], mla_kr_g[l], dil_q_g[l], dil_k_g[l])
        attn_w = (w_uk[l], w_uv[l], mla_kn_g[l])
        out_w = (w_pa[l], w_pb[l], w_out[l])
        h_p, r_p, b_p = _layer_prompt(h_p, c_prompt, proj_w, attn_w, out_w)
        h_s, r_s, b_s = _layer_sample(h_s, c_sample, cache_mla[l], page_table,
                                      (cache_win0[l], cache_win1[l], cache_win2[l]), proj_w, attn_w, out_w)
        rows_p.append(r_p)
        rows_s.append(r_s)
        win_p.append(b_p)
        win_s.append(b_s)
    mla_rows_prompt = jnp.stack(rows_p)
    win0_prompt = jnp.stack([b[0] for b in win_p])
    win1_prompt = jnp.stack([b[1] for b in win_p])
    win2_prompt = jnp.stack([b[2] for b in win_p])
    mla_rows_sample = jnp.stack(rows_s)
    win0_sample = jnp.stack([b[0] for b in win_s])
    win1_sample = jnp.stack([b[1] for b in win_s])
    win2_sample = jnp.stack([b[2] for b in win_s])
    return (h_p, h_s, mla_rows_prompt, win0_prompt, win1_prompt, win2_prompt,
            mla_rows_sample, win0_sample, win1_sample, win2_sample)


_drawn_inputs = setup_inputs


def setup_inputs(seed=0):
    import zlib

    import numpy as np

    out = dict(_drawn_inputs(seed))
    spreads = {}
    factors = {'cache_mla': 8.0,
     'cache_win0': 4.457,
     'cache_win1': 4.238,
     'cache_win2': 4.335,
     'mla_qa_norm': 8.0,
     'mla_qn_g': 8.0,
     'mla_qr_g': 8.0,
     'mla_kn_g': 8.0,
     'mla_kr_g': 5.434,
     'dil_q_g': 8.0}
    for name, (base, spread) in spreads.items():
        noise = np.random.default_rng([zlib.crc32(name.encode()), seed]).standard_normal(out[name].shape)
        drawn = base * np.exp(spread * noise) if base else spread * noise
        out[name] = __import__('jax').numpy.asarray(drawn.astype(out[name].dtype))
    for name, factor in factors.items():
        out[name] = (out[name] * factor).astype(out[name].dtype)
    return out
```

```python
from contextlib import ExitStack

import numpy as np

import concourse.bass as bass
from concourse import mybir

P = 128
F32 = mybir.dt.float32
F32R = mybir.dt.float32r
I32 = mybir.dt.int32
ALU = mybir.AluOpType
ACT = mybir.ActivationFunctionType
AX = mybir.AxisListType.X

D = 1024
S = 512
NT = S // P
TS = NT
NB = 8
PAST = 4096
NPAGE = PAST // P
HM, NOPE, ROPE = 8, 64, 32
QK = NOPE + ROPE
QR, KVR = 384, 256
CW = KVR + ROPE
ND, HD, DH = 3, 4, 64
BW = HD * DH
AW = HM * 64
PATTERNS = ((128, 1), (512, 4), (2048, 16))
MLA_SCALE = QK ** -0.5
DIL_SCALE = DH ** -0.5
EPS = 1e-6
NEG = -1e30
RSQRT_MAGIC = float(0x5F3759DF)
KD = D // P
LO = 64

C_Q, C_KV, C_D = 0, QR, QR + CW
C_GA = C_D + ND * 3 * BW
C_GB = C_GA + AW
C_MA = C_GB + BW
C_MB = C_MA + D

G_KV, G_KR, G_QN, G_KN, G_QR, G_DQ, G_DK = 0, 256, 288, 352, 416, 448, 640
G_ALL = 832

M_CAUSAL = 3 * P
M_R4, M_R16, M_PREV = 4 * P, 8 * P, 12 * P
M_ALL = 14 * P

BLOCKS = ([(f"ada{n}", "w_ada", 0, KD, n * 512, 512) for n in range(6)]
          + [("Q", "w_in", 0, KD, C_Q, QR), ("KV", "w_in", 0, KD, C_KV, CW)]
          + [(f"QB{i}", "w_qb", 0, QR // P, i * 384, 384) for i in range(2)]
          + [("V", "w_uv", 0, KVR // P, 0, AW)])
for _g in range(ND):
    BLOCKS += [(f"D{_g}QK", "w_in", 0, KD, C_D + _g * 3 * BW, 2 * BW),
               (f"D{_g}V", "w_in", 0, KD, C_D + _g * 3 * BW + 2 * BW, BW)]
BLOCKS += [("GA", "w_in", 0, KD, C_GA, AW), ("GB", "w_in", 0, KD, C_GB, BW)]
BLOCKS += [(f"P{_b}{n}", f"w_p{_b.lower()}", 0, k, n * 512, 512)
           for n in range(2) for _b, k in (("A", AW // P), ("B", BW // P))]
BLOCKS += [(f"M{_b}{n}", "w_in", 0, KD, c + n * 512, 512)
           for n in range(2) for _b, c in (("A", C_MA), ("B", C_MB))]
BLOCKS += [(f"WO{n}", "w_out", 0, KD, n * 512, 512) for n in range(2)]
BLOCKS += [(f"P{_b}s{n}", f"w_p{_b.lower()}", 0, k, n * 512, 512)
           for n in range(2) for _b, k in (("A", AW // P), ("B", BW // P))]
BLOCKS += [(f"WOs{n}", "w_out", 0, KD, n * 512, 512) for n in range(2)]
CHUNKS = []
FIRST = {}
COUNT = {}
WIDTH = {}
for _name, _w, _k0, _nk, _c, _width in BLOCKS:
    FIRST[_name], COUNT[_name], WIDTH[_name] = len(CHUNKS), _nk, _width
    CHUNKS += [(_w, k, _c, _width) for k in range(_nk)]

STAGES = ([("ada0", 1, "A"), ("ada1", 1, "A"), ("wukT", 2, "A"), ("xT", KD, "A")]
          + [(f"ada{n}", 1, "A") for n in range(2, 6)]
          + [("gate", 2, "A"), ("Q", 5, "A"), ("KV", 5, "A"), ("Tq", 3, "D"), ("QB0", 5, "A"), ("QB1", 5, "A"),
             ("Tr", 2, "D"), ("K", 5, "A"), ("V", 4, "A"), ("TqM", 8, "A"), ("TkM", 8, "A")])
for _g in range(ND):
    STAGES += [(f"D{_g}QK", 5, "A"), (f"D{_g}V", 5, "A")]
STAGES += [("TD", 4 * ND, "A"), ("GA", 4, "D"), ("GAs", 1, "A"), ("GB", 4, "D"), ("GBs", 1, "A"), ("To", 6, "D")]
STAGES += [(f"P{b}{n}", 4, "A") for n in range(2) for b in "AB"]
STAGES += [(f"M{b}{n}", 5, "A") for n in range(2) for b in "AB"]
STAGES += [("Tm", KD, "D"), ("WO0", 4, "A"), ("WO1", 4, "A")]
STAGES += [(f"P{b}s{n}", 1, "A") for n in range(2) for b in "AB"] + [("WOs0", 1, "A"), ("WOs1", 1, "A")]
ITEM = {}
READER = []
_seen = {"A": 0, "D": 0}
for _name, _n, _e in STAGES:
    ITEM[_name] = len(READER)
    for _ in range(_n):
        _seen[_e] += 1
        READER.append((_e, _seen[_e]))
BANKS = 7
LAST_ITEM = {n: ITEM[n] + c - 1 for n, c, _ in STAGES}
LAST_ITEM["GA"], LAST_ITEM["GB"] = ITEM["GAs"], ITEM["GBs"]
END_ITEM = {}
for _name, *_ in BLOCKS:
    END_ITEM[FIRST[_name] + COUNT[_name] - 1] = LAST_ITEM[_name]
NRAW, NHL = 4, 3
NSTAGE = 5

MLA_JOBS = [(i, h, i + 1) for i in range(NT) for h in range(HM)]
DIL_JOBS = [(i, h, (1 if i == 0 else 2) + 2 * (i + 1)) for i in range(NT) for h in range(HD)]


def widths(nb):
    return [min(4, nb - c) for c in range(0, nb, 4)]


CHUNK_END = [int(n) for n in np.cumsum([len(widths(j[2])) for j in MLA_JOBS + DIL_JOBS])]
N_MLA_CHUNKS = CHUNK_END[len(MLA_JOBS) - 1]

SMP_Q, SMP_R, SMP_KV = 1, 2, 3
F_MAX, F_DIAG, F_SUB, F_SUM, F_OBT, F_OG, F_OST, F_MS, F_MST, F_Y = range(1, 11)
LSTEPS = 39


def trunk_step(nc, x_prompt, x_sample, cache_mla, cw0, cw1, cw2, page_table, c_prompt, c_sample, b_ada,
               w_ada, w_in, w_qb, w_uk, w_uv, w_pa, w_pb, w_out, gains, cols, tables, rope,
               y_prompt, y_sample, rows_p, win0_p, win1_p, win2_p, rows_s, win0_s, win1_s, win2_s):
    weights = dict(w_ada=w_ada, w_in=w_in, w_qb=w_qb, w_uv=w_uv, w_pa=w_pa, w_pb=w_pb, w_out=w_out)
    ctx = ExitStack()
    with ctx:
        def sem(name):
            return ctx.enter_context(nc.semaphore(name))

        at = [16512]

        def region(nbytes):
            at[0] += nbytes
            assert at[0] <= 229344, at[0]
            return at[0] - nbytes

        def put(name, shape, offset, dt=F32):
            return nc.alloc_sbuf_tensor_at(name, [shape[0], int(np.prod(shape[1:]))], dt, offset=offset)

        def new(name, shape, dt=F32):
            n = int(np.prod(shape[1:])) * 4
            return put(name, shape, region((n + 31) // 32 * 32), dt)

        def v3(t, a, b):
            return t[:, :].rearrange("p (a b) -> p a b", a=a, b=b)

        def v4(t, a, b, c):
            return t[:, :].rearrange("p (a b c) -> p a b c", a=a, b=b, c=c)

        tab = new("tab", [P, P + M_ALL + 8])
        ident = tab[:, 0:P]
        masks = tab[:, P:P + M_ALL]
        newmask = tab[0:NB, P + M_ALL:P + M_ALL + 8]
        ones = new("ones", [P, P])
        ropes_t = new("ropes", [P, 5 * 192])
        ropes = v3(ropes_t, 5, 192)
        gn = new("gn", [P, G_ALL])
        g96 = new("g96", [P, QK])
        colt = new("colt", [P, 11])
        raw_t = new("raw", [P, NRAW * 512])
        raw = v3(raw_t, NRAW, 512)
        whi_t = new("whi", [P, NHL * 512], F32R)
        whi = v3(whi_t, NHL, 512)
        wlo_t = new("wlo", [P, NHL * 512], F32R)
        wlo = v3(wlo_t, NHL, 512)
        wuk_hi_t = new("wuk_hi", [P, 2 * 512], F32R)
        wuk_hi = v3(wuk_hi_t, 2, 512)
        wuk_lo_t = new("wuk_lo", [P, 2 * 512], F32R)
        wuk_lo = v3(wuk_lo_t, 2, 512)
        hTs_t = new("hTs", [P, KD * P], F32R)
        hTs = v3(hTs_t, KD, P)
        rows_t = new("rows", [P, 5 * CW])
        rows = v3(rows_t, 5, CW)
        gate_bc = new("gate_bc", [P, D])
        gate_s = new("gate_s", [NB, D])
        q_s = new("q_s", [NB, HM * QK])
        kv_s_t = new("kv_s", [NB, ND * 512])
        kv_s = v3(kv_s_t, ND, 512)
        dq_s_t = new("dq_s", [NB, ND * BW])
        dq_s = v3(dq_s_t, ND, BW)
        small = region(4096)
        ms = put("ms", [P, 32], small)
        rsx = put("rsx", [P, 32], small + 128)
        rsa = put("rsa", [P, 32], small + 256)
        rsy = put("rsy", [P, 32], small + 384)
        pe1 = put("pe1", [P, 128], small + 512)
        pe2 = put("pe2", [P, 128], small + 1024)
        amax = put("amax", [P, 8], small + 1536)
        flag = put("flag", [1, 8], small + 2848)
        mx1 = put("mx1", [32, 1], small + 2880)
        dgm = put("dgm", [32, 32], small + 2944)
        dns = put("dns", [NB, 8], small + 2816)
        qsT = put("qsT", [P, 32], small + 1920)
        lsum = put("lsum", [P, 4], small + 1600)
        snew = put("snew", [NB, NB * HM], small + 1664)
        qabs_f = put("qabs_f", [P, 2 * NB * HM], small + 2048)
        qpe = put("qpe", [ROPE, NB * HM], small + 2048 + 512)
        qabs_t = put("qabs", [P, 2 * NB * 16], small + 3072, F32R)
        qabs = v4(qabs_t, 2, NB, 16)

        W = region(22 * 1024)
        stage_t = put("stage", [P, NSTAGE * 512], W)
        stage = v3(stage_t, NSTAGE, 512)
        sqt = put("sqt", [P, 512], W + 10240)
        tmp_t = put("tmp", [P, 5 * 512], W + 12288)
        tmp = v3(tmp_t, 5, 512)
        PT_t = put("PT", [P, 3 * 512], W + 12288)
        PT = v3(PT_t, 3, 512)
        wukT_t = put("wukT", [P, 4 * KVR], W + 12288)
        wukT = v3(wukT_t, 4, KVR)
        qn_s = put("qn_s", [NB, HM * NOPE], W + 12288 + 4 * 1792)
        k_s = put("k_s", [NB, HM * QK], W + 16384)
        low_s = new("low_s", [NB + 1, 512])

        ON = region(12 * 1024)
        HT = region(32 * 1024)
        V = region(229344 - at[0])
        K1 = 1024
        assert 229344 - V >= 62.75 * K1, 229344 - V
        oN = v3(put("oN", [P, NT * 768], ON), NT, 768)
        hThi = v3(put("hT_hi", [P, KD * S], HT, F32R), KD, S)
        hTlo = v3(put("hT_lo", [P, KD * S], HT + 16 * K1, F32R), KD, S)
        wukr = v3(put("wuk_raw", [P, 2 * 512], ON), 2, 512)
        xsq = put("xsq", [P, D], ON + 4 * K1)
        xT = v3(put("xT", [P, KD * S], HT + 16 * K1), KD, S)
        xt = v3(put("x_tiles", [P, NT * D], V), NT, D)
        xs1 = put("x_s1", [NB, D], V + 16 * K1)
        cs = v3(put("c_split", [P, KD * P], V + 20 * K1, F32R), KD, P)
        c9 = put("c9", [NB + 1, D], V + 24 * K1)
        c9b = put("c9b", [NB + 1, D], V + 28 * K1)
        ada = put("ada", [NB + 1, 3 * D], V + 32 * K1)
        bada = put("bada", [NB + 1, 3 * D], V + 44 * K1)
        xTs = put("xTs", [P, KD * NB], V + 56 * K1)
        G1 = v3(put("G1", [P, KD * 9], V + 57 * K1), KD, 9)
        SH = v3(put("SH", [P, KD * 9], V + 57 * K1 + 512), KD, 9)
        hs_f = v3(put("hs_f", [P, KD * NB], V + 58 * K1), KD, NB)
        qh = v3(put("qh", [P, 8 * 384], ON), 8, 384)
        qan = v3(put("qan", [P, 5 * QR], V), 5, QR)
        qTm = v3(put("qTm", [QK, HM * S], V), HM, S)
        kTm = v3(put("kTm", [QK, HM * S], V + 16 * K1), HM, S)
        vm = v3(put("v_mla", [P, NT * AW], V + 32 * K1), NT, AW)
        qaThi = v3(put("qaT_hi", [P, 3 * S], V + 16 * K1, F32R), 3, S)
        qaTlo = v3(put("qaT_lo", [P, 3 * S], V + 22 * K1, F32R), 3, S)
        qaTs = v3(put("qaTs", [P, 3 * P], V + 28 * K1, F32R), 3, P)
        rTs = v3(put("rTs", [P, 2 * P], V + 30 * K1, F32R), 2, P)
        rThi = v3(put("rT_hi", [P, 2 * S], V + 40 * K1, F32R), 2, S)
        rTlo = v3(put("rT_lo", [P, 2 * S], V + 44 * K1, F32R), 2, S)
        kc = v3(put("kc", [P, NT * HM * QK], V + 48 * K1), NT, HM * QK)
        Pm = v3(put("probs", [P, 2 * 1280], V + 48 * K1), 2, 1280)
        kvo = v4(put("kvo", [P, ND * NT * 512], V), ND, NT, 512)
        dqT = v4(put("dqT", [P, ND * 2 * S], V + 24 * K1), ND, 2, S)
        dkT = v4(put("dkT", [P, ND * 2 * S], V + 36 * K1), ND, 2, S)
        dqn = v4(put("dqn", [P, ND * NT * BW], V + 48 * K1), ND, NT, BW)
        oThi = v3(put("oT_hi", [P, 6 * S], V, F32R), 6, S)
        oTlo = v3(put("oT_lo", [P, 6 * S], V + 12 * K1, F32R), 6, S)
        ya = v3(put("ya", [P, NT * D], V + 24 * K1), NT, D)
        yb = v3(put("yb", [P, NT * D], V + 40 * K1), NT, D)
        merge_s = put("merge_gates_s", [NB, 2 * D], V)
        mix_s = put("mix_gates_s", [NB, 768], V + 59 * K1 + 768)
        xr = [v3(put("x_again0", [P, NT * 512], V + 44 * K1), NT, 512),
              v3(put("x_again1", [P, NT * 512], ON), NT, 512)]
        cn = [v3(put(f"cn{p}", [P, NPAGE * CW], (V + 8 * K1, ON)[p]), NPAGE, CW) for p in range(2)]
        cThi = v3(put("cT_hi", [P, 2 * 1024], W, F32R), 2, 1024)
        cTlo = v3(put("cT_lo", [P, 2 * 1024], W + 8 * K1, F32R), 2, 1024)
        sq4 = v3(put("sq4", [P, 4 * 512], V + 44 * K1), 4, 512)
        kpT = v3(put("kpT", [ROPE, 2 * 512], V + 52 * K1), 2, 512)
        HE = HT + 24 * K1
        Sr = v3(put("s_parts", [P, NPAGE * 24], HE), NPAGE, 24)
        ssq = put("ssq", [P, NPAGE * HM], HE + 3 * K1)
        lx = put("lx", [P, 128], HE + 4 * K1)
        lax = put("lax", [P, 128], HE + 4 * K1 + 512)
        ly = put("ly", [P, 128], HE + 5 * K1)
        Sc_t = put("scores", [P, 33 * HM], HE + 5 * K1 + 512)
        Sc = v3(Sc_t, 33, HM)
        Ex_t = put("expd", [P, 33 * HM], HE + 6 * K1 + 768)
        Ex = v3(Ex_t, 33, HM)
        latT = put("latT", [P, NB * 16], V + 56 * K1)
        pmx = put("pmx", [P, 8], V + 57 * K1)
        pt = put("pt", [1, NB * NPAGE], V + 58 * K1, I32)
        esm = put("esm", [P, 8], V + 57 * K1 + 256)
        rdn = put("rdn", [P, 8], V + 57 * K1 + 288)
        sdk0 = v3(put("sdk0", [P, 18 * 512], V + 8 * K1), 18, 512)
        sdk1 = v3(put("sdk1", [P, 6 * 512], V + 44 * K1), 6, 512)
        wuvr = v3(put("wuv_raw", [P, 2 * 512], ON), 2, 512)
        prod = v3(put("prod", [P, 2 * 768], ON + 4 * K1), 2, 768)
        SD_t = put("sd", [P, NB * 24], ON + 10 * K1)
        SD = v3(SD_t, NB, 24)
        ED_t = put("ed", [P, NB * 24], ON + 11 * K1)
        dn = put("dn", [NB, 16], ON + 12 * K1)
        dpm = put("dpm", [P, 32], ON + 12 * K1 + 64)
        dsm = put("dsm", [P, 32], ON + 12 * K1 + 192)
        rl = put("rl", [P, 32], ON + 12 * K1 + 320)
        obT = put("obT", [P, 2 * NB], ON + 12 * K1 + 448)
        osT = v3(put("osT", [P, 6 * P], ON + 13 * K1, F32R), 6, P)
        og = put("og", [NB, 768], ON + 16 * K1)
        sgm = put("sgm", [NB, 768], ON + 19 * K1)
        mgm = put("mgm", [NB, 2 * D], ON + 22 * K1)
        yab = v3(put("yab", [NB, 2 * D], ON + 30 * K1), 2, D)
        xs2 = put("x_s2", [NB, D], ON + 38 * K1)

        ps = ctx.enter_context(nc.psum_tensor("ps", [P, 8, 512], F32))

        def psw(bank, w):
            return ps[:, :, :].rearrange("p b c -> p (b c)")[:, bank * 512:bank * 512 + w]

        consts_in, c_in, wuk_in, bada_in = sem("consts_in"), sem("c_in"), sem("wuk_in"), sem("bada_in")
        x_in = [sem(f"x_in{t}") for t in range(5)]
        raw_in = [sem(f"raw_in{i}") for i in range(NRAW)]
        w_hi_ready, w_lo_ready, w_used = sem("w_hi_ready"), sem("w_lo_ready"), sem("w_used")
        z_done = sem("z_done")
        evac_a, evac_d = sem("evac_a"), sem("evac_d")
        act_half = sem("act_half")
        stage_free = sem("stage_free")
        even_done = sem("even_done")
        misc_done, misc_free = sem("misc_done"), sem("misc_free")
        dve_step = sem("dve_step")
        pool_step = sem("pool_step")
        zeroed, sigm_c, csilu, cs_ready, wuk_h, wuk_split = (
            sem("zeroed"), sem("sigm_c"), sem("csilu"), sem("cs_ready"), sem("wuk_h"), sem("wuk_split"))
        xn_ready, ada_ready, h_f, h_hi, h_ready = (
            sem("xn_ready"), sem("ada_ready"), sem("h_f"), sem("h_hi"), sem("h_ready"))
        qan_ready, rows_ready, qh_ready, kc_ready = (
            sem("qan_ready"), sem("rows_ready"), sem("qh_ready"), sem("kc_ready"))
        smp_ready = sem("smp_ready")
        y_roped, rope_done = sem("y_roped"), sem("rope_done")
        qk_done, masked, exp_done, tr_done, trp_done, pt_a, pt_d, pv_chunk, o_done = (
            sem("qk_done"), sem("masked"), sem("exp_done"), sem("tr_done"), sem("trp_done"), sem("pt_a"),
            sem("pt_d"), sem("pv_chunk"), sem("o_done"))
        rows_out, win_out, y_rdy, pt_in = sem("rows_out"), sem("win_out"), sem("y_rdy"), sem("pt_in")
        gated, merged = sem("gated"), sem("merged")
        xr_in = [sem(f"xr_in{n}") for n in range(2)]
        y_out = [sem(f"y_out{n}") for n in range(2)]
        cn_in = [[sem(f"cn_in{p}{q}") for q in range(4)] for p in range(2)]
        ct_done, ct_hi, ct_ready, k_done, sq_done, red_done, s_done, s_read = (
            sem("ct_done"), sem("ct_hi"), sem("ct_ready"), sem("k_done"), sem("sq_done"), sem("red_done"),
            sem("s_done"), sem("s_read"))
        pm_ready, pmT_done, dg_ready, mx_done, sub_done, ex_done, es_ready, pv_done, lat_done, lstep = (
            sem("pm_ready"), sem("pmT_done"), sem("dg_ready"), sem("mx_done"), sem("sub_done"), sem("ex_done"),
            sem("es_ready"), sem("pv_done"), sem("lat_done"), sem("lstep"))
        sdk_in = [sem("sdk_in0"), sem("sdk_in1")]
        late_in = sem("late_in")
        qb_done, qb_read, f_pe, f_dve, f_act = (
            sem("qb_done"), sem("qb_read"), sem("f_pe"), sem("f_dve"), sem("f_act"))
        s_out = sem("s_out")

        def rep(ap, axis, n):
            u = ap.unsqueeze(axis)
            shape = list(u.shape)
            shape[axis] = n
            return u.to_broadcast(shape)

        def wait_used(eng, j):
            if j in END_ITEM:
                eng.wait_ge(z_done, END_ITEM[j] + 1)
            else:
                eng.wait_ge(w_used, sum(1 for i in range(j + 1) if i not in END_ITEM))

        def wait_evac(eng, idx):
            e, n = READER[idx]
            eng.wait_ge(evac_a if e == "A" else evac_d, n)

        def pt_copy(eng, fn, chunk, w, signal, extra):
            eng.wait_ge(trp_done, chunk + 1)
            if chunk >= 3:
                eng.wait_ge(pv_chunk, chunk - 2)
            fn(PT[:, chunk % 3, 0:w * P], ps[:, 6 + chunk % 2, 0:w * P], *extra).then_inc(signal, 1)

        def wait_pt(eng, c):
            if c % 2 == 0:
                eng.wait_ge(pt_d, c // 2 + 1)
            else:
                eng.wait_ge(pt_a, (c + 1) // 2)

        def lanes(t):
            return NB if t == TS else P

        block = ctx.enter_context(nc.Block())

        @block.sync
        def _(sp):
            done = [0]

            def stream_to(last):
                while done[0] < min(last, len(CHUNKS)):
                    j = done[0]
                    w, k, c, width = CHUNKS[j]
                    if j >= NRAW:
                        sp.wait_ge(w_lo_ready, j - NRAW + 1)
                    sp.dma_start(raw[:, j % NRAW, 0:width], weights[w][k * P:(k + 1) * P, c:c + width])\
                      .then_inc(raw_in[j % NRAW], 16)
                    done[0] += 1

            def load_page(p, quarter, index, tile, summed=None):
                page = sp.value_load(pt[0:1, bass.ds(index, 1)], min_val=0, max_val=cache_mla.shape[0] - 1)
                if summed is not None:
                    sp.wait_ge(pv_done, summed + 1)
                sp.dma_start(cn[p][:, bass.ds(tile, 1), :],
                             cache_mla[bass.ds(page, 1), :, :].rearrange("a p c -> p a c"))\
                  .then_inc(cn_in[p][quarter], 16)

            sp.dma_start(c9[0:NB, :], c_sample).then_inc(c_in, 16)
            sp.dma_start(c9[NB:NB + 1, :], c_prompt).then_inc(c_in, 16)
            sp.dma_start(tab[:, :], tables).then_inc(consts_in, 16)
            sp.dma_start(colt[:, :], cols).then_inc(consts_in, 16)
            stream_to(NRAW)
            sp.dma_start(wukr[:, :, :], w_uk.rearrange("(k p) n -> p k n", p=P)).then_inc(wuk_in, 16)
            sp.dma_start(bada[:, :], b_ada.rearrange("(a n) -> a n", a=1).to_broadcast([NB + 1, 3 * D]))\
              .then_inc(bada_in, 16)
            sp.dma_start(ropes[:, 0:NT, :], rope[0:S, :].rearrange("(t p) c -> p t c", p=P)).then_inc(consts_in, 16)
            sp.dma_start(ropes[0:NB, TS, :], rope[S:S + NB, :]).then_inc(consts_in, 16)
            sp.dma_start(gn[:, :], gains.rearrange("(a n) -> a n", a=1).to_broadcast([P, G_ALL]))\
              .then_inc(consts_in, 16)
            stream_to(FIRST["WO0"])
            sp.wait_ge(z_done, ITEM["To"] + 1)
            sp.dma_start(pt[:, :], page_table.rearrange("b n -> (b n)").rearrange("(a n) -> a n", a=1))\
              .then_inc(pt_in, 16)
            stream_to(FIRST["WO0"] + NRAW)
            sp.wait_ge(pt_in, 16)
            sp.wait_ge(z_done, LAST_ITEM["Tm"] + 1)
            n = 0
            for j in range(FIRST["WO0"] + NRAW, FIRST["PAs0"]):
                stream_to(j + 1)
                for _ in range(3):
                    if n < NPAGE:
                        load_page(0, n // 8, n, n)
                        n += 1
            stream_to(FIRST["PAs0"] + NRAW)
            sp.wait_ge(z_done, LAST_ITEM["WO1"] + 1)
            sp.wait_ge(y_out[1], 16)
            for quarter in range(4):
                with sp.Fori(0, 8) as u:
                    load_page(1, quarter, NPAGE + 8 * quarter + u, 8 * quarter + u)
            with sp.Fori(0, (NB - 2) // 2) as i:
                for p in range(2):
                    for quarter in range(4):
                        with sp.Fori(0, 8) as u:
                            load_page(p, quarter, 2 * NPAGE * i + (2 + p) * NPAGE + 8 * quarter + u, 8 * quarter + u,
                                      2 * i + p)
            wins = [cw[:, :, :].rearrange("b (r s) c -> r b s c", s=dil)[:, :, 0, :]
                    for cw, (_, dil) in zip((cw0, cw1, cw2), PATTERNS)]
            sp.wait_ge(pv_done, NB - 1)
            for g in range(ND):
                sp.dma_start(sdk0[:, :, :].rearrange("p (b g) c -> p b g c", g=ND)[:, :, g, :],
                             wins[g][:, 0:6, :]).then_inc(sdk_in[0], 16)
            sp.wait_ge(pv_done, NB)
            sp.wait_ge(red_done, NB * NPAGE)
            sp.wait_ge(ct_ready, NB * 8)
            for g in range(ND):
                sp.dma_start(sdk1[:, :, :].rearrange("p (b g) c -> p b g c", g=ND)[:, :, g, :],
                             wins[g][:, 6:8, :]).then_inc(sdk_in[1], 16)
            sp.dma_start(wuvr[:, :, :], w_uv.rearrange("(k p) n -> p k n", p=P)).then_inc(late_in, 16)
            sp.dma_start(xs2[:, :], x_sample).then_inc(late_in, 16)
            stream_to(len(CHUNKS))
            sp.wait_ge(f_dve, F_Y)
            sp.dma_start(y_sample, xs2[:, :]).then_inc(s_out, 16)
            sp.wait_ge(s_out, 16)
            sp.wait_ge(rows_out, 32)
            sp.wait_ge(win_out, 16 * 6)
            for n in range(2):
                sp.wait_ge(y_out[n], 16)

        @block.scalar
        def _(act):
            split = [0]
            staged = [0]
            lows = [0]

            def split_to(last):
                while split[0] < min(last, len(CHUNKS)):
                    j = split[0]
                    width = CHUNKS[j][3]
                    act.wait_ge(raw_in[j % NRAW], 16 * (j // NRAW + 1))
                    if j >= NHL:
                        wait_used(act, j - NHL)
                    nc.scalar.activation(whi[:, j % NHL, 0:width], raw[:, j % NRAW, 0:width], ACT.Copy)\
                      .then_inc(w_hi_ready, 1)
                    split[0] += 1

            def split_for(name):
                split_to(FIRST[name] + COUNT[name] + NHL)

            def bank(idx, w, n=P, start=0):
                return ps[start:start + n, idx % BANKS, 0:w]

            def copy_out(idx, out, w, n=P, func=ACT.Copy):
                act.wait_ge(z_done, idx + 1)
                nc.scalar.activation(out, bank(idx, w, n), func).then_inc(evac_a, 1)

            def next_stage():
                k = staged[0]
                staged[0] += 1
                if k >= NSTAGE:
                    act.wait_ge(stage_free, k - NSTAGE + 1)
                return stage[:, k % NSTAGE, :]

            def to_stage(idx, w, func=ACT.Copy):
                copy_out(idx, next_stage()[:, 0:w], w, func=func)

            def to_stage_small(idx, w, n=NB):
                out = next_stage()
                if lows[0]:
                    act.wait_ge(stage_free, lows[0])
                lows[0] = staged[0]
                act.wait_ge(z_done, idx + 1)
                nc.scalar.activation(out[0:n, 0:w], bank(idx, w, n), ACT.Copy)
                nc.scalar.activation(low_s[0:n, 0:w], bank(idx, w, n, LO), ACT.Copy).then_inc(evac_a, 1)

            def half(idx, out, func=ACT.Copy, scale=1.0):
                act.wait_ge(z_done, idx + 1)
                nc.scalar.activation(out, bank(idx, 512), func, scale=scale).then_inc(act_half, 1)

            def attention(jobs, n0, c0, scale):
                def exp(n):
                    s = n % 2
                    w = jobs[n - n0][2] * P
                    act.wait_ge(masked, n + 1)
                    nc.scalar.activation(Pm[:, s, 0:w], Pm[:, s, 0:w], ACT.Exp, bias=amax[:, 4 * s + 2:4 * s + 3],
                                         scale=scale, accum_out=lsum[:, s:s + 1]).then_inc(exp_done, 1)

                chunk = c0
                exp(n0)
                for n in range(n0, n0 + len(jobs)):
                    if n + 1 < n0 + len(jobs):
                        exp(n + 1)
                    for w in widths(jobs[n - n0][2]):
                        if chunk % 2:
                            pt_copy(act, nc.scalar.activation, chunk, w, pt_a, (ACT.Copy,))
                        chunk += 1

            for t in range(NT):
                act.dma_start(xt[:, t, :], x_prompt[t * P:(t + 1) * P, :]).then_inc(x_in[t], 16)
            act.dma_start(xs1[:, :], x_sample).then_inc(x_in[TS], 16)
            act.wait_ge(c_in, 32)
            nc.scalar.activation(c9b[:, :], c9[:, :], ACT.Sigmoid).then_inc(sigm_c, 1)
            split_to(NHL)
            act.wait_ge(wuk_in, 16)
            nc.scalar.activation(wuk_hi[:, :, :], wukr[:, :, :], ACT.Copy).then_inc(wuk_h, 1)
            for n in range(2):
                split_for(f"ada{n}")
                to_stage_small(ITEM[f"ada{n}"], 512, NB + 1)
            for i in range(2):
                copy_out(ITEM["wukT"] + i, wukT_t[:, i * 512:(i + 1) * 512], 512)
            for k in range(KD):
                copy_out(ITEM["xT"] + k, xT[:, k, :], 512)
            for n in range(2, 6):
                split_for(f"ada{n}")
                to_stage_small(ITEM[f"ada{n}"], 512, NB + 1)
            for n in range(2):
                copy_out(ITEM["gate"] + n, gate_bc[:, n * 512:(n + 1) * 512], 512)
            for k in range(KD):
                act.wait_ge(h_f, k + 1)
                nc.scalar.activation(hThi[:, k, :], xT[:, k, :], ACT.Copy).then_inc(h_hi, 1)
            for name, w in (("Q", QR), ("KV", CW)):
                split_for(name)
                for t in range(NT):
                    to_stage(ITEM[name] + t, w)
                to_stage_small(ITEM[name] + TS, w)
            for c in range(3):
                half(ITEM["Tq"] + c, qaThi[:, c, :], scale=colt[:, KD + c:KD + c + 1])
            for i in range(2):
                split_for(f"QB{i}")
                for t in range(NT):
                    to_stage(ITEM[f"QB{i}"] + t, 384)
                to_stage_small(ITEM[f"QB{i}"] + TS, 384)
            for c in range(2):
                half(ITEM["Tr"] + c, rThi[:, c, :])
            for t in range(NT):
                to_stage(ITEM["K"] + t, 512)
            to_stage_small(ITEM["K"] + TS, 512)
            split_for("V")
            for t in range(NT):
                copy_out(ITEM["V"] + t, vm[:, t, :], 512)
            for i in range(2):
                for t in range(NT):
                    idx = ITEM["TqM"] + i * NT + t
                    copy_out(idx, qTm[:, 4 * i:4 * i + 4, t * P:(t + 1) * P], 512, QK)
            for t in range(NT):
                for i in range(2):
                    idx = ITEM["TkM"] + 2 * t + i
                    copy_out(idx, kTm[:, 4 * i:4 * i + 4, t * P:(t + 1) * P], 512, QK)
            attention(MLA_JOBS, 0, 0, MLA_SCALE)
            for g in range(ND):
                split_for(f"D{g}QK")
                for t in range(NT):
                    to_stage(ITEM[f"D{g}QK"] + t, 512)
                to_stage_small(ITEM[f"D{g}QK"] + TS, 512)
                split_for(f"D{g}V")
                for t in range(NT):
                    copy_out(ITEM[f"D{g}V"] + t, kvo[:, g, t, BW:2 * BW], BW)
                to_stage_small(ITEM[f"D{g}V"] + TS, BW)
            for i in range(4 * ND):
                g, is_k, p = i // 4, i // 2 % 2, i % 2
                copy_out(ITEM["TD"] + i, (dkT if is_k else dqT)[:, g, p, :], 512)
            attention(DIL_JOBS, len(MLA_JOBS), N_MLA_CHUNKS, DIL_SCALE)
            for name, w in (("GA", AW), ("GB", BW)):
                split_for(name)
                for t in range(NT):
                    act.wait_ge(z_done, ITEM[name] + t + 1)
                    out = next_stage()
                    nc.scalar.activation(out[:, 0:w], bank(ITEM[name] + t, w), ACT.Sigmoid).then_inc(act_half, 1)
                to_stage_small(ITEM[name + "s"], w)
            act.wait_ge(win_out, 16 * 3)
            for c in range(6):
                half(ITEM["To"] + c, oThi[:, c, :])
            for n in range(2):
                for b, out in (("A", ya), ("B", yb)):
                    split_for(f"P{b}{n}")
                    for t in range(NT):
                        copy_out(ITEM[f"P{b}{n}"] + t, out[:, t, n * 512:(n + 1) * 512], 512)
            act.dma_start(xr[1][:, :, :], x_prompt[:, 512:1024].rearrange("(t p) c -> p t c", p=P))\
               .then_inc(xr_in[1], 16)
            for n in range(2):
                for b in "AB":
                    split_for(f"M{b}{n}")
                    for t in range(NT):
                        to_stage(ITEM[f"M{b}{n}"] + t, 512, ACT.Sigmoid)
                    to_stage_small(ITEM[f"M{b}{n}"] + TS, 512)
            for k in range(KD):
                half(ITEM["Tm"] + k, hThi[:, k, :])
            act.wait_ge(merged, 2 * NT)
            act.dma_start(xr[0][:, :, :], x_prompt[:, 0:512].rearrange("(t p) c -> p t c", p=P))\
               .then_inc(xr_in[0], 16)
            for n in range(2):
                split_for(f"WO{n}")
                for t in range(NT):
                    to_stage(ITEM[f"WO{n}"] + t, 512)
            act.wait_ge(stage_free, staged[0])
            act.wait_ge(y_out[0], 16)

            def hi_rows(G, q):
                act.wait_ge(ct_done, G + 1)
                if not (isinstance(G, int) and G < 2):
                    act.wait_ge(s_done, G - 1)
                nc.scalar.activation(cThi[:, q % 2, :], psw(0, 1024), ACT.Copy).then_inc(ct_hi, 1)

            def batch(b, first, last):
                for g in range(8):
                    if g == 0 and first:
                        hi_rows(b * 8, 0)
                    if not (last and g == 7):
                        hi_rows(b * 8 + g + 1, g + 1)
                    for u in range(4):
                        U = b * NPAGE + 4 * g + u
                        act.wait_ge(k_done, U + 1)
                        if not (first and 4 * g + u < 4):
                            act.wait_ge(red_done, U - 3)
                        nc.scalar.activation(sq4[:, u, :], ps[:, 3 + u % 2, :], ACT.Square).then_inc(sq_done, 1)
                        if g == 2 and u == 0 and not first:
                            expo(b - 1)

            def expo(b):
                act.wait_ge(sub_done, b + 1)
                nc.scalar.activation(Ex_t[:, :], Sc_t[:, :], ACT.Exp, scale=MLA_SCALE).then_inc(ex_done, 1)

            batch(0, True, False)
            with act.Fori(0, (NB - 2) // 2) as i:
                batch(2 * i + 1, False, False)
                batch(2 * i + 2, False, False)
            batch(NB - 1, False, True)
            expo(NB - 1)
            act.wait_ge(f_dve, F_SUB)
            nc.scalar.activation(ED_t[:, :], SD_t[:, :], ACT.Exp, scale=DIL_SCALE).then_inc(f_act, 1)
            nc.scalar.activation(sgm[:, :], mix_s[:, :], ACT.Sigmoid).then_inc(f_act, 1)
            nc.scalar.activation(mgm[:, :], merge_s[:, :], ACT.Sigmoid).then_inc(f_act, 1)
            for n in range(2):
                for b in "AB":
                    split_for(f"P{b}s{n}")
                    to_stage_small(ITEM[f"P{b}s{n}"], 512)
            for n in range(2):
                split_for(f"WOs{n}")
                to_stage_small(ITEM[f"WOs{n}"], 512)

        @block.gpsimd
        def _(pool):
            low = [0]
            steps = [0]

            def link(ins):
                steps[0] += 1
                ins.then_inc(pool_step, 1)
                pool.wait_ge(pool_step, steps[0])

            def low_to(last):
                while low[0] < min(last, len(CHUNKS)):
                    j = low[0]
                    width = CHUNKS[j][3]
                    pool.wait_ge(w_hi_ready, j + 1)
                    nc.gpsimd.tensor_tensor(out=wlo[:, j % NHL, 0:width], in0=raw[:, j % NRAW, 0:width],
                                            in1=whi[:, j % NHL, 0:width].bitcast(F32), op=ALU.subtract)\
                      .then_inc(w_lo_ready, 1)
                    low[0] += 1

            def rotate(g, t, c):
                n = lanes(t)
                y = tmp[0:n, c % 2, :].rearrange("p (h e) -> p h e", e=DH)
                t1 = tmp[0:n, 2, :]
                t2 = tmp[0:n, 3, :].rearrange("p (h e) -> p h e", e=DH)
                sin = ropes[0:n, t, 64:128]
                pool.wait_ge(y_roped, 2 * c + 1)
                if c:
                    pool.wait_ge(rope_done, c)
                nc.gpsimd.tensor_tensor(out=t2[:, :, 0:32], in0=y[:, :, 32:64], in1=rep(sin[:, 0:32], 1, 8), op=ALU.mult)
                link(nc.gpsimd.tensor_tensor(out=t2[:, :, 32:64], in0=y[:, :, 0:32], in1=rep(sin[:, 32:64], 1, 8),
                                             op=ALU.mult))
                pool.wait_ge(y_roped, 2 * c + 2)
                q_out = dq_s[:, g, :] if t == TS else dqn[:, g, t, :]
                k_out = kv_s[:, g, 0:BW] if t == TS else kvo[:, g, t, 0:BW]
                t2f = tmp[0:n, 3, :]
                nc.gpsimd.tensor_tensor(out=q_out, in0=t1[:, 0:BW], in1=t2f[:, 0:BW], op=ALU.add)
                nc.gpsimd.tensor_tensor(out=k_out, in0=t1[:, BW:2 * BW], in1=t2f[:, BW:2 * BW], op=ALU.add)\
                  .then_inc(rope_done, 1)

            nc.gpsimd.memset(ones[:, :], 1.0).then_inc(zeroed, 1)
            nc.gpsimd.memset(cs[:, :, :].bitcast(F32), 0.0).then_inc(zeroed, 1)
            nc.gpsimd.memset(hTs[:, :, :].bitcast(F32), 0.0).then_inc(zeroed, 1)
            low_to(NHL)
            pool.wait_ge(cs_ready, 1)
            nc.gpsimd.memset(qaTs[:, :, :].bitcast(F32), 0.0).then_inc(zeroed, 1)
            nc.gpsimd.memset(rTs[:, :, :].bitcast(F32), 0.0).then_inc(zeroed, 1)
            low_to(FIRST["D0QK"] + NHL)
            pool.wait_ge(rows_ready, 5)
            pool.dma_start(rows_p.rearrange("(t p) c -> p t c", p=P), rows[:, 0:NT, :]).then_inc(rows_out, 16)
            pool.dma_start(rows_s, rows[0:NB, TS, :]).then_inc(rows_out, 16)
            for g in range(ND):
                low_to(FIRST[f"D{g}QK"] + COUNT[f"D{g}QK"] + NHL)
                for t in range(5):
                    rotate(g, t, 5 * g + t)
                    low_to(low[0] + 1)
                low_to(FIRST[f"D{g}V"] + COUNT[f"D{g}V"] + NHL)
            wait_evac(pool, ITEM[f"D{ND - 1}V"] + TS)
            pool.dma_start(win0_p, kvo[:, 0, NT - 1, :]).then_inc(win_out, 16)
            for g, out in ((1, win1_p), (2, win2_p)):
                pool.dma_start(out.rearrange("(t p) c -> p t c", p=P), kvo[:, g, :, :]).then_inc(win_out, 16)
            low_to(FIRST["WO0"])
            pool.wait_ge(smp_ready, SMP_KV)
            for g, out in enumerate((win0_s, win1_s, win2_s)):
                pool.dma_start(out, kv_s[:, g, :]).then_inc(win_out, 16)
            for n in range(2):
                low_to(FIRST[f"WO{n}"] + COUNT[f"WO{n}"] + NHL)
                pool.wait_ge(y_rdy, NT * (n + 1))
                pool.dma_start(y_prompt[:, n * 512:(n + 1) * 512].rearrange("(t p) c -> p t c", p=P), xr[n][:, :, :])\
                    .then_inc(y_out[n], 16)
            pool.wait_ge(pv_done, NB)
            nc.gpsimd.memset(osT[:, :, :].bitcast(F32), 0.0).then_inc(zeroed, 1)
            low_to(len(CHUNKS))

        @block.tensor
        def _(pe):
            mm = nc.tensor.matmul
            miscs = [0]

            def wait_bank(idx):
                if idx >= BANKS:
                    wait_evac(pe, idx - BANKS)

            def misc_begin():
                if miscs[0]:
                    pe.wait_ge(misc_free, miscs[0])
                miscs[0] += 1

            def block_of(name, first, tiles, hi=None, lo=None, small=None):
                f, nk, w = FIRST[name], COUNT[name], WIDTH[name]
                for k in range(nk):
                    j = f + k
                    pe.wait_ge(w_lo_ready, j + 1)
                    bh, bl = whi[:, j % NHL, 0:w], wlo[:, j % NHL, 0:w]
                    for n, t in enumerate(tiles):
                        idx = first + n
                        if k == 0:
                            wait_bank(idx)
                        out = ps[:, idx % BANKS, 0:w]
                        st, en = k == 0, k == nk - 1
                        if t == TS:
                            mm(out, small[:, k, :], bh, start=st, stop=False)
                            last = mm(out, small[:, k, :], bl, start=False, stop=en)
                        else:
                            c = slice(t * P, (t + 1) * P)
                            mm(out, hi[:, k, c], bh, start=st, stop=False)
                            mm(out, hi[:, k, c], bl, start=False, stop=False)
                            last = mm(out, lo[:, k, c], bh, start=False, stop=en)
                        if en:
                            last.then_inc(z_done, 1)
                    if k < nk - 1:
                        last.then_inc(w_used, 1)

            def transposes(idx, parts, n_in=P):
                wait_bank(idx)
                for col, rows_out_, src in parts:
                    last = nc.tensor.transpose(ps[0:rows_out_, idx % BANKS, col:col + n_in], src, ident[0:n_in, 0:n_in])
                last.then_inc(z_done, 1)

            def misc_transposes(parts, n_in):
                misc_begin()
                for col, rows_out_, src in parts:
                    last = nc.tensor.transpose(ps[0:rows_out_, 7, col:col + n_in], src, ident[0:n_in, 0:n_in])
                last.then_inc(misc_done, 1)

            pe.wait_ge(consts_in, 80)
            pe.wait_ge(csilu, 1)
            misc_transposes([(9 * k, P, c9b[0:9, k * P:(k + 1) * P]) for k in range(KD)], NB + 1)
            pe.wait_ge(cs_ready, 1)
            for n in range(2):
                block_of(f"ada{n}", ITEM[f"ada{n}"], [TS], small=cs)
            pe.wait_ge(wuk_in, 16)
            for i in range(2):
                transposes(ITEM["wukT"] + i, [(2 * P * q + P * r, P, wukr[:, r, (2 * i + q) * P:(2 * i + q + 1) * P])
                                              for q in range(2) for r in range(2)])
            pe.wait_ge(xn_ready, 5)
            for k in range(KD):
                transposes(ITEM["xT"] + k, [(t * P, P, xt[:, t, k * P:(k + 1) * P]) for t in range(NT)])
            misc_transposes([(NB * k, P, xs1[:, k * P:(k + 1) * P]) for k in range(KD)], NB)
            for n in range(2, 6):
                block_of(f"ada{n}", ITEM[f"ada{n}"], [TS], small=cs)
            pe.wait_ge(ada_ready, 6)
            misc_transposes([(9 * k, P, ada[:, k * P:(k + 1) * P]) for k in range(2 * KD)], NB + 1)
            for n in range(2):
                idx = ITEM["gate"] + n
                wait_bank(idx)
                mm(ps[:, idx % BANKS, :], ident[0:NB + 1, NB:NB + 1].to_broadcast([NB + 1, P]),
                   ada[:, 2 * D + n * 512:2 * D + (n + 1) * 512], start=True, stop=True).then_inc(z_done, 1)
            pe.wait_ge(h_ready, KD + 1)
            for name in ("Q", "KV"):
                block_of(name, ITEM[name], range(5), hThi, hTlo, hTs)
            pe.wait_ge(qan_ready, 5)
            for c in range(3):
                transposes(ITEM["Tq"] + c, [(t * P, P, qan[:, t, c * P:(c + 1) * P]) for t in range(NT)])
            misc_transposes([(NB * c, P, qan[0:NB, TS, c * P:(c + 1) * P]) for c in range(3)], NB)
            wait_evac(pe, ITEM["Tq"] + 2)
            pe.wait_ge(smp_ready, SMP_Q)
            for i in range(2):
                block_of(f"QB{i}", ITEM[f"QB{i}"], range(5), qaThi, qaTlo, qaTs)
            pe.wait_ge(rows_ready, 5)
            for c in range(2):
                transposes(ITEM["Tr"] + c, [(t * P, P, rows[:, t, c * P:(c + 1) * P]) for t in range(NT)])
            misc_transposes([(NB * c, P, rows[0:NB, TS, c * P:(c + 1) * P]) for c in range(2)], NB)
            wait_evac(pe, ITEM["Tr"] + 1)
            pe.wait_ge(smp_ready, SMP_R)
            for t in range(5):
                idx = ITEM["K"] + t
                wait_bank(idx)
                for k in range(2):
                    if t == TS:
                        pairs = [(rTs[:, k, :], wuk_hi[:, k, :]), (rTs[:, k, :], wuk_lo[:, k, :])]
                    else:
                        c = slice(t * P, (t + 1) * P)
                        pairs = [(rThi[:, k, c], wuk_hi[:, k, :]), (rThi[:, k, c], wuk_lo[:, k, :]),
                                 (rTlo[:, k, c], wuk_hi[:, k, :])]
                    for m, (a, b) in enumerate(pairs):
                        last = mm(ps[:, idx % BANKS, :], a, b, start=k == 0 and m == 0,
                                  stop=k == 1 and m == len(pairs) - 1)
                last.then_inc(z_done, 1)
            block_of("V", ITEM["V"], range(NT), rThi, rTlo)
            for i in range(2):
                for t in range(NT):
                    pe.wait_ge(qh_ready, 5 * i + t + 1)
                    transposes(ITEM["TqM"] + i * NT + t,
                               [(m * P, QK, qh[:, i * NT + t, m * QK:(m + 1) * QK]) for m in range(4)])
            pe.wait_ge(qh_ready, 10)
            misc_begin()
            for p in range(4):
                nc.tensor.transpose(ps[:, 7, NB * p:NB * p + NB],
                                    qn_s[:, p * P:(p + 1) * P],
                                    ident[0:NB, 0:NB])
            for h in range(HM):
                last = nc.tensor.transpose(ps[0:ROPE, 7, 32 + NB * h:32 + NB * h + NB],
                                           q_s[:, h * QK + NOPE:(h + 1) * QK], ident[0:NB, 0:NB])
            last.then_inc(misc_done, 1)
            misc_begin()
            for odd in range(2):
                o = 64 * odd
                for c in range(2):
                    for h in range(odd, HM, 2):
                        last = mm(ps[:, 7, c * 64 + h * NB:c * 64 + (h + 1) * NB],
                                  wukT[o:o + 64, h // 2, c * P:(c + 1) * P],
                                  qsT[o:o + 64, h // 2 * NB:(h // 2 + 1) * NB], start=True, stop=True)
                if odd == 0:
                    last.then_inc(even_done, 1)
                    pe.wait_ge(even_done, 1)
            last.then_inc(misc_done, 1)
            for t in range(NT):
                pe.wait_ge(kc_ready, t + 1)
                for i in range(2):
                    transposes(ITEM["TkM"] + 2 * t + i,
                               [(m * P, QK, kc[:, t, (4 * i + m) * QK:(4 * i + m + 1) * QK]) for m in range(4)])

            def attention(jobs, n0, c0, first_idx, scores, values):
                wait_evac(pe, first_idx)
                pe.wait_ge(misc_free, miscs[0])
                end = n0 + len(jobs)

                def qk(n):
                    if n - n0 >= 2:
                        pe.wait_ge(o_done, n - 1)
                    scores(jobs[n - n0], 3 * (n % 2)).then_inc(qk_done, 1)

                chunk = c0
                qk(n0)
                for n in range(n0, end):
                    if n + 1 < end:
                        qk(n + 1)
                    s = n % 2
                    pe.wait_ge(exp_done, n + 1)
                    ws = widths(jobs[n - n0][2])

                    def tr(m):
                        c = chunk + m
                        if c - c0 >= 2:
                            wait_pt(pe, c - 2)
                        for q in range(ws[m]):
                            last = nc.tensor.transpose(ps[:, 6 + c % 2, q * P:(q + 1) * P],
                                                       Pm[:, s, (4 * m + q) * P:(4 * m + q + 1) * P], ident)
                        last.then_inc(trp_done, 1)

                    tr(0)
                    out, vals = values(jobs[n - n0], 3 * s)
                    for m in range(len(ws)):
                        if m + 1 < len(ws):
                            tr(m + 1)
                        c = chunk + m
                        wait_pt(pe, c)
                        for q in range(ws[m]):
                            b = 4 * m + q
                            last = mm(out, PT[:, c % 3, q * P:(q + 1) * P], vals[b], start=b == 0,
                                      stop=b == len(vals) - 1)
                        last.then_inc(pv_chunk, 1)
                    chunk += len(ws)
                pe.wait_ge(o_done, end)

            def mla_scores(job, bank0):
                i, h, nb = job
                return mm(ps[:, bank0, 0:nb * P], qTm[:, h, i * P:(i + 1) * P], kTm[:, h, 0:nb * P],
                          start=True, stop=True)

            def mla_values(job, bank0):
                i, h, nb = job
                return ps[:, bank0 + 1, 0:64], [vm[:, b, h * 64:(h + 1) * 64] for b in range(nb)]

            attention(MLA_JOBS, 0, 0, LAST_ITEM["TkM"], mla_scores, mla_values)
            for g in range(ND):
                block_of(f"D{g}QK", ITEM[f"D{g}QK"], range(5), hThi, hTlo, hTs)
                block_of(f"D{g}V", ITEM[f"D{g}V"], range(5), hThi, hTlo, hTs)
            for i in range(4 * ND):
                g, is_k, p = i // 4, i // 2 % 2, i % 2
                pe.wait_ge(rope_done, 5 * g + NT)
                transposes(ITEM["TD"] + i,
                           [(t * P, P, (kvo if is_k else dqn)[:, g, t, p * P:(p + 1) * P]) for t in range(NT)])

            def dil_scores(job, bank0):
                i, h, nb = job
                r = slice(64 * (h % 2), 64 * (h % 2) + 64)
                for g in range(ND):
                    lo = max(0, i - 1) if g == 0 else 0
                    last = mm(ps[:, bank0 + g, 0:(i + 1 - lo) * P], dqT[r, g, h // 2, i * P:(i + 1) * P],
                              dkT[r, g, h // 2, lo * P:(i + 1) * P], start=True, stop=True)
                return last

            def dil_values(job, bank0):
                i, h, nb = job
                blocks = [(g, b) for g in range(ND) for b in range(max(0, i - 1) if g == 0 else 0, i + 1)]
                return ps[:, bank0, 256:320], [kvo[:, g, b, BW + h * 64:BW + (h + 1) * 64] for g, b in blocks]

            attention(DIL_JOBS, len(MLA_JOBS), N_MLA_CHUNKS, LAST_ITEM["TD"], dil_scores, dil_values)
            for name in ("GA", "GB"):
                block_of(name, ITEM[name], range(5), hThi, hTlo, hTs)
            pe.wait_ge(gated, 2 * NT)
            for c in range(6):
                transposes(ITEM["To"] + c, [(t * P, P, oN[:, t, c * P:(c + 1) * P]) for t in range(NT)])
            wait_evac(pe, ITEM["To"] + 5)
            for n in range(2):
                block_of(f"PA{n}", ITEM[f"PA{n}"], range(NT), oThi, oTlo)
                block_of(f"PB{n}", ITEM[f"PB{n}"], range(NT), oThi[:, 4:6, :], oTlo[:, 4:6, :])
            for n in range(2):
                for b in "AB":
                    block_of(f"M{b}{n}", ITEM[f"M{b}{n}"], range(5), hThi, hTlo, hTs)
            pe.wait_ge(merged, 2 * NT)
            for k in range(KD):
                transposes(ITEM["Tm"] + k, [(t * P, P, ya[:, t, k * P:(k + 1) * P]) for t in range(NT)])
            wait_evac(pe, ITEM["Tm"] + KD - 1)
            for n in range(2):
                block_of(f"WO{n}", ITEM[f"WO{n}"], range(NT), hThi, hTlo)
            wait_evac(pe, LAST_ITEM["WO1"])

            def group_in(b, g, p, turn):
                G = 8 * b + g
                if g % 2 == 0:
                    pe.wait_ge(cn_in[p][g // 2], 128 * turn + 128)
                if not (isinstance(G, int) and G == 0):
                    pe.wait_ge(ct_ready, G)
                for u in range(4):
                    src = cn[p][:, 4 * g + u, :]
                    for c in range(2):
                        nc.tensor.transpose(ps[:, c, u * P:(u + 1) * P], src[:, c * P:(c + 1) * P], ident)
                    last = nc.tensor.transpose(ps[0:ROPE, 2, u * P:(u + 1) * P], src[:, KVR:CW], ident)
                last.then_inc(ct_done, 1)

            def group_products(b, g):
                G = 8 * b + g
                q = g % 2
                pe.wait_ge(ct_ready, G + 1)
                for u in range(4):
                    U = 4 * G + u
                    if not (isinstance(U, int) and U < 2):
                        pe.wait_ge(sq_done, U - 1)
                    k_bank = ps[:, 3 + u % 2, :]
                    hi = [cThi[:, q, c * 512 + u * P:c * 512 + (u + 1) * P] for c in range(2)]
                    lo = [cTlo[:, q, c * 512 + u * P:c * 512 + (u + 1) * P] for c in range(2)]
                    sc = ps[:, 5 + q, 24 * u:24 * u + 24]
                    for c in range(2):
                        mm(k_bank, hi[c], wuk_hi[:, c, :], start=c == 0, stop=False)
                        mm(k_bank, hi[c], wuk_lo[:, c, :], start=False, stop=False)
                        last = mm(k_bank, lo[c], wuk_hi[:, c, :], start=False, stop=c == 1)
                    last.then_inc(k_done, 1)
                    if u == 0 and not (isinstance(G, int) and G < 2):
                        pe.wait_ge(s_read, G - 1)
                    for c in range(2):
                        qa = qabs[:, c, bass.ds(b, 1), :].rearrange("p a n -> p (a n)")
                        mm(sc[:, 0:16], hi[c], qa, start=c == 0, stop=False)
                        mm(sc[:, 0:16], lo[c], qa, start=False, stop=c == 1)
                    last = mm(sc[:, 16:24], kpT[:, q, u * P:(u + 1) * P], qpe[:, bass.ds(8 * b, 8)],
                              start=True, stop=True)
                    if u == 3:
                        last.then_inc(s_done, 1)

            def softmax_max(b):
                pe.wait_ge(pm_ready, b + 1)
                nc.tensor.transpose(ps[0:HM, 7, 0:P], pmx[:, :], ident).then_inc(pmT_done, 1)

            def softmax_spread(b):
                pe.wait_ge(dg_ready, b + 1)
                mm(ps[:, 7, P:P + HM], ones[0:HM, :], dgm[0:HM, 0:HM], start=True, stop=True).then_inc(mx_done, 1)

            def weighted_sum(b, p):
                pe.wait_ge(es_ready, b + 1)
                mm(ps[:, 7, P + 8:P + 16], ones[:, :], esm[:, :], start=True, stop=True)
                if not (isinstance(b, int) and b == 0):
                    pe.wait_ge(lat_done, b)
                for c in range(2):
                    for t in range(NPAGE):
                        mm(ps[:, 7, 256 + c * 8:264 + c * 8], cn[p][:, t, c * P:(c + 1) * P], Ex[:, t, :],
                           start=t == 0, stop=False)
                    last = mm(ps[:, 7, 256 + c * 8:264 + c * 8], rows[0:NB, TS, c * P:(c + 1) * P], Ex[0:NB, NPAGE, :],
                              start=False, stop=True)
                last.then_inc(pv_done, 1)

            def batch(b, p, turn, next_turn, first, last):
                if first:
                    group_in(b, 0, p, turn)
                for g in range(8):
                    if g < 7:
                        group_in(b, g + 1, p, turn)
                    elif not last:
                        group_in(b + 1, 0, 1 - p, next_turn)
                    group_products(b, g)
                    if not first:
                        if g == 0:
                            softmax_max(b - 1)
                        elif g == 1:
                            softmax_spread(b - 1)
                        elif g == 2:
                            weighted_sum(b - 1, 1 - p)

            batch(0, 0, 0, 0, True, False)
            with pe.Fori(0, (NB - 2) // 2) as i:
                batch(2 * i + 1, 1, i, i + 1, False, False)
                batch(2 * i + 2, 0, i + 1, i + 1, False, False)
            batch(NB - 1, 1, (NB - 1) // 2, 0, False, True)
            softmax_max(NB - 1)
            softmax_spread(NB - 1)
            weighted_sum(NB - 1, 1)
            pe.wait_ge(late_in, 32)
            pe.wait_ge(lat_done, NB)
            lat = latT[:, :].rearrange("p (b c h) -> p b c h", b=NB, c=2)
            for h in range(HM):
                for c in range(2):
                    last = mm(ps[0:NB, 0, h * 64:(h + 1) * 64], lat[:, :, c, h], wuvr[:, c, h * 64:(h + 1) * 64],
                              start=c == 0, stop=c == 1)
            last.then_inc(f_pe, 1)
            for b in range(NB):
                if b >= 2:
                    pe.wait_ge(qb_read, b - 1)
                for g in range(ND):
                    q0 = (1 + 2 * (b % 2)) * 512 + g * BW
                    last = mm(psw(0, 8 * 512)[:, q0:q0 + BW], ident[0:NB, b:b + 1].to_broadcast([NB, P]),
                              dq_s[:, g, :], start=True, stop=True)
                last.then_inc(qb_done, 1)
            pe.wait_ge(f_dve, F_MAX)
            nc.tensor.transpose(ps[0:32, 5, 0:P], dpm[:, :], ident).then_inc(f_pe, 1)
            pe.wait_ge(f_dve, F_DIAG)
            mm(ps[:, 5, 128:160], ones[0:32, :], dgm[:, :], start=True, stop=True).then_inc(f_pe, 1)
            pe.wait_ge(f_dve, F_SUM)
            mm(ps[:, 5, 160:192], ones[:, :], dsm[:, :], start=True, stop=True).then_inc(f_pe, 1)
            ED = ED_t[:, :].rearrange("p (b s h) -> p b s h", b=NB, h=HD)
            for b in range(NB):
                kv = [(sdk0 if b < 6 else sdk1)[:, (b if b < 6 else b - 6) * ND + g, :] for g in range(ND)]
                for p in range(2):
                    c = BW + p * P
                    for g in range(ND):
                        mm(ps[:, 6, 4 * b + 2 * p:4 * b + 2 * p + 2], kv[g][:, c:c + P], ED[:, b, g, 2 * p:2 * p + 2],
                           start=g == 0, stop=False)
                    for g in range(ND):
                        last = mm(ps[:, 6, 4 * b + 2 * p:4 * b + 2 * p + 2], kv_s[:, g, c:c + P],
                                  ED[0:NB, b, ND + g, 2 * p:2 * p + 2], start=False, stop=g == ND - 1)
            last.then_inc(f_pe, 1)
            pe.wait_ge(f_dve, F_OBT)
            for p in range(2):
                last = nc.tensor.transpose(ps[0:NB, 7, p * P:(p + 1) * P], obT[:, p * NB:(p + 1) * NB], ident)
            last.then_inc(f_pe, 1)
            pe.wait_ge(f_dve, F_OG)
            for c in range(6):
                last = nc.tensor.transpose(ps[:, 7, 256 + NB * c:256 + NB * (c + 1)], og[:, c * P:(c + 1) * P],
                                           ident[0:NB, 0:NB])
            last.then_inc(f_pe, 1)
            pe.wait_ge(zeroed, 6)
            pe.wait_ge(f_dve, F_OST)
            for n in range(2):
                block_of(f"PAs{n}", ITEM[f"PAs{n}"], [TS], small=osT)
                block_of(f"PBs{n}", ITEM[f"PBs{n}"], [TS], small=osT[:, 4:6, :])
            pe.wait_ge(f_dve, F_MS)
            for c in range(KD):
                last = nc.tensor.transpose(ps[:, 7, 320 + NB * c:320 + NB * (c + 1)], yab[:, 0, c * P:(c + 1) * P],
                                           ident[0:NB, 0:NB])
            last.then_inc(f_pe, 1)
            pe.wait_ge(f_dve, F_MST)
            for n in range(2):
                block_of(f"WOs{n}", ITEM[f"WOs{n}"], [TS], small=hTs)

        @block.vector
        def _(dve):
            v = nc.vector
            steps = [0]
            staged = [0]
            miscs = [0]
            fcount = [0]

            def link(ins):
                steps[0] += 1
                ins.then_inc(dve_step, 1)
                dve.wait_ge(dve_step, steps[0])

            def rsqrt(x, a, y, step):
                step(v.tensor_scalar(out=a.bitcast(I32), in0=x.bitcast(I32), scalar1=1, scalar2=None,
                                     op0=ALU.logical_shift_right))
                step(v.tensor_scalar(out=y.bitcast(I32), in0=a.bitcast(I32), scalar1=-1.0, scalar2=RSQRT_MAGIC,
                                     op0=ALU.mult, op1=ALU.add))
                for _ in range(4):
                    step(v.tensor_tensor(out=a, in0=y, in1=y, op=ALU.mult))
                    step(v.scalar_tensor_tensor(out=a, in0=a, scalar=-0.5, in1=x, op0=ALU.mult, op1=ALU.mult))
                    step(v.scalar_tensor_tensor(out=y, in0=a, scalar=1.5, in1=y, op0=ALU.add, op1=ALU.mult))

            def inv_rms(n, cols_, scale=1.0):
                link(v.tensor_scalar(out=rsx[0:n, 0:cols_], in0=ms[0:n, 0:cols_], scalar1=scale, scalar2=EPS,
                                     op0=ALU.mult, op1=ALU.add))
                rsqrt(rsx[0:n, 0:cols_], rsa[0:n, 0:cols_], rsy[0:n, 0:cols_], link)

            def take(idx, n, w, small):
                wait_evac(dve, idx)
                z = stage[0:n, staged[0] % NSTAGE, 0:w]
                staged[0] += 1
                if small:
                    link(v.tensor_tensor(out=z, in0=z, in1=low_s[0:n, 0:w], op=ALU.add))
                return z

            def free_stage(ins):
                ins.then_inc(stage_free, 1)
                dve.wait_ge(stage_free, staged[0])

            def mean_square(z, w, col):
                n = z.shape[0]
                link(v.tensor_tensor_reduce(out=sqt[0:n, 0:w], in0=z, in1=z, scale=1.0 / w, scalar=0.0,
                                            op0=ALU.mult, op1=ALU.add, accum_out=ms[0:n, col:col + 1]))

            def rotate(x, out, sin_cos, heads):
                n = x.shape[0]
                a = pe1[0:n, 0:heads * ROPE].rearrange("p (h e) -> p h e", e=ROPE)
                b = pe2[0:n, 0:heads * ROPE].rearrange("p (h e) -> p h e", e=ROPE)
                v.tensor_tensor(out=a, in0=x, in1=rep(sin_cos[:, 0:32], 1, heads), op=ALU.mult)
                v.tensor_tensor(out=b[:, :, 0:16], in0=x[:, :, 16:32], in1=rep(sin_cos[:, 32:48], 1, heads), op=ALU.mult)
                link(v.tensor_tensor(out=b[:, :, 16:32], in0=x[:, :, 0:16], in1=rep(sin_cos[:, 48:64], 1, heads),
                                     op=ALU.mult))
                return v.tensor_tensor(out=out, in0=a, in1=b, op=ALU.add)

            def misc_wait():
                miscs[0] += 1
                dve.wait_ge(misc_done, miscs[0])

            def misc_read(ins):
                ins.then_inc(misc_free, 1)
                dve.wait_ge(misc_free, miscs[0])

            def split_small(src, dst, count, n=NB):
                link(v.tensor_copy(dst[:, 0:count, 0:n], src))
                return v.tensor_tensor(out=dst[:, 0:count, LO:LO + n], in0=src,
                                       in1=dst[:, 0:count, 0:n].bitcast(F32), op=ALU.subtract)

            def low_half(idx, out, hi, scale=None):
                dve.wait_ge(act_half, READER[idx][1])
                src = ps[:, idx % BANKS, :]
                if scale is None:
                    ins = v.tensor_tensor(out=out, in0=src, in1=hi.bitcast(F32), op=ALU.subtract)
                else:
                    ins = v.scalar_tensor_tensor(out=out, in0=src, scalar=scale, in1=hi.bitcast(F32), op0=ALU.mult,
                                                 op1=ALU.subtract)
                ins.then_inc(evac_d, 1)

            dve.wait_ge(sigm_c, 1)
            v.tensor_tensor(out=c9b[:, :], in0=c9[:, :], in1=c9b[:, :], op=ALU.mult).then_inc(csilu, 1)
            dve.wait_ge(zeroed, 3)
            misc_wait()
            csf = ps[:, 7, 0:72].rearrange("p (k n) -> p k n", n=9)
            link(v.tensor_copy(cs[:, :, 0:9], csf))
            misc_read(v.tensor_tensor(out=cs[:, :, LO:LO + 9], in0=csf, in1=cs[:, :, 0:9].bitcast(F32), op=ALU.subtract))
            v.memset(flag[:, :], 0.0).then_inc(cs_ready, 1)
            dve.wait_ge(wuk_h, 1)
            v.tensor_tensor(out=wuk_lo[:, :, :], in0=wukr[:, :, :], in1=wuk_hi[:, :, :].bitcast(F32), op=ALU.subtract)\
             .then_inc(wuk_split, 1)

            def ada_item(n):
                z = take(ITEM[f"ada{n}"], NB + 1, 512, True)
                if n == 0:
                    dve.wait_ge(bada_in, 16)
                free_stage(v.tensor_tensor(out=ada[:, n * 512:(n + 1) * 512], in0=z,
                                           in1=bada[:, n * 512:(n + 1) * 512], op=ALU.add))
                if n >= 4:
                    v.tensor_copy(gate_s[:, (n - 4) * 512:(n - 3) * 512], ada[0:NB, n * 512:(n + 1) * 512])\
                     .then_inc(ada_ready, 1)
                else:
                    v.memset(flag[:, :], 0.0).then_inc(ada_ready, 1)

            for t in range(5):
                n = lanes(t)
                x = xs1[:, :] if t == TS else xt[:, t, :]
                dve.wait_ge(x_in[t], 16)
                link(v.tensor_tensor_reduce(out=xsq[0:n, :], in0=x, in1=x, scale=1.0 / D, scalar=0.0,
                                            op0=ALU.mult, op1=ALU.add, accum_out=ms[0:n, 0:1]))
                inv_rms(n, 1)
                v.tensor_scalar(out=x, in0=x, scalar1=rsy[0:n, 0:1], scalar2=None, op0=ALU.mult)\
                 .then_inc(xn_ready, 1)
            for n in range(2):
                ada_item(n)
            misc_wait()
            misc_read(v.tensor_copy(xTs[:, :], ps[:, 7, 0:64]))
            for n in range(2, 6):
                ada_item(n)
            misc_wait()
            adaT = ps[:, 7, 0:144].rearrange("p (k n) -> p k n", n=9)
            dve.wait_ge(consts_in, 80)
            v.scalar_tensor_tensor(out=G1[:, :, :], in0=adaT[:, KD:2 * KD, :], scalar=1.0,
                                   in1=rep(colt[:, 0:KD], 2, 9), op0=ALU.add, op1=ALU.mult)
            misc_read(v.tensor_copy(SH[:, :, :], adaT[:, 0:KD, :]))
            xTs3 = xTs[:, :].rearrange("p (k n) -> p k n", n=NB)
            link(v.tensor_tensor(out=hs_f[:, :, :], in0=xTs3, in1=G1[:, :, 0:NB], op=ALU.mult))
            link(v.tensor_tensor(out=hs_f[:, :, :], in0=hs_f[:, :, :], in1=SH[:, :, 0:NB], op=ALU.add))
            split_small(hs_f[:, :, :], hTs, KD).then_inc(h_ready, 1)

            def low_h(k):
                dve.wait_ge(h_hi, k + 1)
                v.tensor_tensor(out=hTlo[:, k, :], in0=xT[:, k, :], in1=hThi[:, k, :].bitcast(F32), op=ALU.subtract)\
                 .then_inc(h_ready, 1)

            for k in range(KD):
                wait_evac(dve, ITEM["xT"] + k)
                v.tensor_scalar(out=xT[:, k, :], in0=xT[:, k, :], scalar1=G1[:, k, NB:NB + 1],
                                scalar2=SH[:, k, NB:NB + 1], op0=ALU.mult, op1=ALU.add).then_inc(h_f, 1)
                if k:
                    low_h(k - 1)
            low_h(KD - 1)
            v.tensor_tensor(out=g96[:, 0:NOPE], in0=gn[:, G_QN:G_QN + 64], in1=gn[:, G_KN:G_KN + 64], op=ALU.mult)
            link(v.tensor_copy(g96[:, NOPE:QK], gn[:, G_QR:G_QR + 32]))
            for t in range(5):
                n = lanes(t)
                z = take(ITEM["Q"] + t, n, QR, t == TS)
                mean_square(z, QR, 0)
                inv_rms(n, 1)
                free_stage(v.tensor_scalar(out=qan[0:n, t, :], in0=z, scalar1=rsy[0:n, 0:1], scalar2=None, op0=ALU.mult))
                v.memset(flag[:, :], 0.0).then_inc(qan_ready, 1)
            for t in range(5):
                n = lanes(t)
                z = take(ITEM["KV"] + t, n, CW, t == TS)
                mean_square(z[:, 0:KVR], KVR, 0)
                mean_square(z[:, KVR:CW], ROPE, 1)
                inv_rms(n, 2)
                v.scalar_tensor_tensor(out=rows[0:n, t, 0:KVR], in0=z[:, 0:KVR], scalar=rsy[0:n, 0:1],
                                       in1=gn[0:n, G_KV:G_KV + KVR], op0=ALU.mult, op1=ALU.mult)
                free_stage(v.scalar_tensor_tensor(out=rows[0:n, t, KVR:CW], in0=z[:, KVR:CW], scalar=rsy[0:n, 1:2],
                                                  in1=gn[0:n, G_KR:G_KR + ROPE], op0=ALU.mult, op1=ALU.mult))
                kp = rows[0:n, t, KVR:CW].unsqueeze(1)
                rotate(kp, kp, ropes[0:n, t, 128:192], 1).then_inc(rows_ready, 1)
                dve.wait_ge(rows_ready, t + 1)
            for c in range(3):
                low_half(ITEM["Tq"] + c, qaTlo[:, c, :], qaThi[:, c, :], colt[:, KD + c:KD + c + 1])
            dve.wait_ge(zeroed, 5)
            misc_wait()
            qaf = pe1[:, 0:24].rearrange("p (k n) -> p k n", n=NB)
            misc_read(v.tensor_tensor(out=qaf, in0=ps[:, 7, 0:24].rearrange("p (k n) -> p k n", n=NB),
                                      in1=rep(colt[:, KD:KD + 3], 2, NB), op=ALU.mult))
            split_small(qaf, qaTs, 3).then_inc(smp_ready, 1)

            def q_item(i, t):
                n = lanes(t)
                z = take(ITEM[f"QB{i}"] + t, n, 384, t == TS)
                z3 = z.rearrange("p (h e) -> p h e", e=QK)
                sq3 = sqt[0:n, 0:384].rearrange("p (h e) -> p h e", e=QK)
                link(v.tensor_tensor(out=sq3, in0=z3, in1=z3, op=ALU.mult))
                v.tensor_reduce(out=ms[0:n, 0:4], in_=sq3[:, :, 0:NOPE], axis=AX, op=ALU.add)
                link(v.tensor_reduce(out=ms[0:n, 4:8], in_=sq3[:, :, NOPE:QK], axis=AX, op=ALU.add))
                v.tensor_scalar(out=rsx[0:n, 0:4], in0=ms[0:n, 0:4], scalar1=1.0 / NOPE, scalar2=EPS,
                                op0=ALU.mult, op1=ALU.add)
                link(v.tensor_scalar(out=rsx[0:n, 4:8], in0=ms[0:n, 4:8], scalar1=1.0 / ROPE, scalar2=EPS,
                                     op0=ALU.mult, op1=ALU.add))
                rsqrt(rsx[0:n, 0:8], rsa[0:n, 0:8], rsy[0:n, 0:8], link)
                out = q_s[:, i * 384:(i + 1) * 384] if t == TS else qh[:, i * NT + t, :]
                o3 = out.rearrange("p (h e) -> p h e", e=QK)
                v.tensor_tensor(out=o3[:, :, 0:NOPE], in0=z3[:, :, 0:NOPE], in1=rep(rsy[0:n, 0:4], 2, NOPE), op=ALU.mult)
                free_stage(v.tensor_tensor(out=o3[:, :, NOPE:QK], in0=z3[:, :, NOPE:QK], in1=rep(rsy[0:n, 4:8], 2, ROPE),
                                           op=ALU.mult))
                link(v.tensor_tensor(out=o3, in0=o3, in1=rep(g96[0:n, :], 1, 4), op=ALU.mult))
                if t == TS:
                    v.tensor_copy(qn_s[:, i * 256:(i + 1) * 256].rearrange("p (h e) -> p h e", e=NOPE), o3[:, :, 0:NOPE])
                rotate(o3[:, :, NOPE:QK], o3[:, :, NOPE:QK], ropes[0:n, t, 128:192], 4).then_inc(qh_ready, 1)
                dve.wait_ge(qh_ready, 5 * i + t + 1)

            for t in range(5):
                q_item(0, t)
            for t in range(5):
                q_item(1, t)
            for c in range(2):
                low_half(ITEM["Tr"] + c, rTlo[:, c, :], rThi[:, c, :])
            misc_wait()
            rf = pe1[:, 0:16].rearrange("p (k n) -> p k n", n=NB)
            misc_read(v.tensor_copy(rf, ps[:, 7, 0:16].rearrange("p (k n) -> p k n", n=NB)))
            split_small(rf, rTs, 2).then_inc(smp_ready, 1)
            for t in range(5):
                n = lanes(t)
                z = take(ITEM["K"] + t, n, 512, t == TS)
                z3 = z.rearrange("p (h e) -> p h e", e=NOPE)
                link(v.tensor_tensor(out=sqt[0:n, :], in0=z, in1=z, op=ALU.mult))
                link(v.tensor_reduce(out=ms[0:n, 0:8], in_=sqt[0:n, :].rearrange("p (h e) -> p h e", e=NOPE), axis=AX,
                                     op=ALU.add))
                inv_rms(n, 8, 1.0 / NOPE)
                out = (k_s[:, :] if t == TS else kc[:, t, :]).rearrange("p (h e) -> p h e", e=QK)
                free_stage(v.tensor_tensor(out=out[:, :, 0:NOPE], in0=z3, in1=rep(rsy[0:n, 0:8], 2, NOPE), op=ALU.mult))
                v.tensor_copy(out[:, :, NOPE:QK], rep(rows[0:n, t, KVR:CW], 1, HM)).then_inc(kc_ready, 1)
            misc_wait()
            v.tensor_copy(qsT[:, :], ps[:, 7, 0:32])
            misc_read(v.tensor_copy(qpe[:, :].rearrange("p (b h) -> p h b", b=NB),
                                    ps[0:ROPE, 7, 32:96].rearrange("p (h b) -> p h b", b=NB)))
            misc_wait()
            misc_read(v.tensor_copy(qabs_f[:, :].rearrange("p (c b h) -> p c h b", c=2, b=NB),
                                    ps[:, 7, 0:128].rearrange("p (c h b) -> p c h b", c=2, b=NB)))
            qaf4 = qabs_f[:, :].rearrange("p (c b h) -> p c b h", c=2, b=NB)
            link(v.tensor_copy(qabs[:, :, :, 0:8], qaf4))
            link(v.tensor_tensor(out=qabs[:, :, :, 8:16], in0=qaf4, in1=qabs[:, :, :, 0:8].bitcast(F32), op=ALU.subtract))
            dve.wait_ge(kc_ready, 5)
            own = tmp_t[0:NB, 1792:2560]
            link(v.tensor_tensor(out=own, in0=q_s[:, :], in1=k_s[:, :], op=ALU.mult))
            link(v.tensor_reduce(out=dns[:, :], in_=own.rearrange("p (h e) -> p h e", e=QK), axis=AX, op=ALU.add))
            link(v.tensor_tensor(out=snew[:, :].rearrange("p (b h) -> p b h", b=NB), in0=rep(dns[:, :], 1, NB),
                                 in1=rep(newmask, 2, HM), op=ALU.add))

            def attention(jobs, n0, c0, mask, place, scale):
                def masks_max(n):
                    s = n % 2
                    dve.wait_ge(qk_done, n + 1)
                    if n - n0 >= 2:
                        dve.wait_ge(trp_done, CHUNK_END[n - 2])
                    a = amax[:, 4 * s:4 * s + 4]
                    parts = mask(jobs[n - n0], 3 * s, s)
                    for m, (out, src, msk) in enumerate(parts):
                        link(v.tensor_tensor_reduce(out=out, in0=src, in1=msk, scale=1.0,
                                                    scalar=NEG if m == 0 else a[:, 0:1], op0=ALU.add, op1=ALU.max,
                                                    accum_out=a[:, m:m + 1]))
                    m = len(parts) - 1
                    v.tensor_scalar(out=a[:, 2:3], in0=a[:, m:m + 1], scalar1=-scale, scalar2=None, op0=ALU.mult)\
                     .then_inc(masked, 1)

                chunk = c0
                masks_max(n0)
                for n in range(n0, n0 + len(jobs)):
                    s = n % 2
                    if n + 1 < n0 + len(jobs):
                        masks_max(n + 1)
                    for w in widths(jobs[n - n0][2]):
                        if chunk % 2 == 0:
                            pt_copy(dve, v.tensor_copy, chunk, w, pt_d, ())
                        chunk += 1
                    dve.wait_ge(exp_done, n + 1)
                    link(v.reciprocal(lsum[:, 2 + s:3 + s], lsum[:, s:s + 1]))
                    dve.wait_ge(pv_chunk, chunk)
                    out, src = place(jobs[n - n0], 3 * s)
                    v.tensor_scalar(out=out, in0=src, scalar1=lsum[:, 2 + s:3 + s], scalar2=None, op0=ALU.mult)\
                     .then_inc(o_done, 1)

            def mla_mask(job, bank0, s):
                w = job[2] * P
                return [(Pm[:, s, 0:w], ps[:, bank0, 0:w], masks[:, M_R4 - w:M_R4])]

            def mla_place(job, bank0):
                i, h, nb = job
                return oN[:, i, h * 64:(h + 1) * 64], ps[:, bank0 + 1, 0:64]

            dve.wait_ge(z_done, LAST_ITEM["TkM"] + 1)
            attention(MLA_JOBS, 0, 0, mla_mask, mla_place, MLA_SCALE)
            for g in range(ND):
                for t in range(5):
                    c = 5 * g + t
                    n = lanes(t)
                    z = take(ITEM[f"D{g}QK"] + t, n, 512, t == TS)
                    z3 = z.rearrange("p (h e) -> p h e", e=DH)
                    link(v.tensor_tensor(out=sqt[0:n, :], in0=z, in1=z, op=ALU.mult))
                    link(v.tensor_reduce(out=ms[0:n, 0:8], in_=sqt[0:n, :].rearrange("p (h e) -> p h e", e=DH),
                                         axis=AX, op=ALU.add))
                    inv_rms(n, 8, 1.0 / DH)
                    y = tmp[0:n, c % 2, :]
                    if c >= 2:
                        dve.wait_ge(rope_done, c - 1)
                    free_stage(v.tensor_tensor(out=y.rearrange("p (h e) -> p h e", e=DH), in0=z3,
                                               in1=rep(rsy[0:n, 0:8], 2, DH), op=ALU.mult))
                    for m, o in enumerate((G_DQ, G_DK)):
                        yh = y[:, m * BW:(m + 1) * BW].rearrange("p (h e) -> p h e", e=DH)
                        last = v.tensor_tensor(out=yh, in0=yh, in1=rep(gn[0:n, o + g * DH:o + (g + 1) * DH], 1, HD),
                                               op=ALU.mult)
                    last.then_inc(y_roped, 1)
                    dve.wait_ge(y_roped, 2 * c + 1)
                    if c >= 1:
                        dve.wait_ge(rope_done, c)
                    v.tensor_tensor(out=tmp[0:n, 2, :].rearrange("p (h e) -> p h e", e=DH),
                                    in0=y.rearrange("p (h e) -> p h e", e=DH),
                                    in1=rep(ropes[0:n, t, 0:64], 1, 2 * HD), op=ALU.mult).then_inc(y_roped, 1)
                wait_evac(dve, ITEM[f"D{g}V"] + TS)
                z = stage[0:NB, staged[0] % NSTAGE, 0:BW]
                staged[0] += 1
                free_stage(v.tensor_tensor(out=kv_s[:, g, BW:2 * BW], in0=z, in1=low_s[0:NB, 0:BW], op=ALU.add))
            dve.wait_ge(rope_done, 5 * ND)
            v.memset(flag[:, :], 0.0).then_inc(smp_ready, 1)

            def dil_mask(job, bank0, s):
                i = job[0]
                w0 = P if i == 0 else 2 * P
                w = (i + 1) * P
                both = masks[:, M_R4:M_R4 + 1024].rearrange("p (g c) -> p g c", g=2)[:, :, 512 - w:512]
                return [(Pm[:, s, 0:w0], ps[:, bank0, 0:w0], masks[:, M_ALL - w0:M_ALL]),
                        (Pm[:, s, w0:w0 + 2 * w].rearrange("p (g c) -> p g c", g=2),
                         ps[:, bank0 + 1:bank0 + 3, 0:w], both)]

            def dil_place(job, bank0):
                i, h, nb = job
                return oN[:, i, AW + h * 64:AW + (h + 1) * 64], ps[:, bank0, 256:320]

            dve.wait_ge(z_done, LAST_ITEM["TD"] + 1)
            attention(DIL_JOBS, len(MLA_JOBS), N_MLA_CHUNKS, dil_mask, dil_place, DIL_SCALE)
            for name, c0, w in (("GA", 0, AW), ("GB", AW, BW)):
                for t in range(NT):
                    idx = ITEM[name] + t
                    dve.wait_ge(act_half, READER[idx][1])
                    sg = stage[:, staged[0] % NSTAGE, 0:w]
                    staged[0] += 1
                    v.tensor_tensor(out=sg, in0=sg, in1=ps[:, idx % BANKS, 0:w], op=ALU.mult).then_inc(evac_d, 1)
                    dve.wait_ge(evac_d, READER[idx][1])
                    free_stage(v.tensor_tensor(out=oN[:, t, c0:c0 + w], in0=oN[:, t, c0:c0 + w], in1=sg, op=ALU.mult))
                    v.memset(flag[:, :], 0.0).then_inc(gated, 1)
                wait_evac(dve, ITEM[name + "s"])
                z = stage[0:NB, staged[0] % NSTAGE, 0:w]
                staged[0] += 1
                free_stage(v.tensor_tensor(out=mix_s[:, c0:c0 + w], in0=z, in1=low_s[0:NB, 0:w], op=ALU.add))
            dve.wait_ge(win_out, 16 * 3)
            for c in range(6):
                low_half(ITEM["To"] + c, oTlo[:, c, :], oThi[:, c, :])
            for n in range(2):
                for b, y in (("A", ya), ("B", yb)):
                    for t in range(NT):
                        z = take(ITEM[f"M{b}{n}"] + t, P, 512, False)
                        yt = y[:, t, n * 512:(n + 1) * 512]
                        free_stage(v.tensor_tensor(out=yt, in0=yt, in1=z, op=ALU.mult))
                        if b == "B":
                            yt2 = ya[:, t, n * 512:(n + 1) * 512]
                            v.tensor_tensor(out=yt2, in0=yt2, in1=yt, op=ALU.add).then_inc(merged, 1)
                    idx = ITEM[f"M{b}{n}"] + TS
                    wait_evac(dve, idx)
                    z = stage[0:NB, staged[0] % NSTAGE, 0:512]
                    staged[0] += 1
                    c0 = (0 if b == "A" else D) + n * 512
                    free_stage(v.tensor_tensor(out=merge_s[:, c0:c0 + 512], in0=z, in1=low_s[0:NB, :], op=ALU.add))
            for k in range(KD):
                low_half(ITEM["Tm"] + k, hTlo[:, k, :], hThi[:, k, :])
            for n in range(2):
                dve.wait_ge(xr_in[n], 16)
                for t in range(NT):
                    z = take(ITEM[f"WO{n}"] + t, P, 512, False)
                    link(v.tensor_tensor(out=z, in0=z, in1=gate_bc[:, n * 512:(n + 1) * 512], op=ALU.mult))
                    free_stage(v.tensor_tensor(out=xr[n][:, t, :], in0=xr[n][:, t, :], in1=z, op=ALU.add))
                    v.memset(flag[:, :], 0.0).then_inc(y_rdy, 1)
            dve.wait_ge(z_done, LAST_ITEM["WO1"] + 1)
            dve.wait_ge(y_out[0], 16)
            v.memset(Sc[:, NPAGE, :], NEG)
            base = [0]
            within = [0]

            def lstep_link(ins):
                within[0] += 1
                ins.then_inc(lstep, 1)
                dve.wait_ge(lstep, base[0] + within[0])

            def lat_rows(G, q):
                dve.wait_ge(ct_hi, G + 1)
                v.tensor_tensor(out=cTlo[:, q % 2, :], in0=psw(0, 1024), in1=cThi[:, q % 2, :].bitcast(F32),
                                op=ALU.subtract)
                v.tensor_copy(kpT[:, q % 2, :], ps[0:ROPE, 2, :]).then_inc(ct_ready, 1)

            def half_scores(h):
                t0 = 16 * h
                lstep_link(v.tensor_scalar(out=lx[:, :], in0=ssq[:, t0 * 8:t0 * 8 + 128], scalar1=1.0 / NOPE,
                                           scalar2=EPS, op0=ALU.mult, op1=ALU.add))
                rsqrt(lx[:, :], lax[:, :], ly[:, :], lstep_link)
                s3 = Sc[:, t0:t0 + 16, :]
                r3 = Sr[:, t0:t0 + 16, :]
                lstep_link(v.tensor_tensor(out=s3, in0=r3[:, :, 0:8], in1=r3[:, :, 8:16], op=ALU.add))
                lstep_link(v.tensor_tensor(out=s3, in0=s3, in1=ly[:, :].rearrange("p (t h) -> p t h", h=8), op=ALU.mult))
                lstep_link(v.tensor_tensor(out=s3, in0=s3, in1=r3[:, :, 16:24], op=ALU.add))

            def softmax_diag(b):
                dve.wait_ge(pmT_done, b + 1)
                lstep_link(v.tensor_reduce(out=mx1[0:HM, :], in_=ps[0:HM, 7, 0:P], axis=AX, op=ALU.max))
                v.tensor_scalar(out=dgm[0:HM, 0:HM], in0=ident[0:HM, 0:HM], scalar1=mx1[0:HM, :], scalar2=None,
                                op0=ALU.mult).then_inc(dg_ready, 1)

            def softmax_shift(b):
                dve.wait_ge(mx_done, b + 1)
                v.tensor_tensor(out=Sc[:, :, :], in0=Sc[:, :, :], in1=rep(ps[:, 7, P:P + HM], 1, 33), op=ALU.subtract)\
                 .then_inc(sub_done, 1)

            def softmax_sum(b):
                dve.wait_ge(ex_done, b + 1)
                v.tensor_reduce(out=esm[:, :], in_=Ex[:, :, :].rearrange("p t h -> p h t"), axis=AX, op=ALU.add)\
                 .then_inc(es_ready, 1)

            def latent(b):
                dve.wait_ge(pv_done, b + 1)
                lstep_link(v.reciprocal(rdn[:, :], ps[:, 7, P + 8:P + 16]))
                v.tensor_tensor(out=latT[:, bass.ds(16 * b, 16)].rearrange("p (c h) -> p c h", c=2),
                                in0=ps[:, 7, 256:272].rearrange("p (c h) -> p c h", c=2), in1=rep(rdn[:, :], 1, 2),
                                op=ALU.mult).then_inc(lat_done, 1)

            def batch(b, first, last):
                within[0] = 0
                base[0] = b * LSTEPS if first is False else 0
                for g in range(8):
                    if g == 0 and first:
                        lat_rows(8 * b, 0)
                    if not (last and g == 7):
                        lat_rows(8 * b + g + 1, g + 1)
                    for u in range(4):
                        if g == 2 and u == 2 and not first:
                            softmax_sum(b - 1)
                        dve.wait_ge(sq_done, NPAGE * b + 4 * g + u + 1)
                        v.tensor_reduce(out=ssq[:, (4 * g + u) * 8:(4 * g + u + 1) * 8],
                                        in_=sq4[:, u, :].rearrange("p (h e) -> p h e", e=NOPE), axis=AX, op=ALU.add)\
                         .then_inc(red_done, 1)
                    dve.wait_ge(s_done, 8 * b + g + 1)
                    v.tensor_copy(Sr[:, 4 * g:4 * g + 4, :],
                                  ps[:, 5 + g % 2, 0:96].rearrange("p (u n) -> p u n", u=4))\
                     .then_inc(s_read, 1)
                    if not first:
                        if g == 0:
                            softmax_diag(b - 1)
                        elif g == 1:
                            softmax_shift(b - 1)
                        elif g == 2:
                            latent(b - 1)
                    if g % 4 == 3:
                        dve.wait_ge(s_read, 8 * b + g + 1)
                        half_scores(g // 4)
                lstep_link(v.tensor_copy(Sc[0:NB, NPAGE, :], snew[:, bass.ds(8 * b, 8)]))
                v.tensor_reduce(out=pmx[:, :], in_=Sc[:, :, :].rearrange("p t h -> p h t"), axis=AX, op=ALU.max)\
                 .then_inc(pm_ready, 1)
                return within[0]

            n0 = batch(0, True, False)
            for _ in range(LSTEPS - n0):
                lstep_link(v.memset(flag[:, :], 0.0))
            with dve.Fori(0, (NB - 2) // 2) as i:
                assert batch(2 * i + 1, False, False) == LSTEPS
                assert batch(2 * i + 2, False, False) == LSTEPS
            assert batch(NB - 1, False, True) == LSTEPS
            softmax_diag(NB - 1)
            softmax_shift(NB - 1)
            softmax_sum(NB - 1)
            latent(NB - 1)
            def signal(ins, want):
                fcount[0] += 1
                assert fcount[0] == want, (fcount[0], want)
                ins.then_inc(f_dve, 1)
                dve.wait_ge(f_dve, want)

            dve.wait_ge(pv_done, NB)
            v.memset(SD_t[:, :], NEG)
            for b in range(NB):
                if b == 0:
                    dve.wait_ge(sdk_in[0], 48)
                if b == 6:
                    dve.wait_ge(sdk_in[1], 48)
                kv = (sdk0 if b < 6 else sdk1)[:, (b if b < 6 else b - 6) * ND:(b if b < 6 else b - 6) * ND + ND, 0:BW]
                dve.wait_ge(qb_done, b + 1)
                q0 = (1 + 2 * (b % 2)) * 512
                pr = prod[:, b % 2, :]
                v.tensor_tensor(out=pr.rearrange("p (g c) -> p g c", g=ND), in0=kv,
                                in1=psw(0, 4096)[:, q0:q0 + 768].rearrange("p (g c) -> p g c", g=ND), op=ALU.mult)\
                 .then_inc(qb_read, 1)
                dve.wait_ge(qb_read, b + 1)
                link(v.tensor_reduce(out=SD[:, b, 0:12], in_=pr.rearrange("p (n e) -> p n e", e=DH), axis=AX, op=ALU.add))
            pr = prod[0:NB, 0, :]
            link(v.tensor_tensor(out=pr.rearrange("p (g c) -> p g c", g=ND), in0=dq_s[:, :, :], in1=kv_s[:, :, 0:BW],
                                 op=ALU.mult))
            link(v.tensor_reduce(out=dn[:, 0:12], in_=pr.rearrange("p (n e) -> p n e", e=DH), axis=AX, op=ALU.add))
            link(v.tensor_tensor(out=SD[0:NB, :, 12:24], in0=rep(dn[:, 0:12], 1, NB), in1=rep(newmask, 2, 12), op=ALU.add))
            sd4 = SD_t[:, :].rearrange("p (b s h) -> p b h s", b=NB, h=HD)
            signal(v.tensor_reduce(out=dpm[:, :].rearrange("p (b h) -> p b h", b=NB), in_=sd4, axis=AX, op=ALU.max), F_MAX)
            dve.wait_ge(f_pe, 2)
            link(v.tensor_reduce(out=mx1[:, :], in_=ps[0:32, 5, 0:P], axis=AX, op=ALU.max))
            signal(v.tensor_scalar(out=dgm[:, :], in0=ident[0:32, 0:32], scalar1=mx1[:, :], scalar2=None, op0=ALU.mult),
                   F_DIAG)
            dve.wait_ge(f_pe, 3)
            signal(v.tensor_tensor(out=sd4, in0=sd4,
                                   in1=rep(ps[:, 5, 128:160].rearrange("p (b h) -> p b h", b=NB), 3, 6),
                                   op=ALU.subtract), F_SUB)
            dve.wait_ge(f_act, 1)
            ed4 = ED_t[:, :].rearrange("p (b s h) -> p b h s", b=NB, h=HD)
            signal(v.tensor_reduce(out=dsm[:, :].rearrange("p (b h) -> p b h", b=NB), in_=ed4, axis=AX, op=ALU.add), F_SUM)
            dve.wait_ge(f_pe, 4)
            link(v.reciprocal(rl[:, :], ps[:, 5, 160:192]))
            dve.wait_ge(f_pe, 5)
            for r in range(2):
                q = slice(64 * r, 64 * r + 64)
                last = v.tensor_tensor(out=obT[q, :].rearrange("p (a b) -> p b a", a=2),
                                       in0=ps[q, 6, 0:32].rearrange("p (b a r) -> p b a r", b=NB, a=2)[:, :, :, r],
                                       in1=rl[q, :].rearrange("p (b a r) -> p b a r", b=NB, a=2)[:, :, :, r], op=ALU.mult)
            signal(last, F_OBT)
            dve.wait_ge(f_act, 2)
            link(v.tensor_tensor(out=sgm[:, :], in0=sgm[:, :], in1=mix_s[:, :], op=ALU.mult))
            v.tensor_tensor(out=og[:, 0:AW], in0=sgm[:, 0:AW], in1=ps[0:NB, 0, 0:AW], op=ALU.mult)
            dve.wait_ge(f_pe, 6)
            signal(v.tensor_tensor(out=og[:, AW:768], in0=sgm[:, AW:768], in1=ps[0:NB, 7, 0:BW], op=ALU.mult), F_OG)
            dve.wait_ge(f_pe, 7)
            dve.wait_ge(zeroed, 6)
            osf = prod[:, 1, 0:48].rearrange("p (k n) -> p k n", n=NB)
            link(v.tensor_copy(osf, ps[:, 7, 256:304].rearrange("p (k n) -> p k n", n=NB)))
            signal(split_small(osf, osT, 6), F_OST)
            dve.wait_ge(f_act, 3)
            for n in range(2):
                for m, b in enumerate("AB"):
                    z = take(ITEM[f"P{b}s{n}"], NB, 512, True)
                    out = yab[:, m, n * 512:(n + 1) * 512]
                    free_stage(v.tensor_tensor(out=out, in0=z, in1=mgm[:, m * D + n * 512:m * D + (n + 1) * 512],
                                               op=ALU.mult))
            signal(v.tensor_tensor(out=yab[:, 0, :], in0=yab[:, 0, :], in1=yab[:, 1, :], op=ALU.add), F_MS)
            dve.wait_ge(f_pe, 8)
            msf = prod[:, 0, 0:64].rearrange("p (k n) -> p k n", n=NB)
            link(v.tensor_copy(msf, ps[:, 7, 320:384].rearrange("p (k n) -> p k n", n=NB)))
            signal(split_small(msf, hTs, KD), F_MST)
            dve.wait_ge(late_in, 32)
            for n in range(2):
                z = take(ITEM[f"WOs{n}"], NB, 512, True)
                c = slice(n * 512, (n + 1) * 512)
                link(v.tensor_tensor(out=z, in0=z, in1=gate_s[:, c], op=ALU.mult))
                free_stage(v.tensor_tensor(out=xs2[:, c], in0=xs2[:, c], in1=z, op=ALU.add))
            signal(v.memset(flag[:, :], 0.0), F_Y)


def _tables():
    q, k = np.arange(P)[:, None], np.arange(P)[None, :]
    none = np.zeros((P, P), bool)
    parts = [none] * 3 + [k > q]
    for d in (4, 16):
        r = (q - k) % d != 0
        parts += [r] * 3 + [r | (k > q)]
    parts += [k < q, k > q]
    masks = np.where(np.concatenate(parts, 1), np.float32(NEG), np.float32(0))
    own = np.zeros((P, 8), np.float32)
    own[:NB] = np.where(np.eye(NB, dtype=bool), 0, np.float32(NEG))
    tab = np.concatenate([np.eye(P, dtype=np.float32), masks, own], 1).astype(np.float32)
    pos = np.concatenate([np.arange(S), np.full(NB, PAST)]).astype(np.float32)
    cols = []
    for half in (DH // 2, ROPE // 2):
        inv = (10000.0 ** (-np.arange(half, dtype=np.float64) / half)).astype(np.float32)
        ang = (pos[:, None] * inv[None, :]).astype(np.float32)
        c, s = np.cos(ang.astype(np.float64)), np.sin(ang.astype(np.float64))
        cols += [c, c, -s, s]
    return tab, np.concatenate(cols, 1).astype(np.float32)


def kernel(**a):
    import concourse.bacc as bacc
    from concourse.bass_utils import run_bass_kernel_spmd

    a = {k: np.asarray(v) for k, v in a.items()}
    nc = bacc.Bacc("TRN2", target_bir_lowering=False, num_devices=1)
    tab, rope = _tables()
    arrays = {
        "x_prompt": a["x_prompt"][0], "x_sample": a["x_sample"][:, 0], "cache_mla": a["cache_mla"][0],
        "cw0": a["cache_win0"][0].reshape(NB, -1, 2 * BW), "cw1": a["cache_win1"][0].reshape(NB, -1, 2 * BW),
        "cw2": a["cache_win2"][0].reshape(NB, -1, 2 * BW), "page_table": a["page_table"],
        "c_prompt": a["c_prompt"], "c_sample": a["c_sample"], "b_ada": a["b_ada"][0],
        "w_ada": a["w_ada"][0], "w_in": a["w_in"][0], "w_qb": a["w_qb"][0],
        "w_uk": a["w_uk"][0].reshape(KVR, -1), "w_uv": a["w_uv"][0].reshape(KVR, -1),
        "w_pa": a["w_pa"][0], "w_pb": a["w_pb"][0], "w_out": a["w_out"][0],
        "gains": np.concatenate([a[n][0].reshape(-1) for n in (
            "mla_kv_norm", "mla_kr_g", "mla_qn_g", "mla_kn_g", "mla_qr_g", "dil_q_g", "dil_k_g")]),
        "cols": np.concatenate([a["norm_w"][0].reshape(KD, P).T, a["mla_qa_norm"][0].reshape(3, P).T], 1),
        "tables": tab, "rope": rope,
    }
    outs = [("y_prompt", (S, D)), ("y_sample", (NB, D)), ("rows_p", (S, CW)), ("win0_p", (P, 512)),
            ("win1_p", (S, 512)), ("win2_p", (S, 512)), ("rows_s", (NB, CW)), ("win0_s", (NB, 512)),
            ("win1_s", (NB, 512)), ("win2_s", (NB, 512))]
    arrays = {f"in_{k}": np.ascontiguousarray(x) for k, x in arrays.items()}
    aps = [nc.dram_tensor(k, x.shape, mybir.dt.from_np(x.dtype), kind="ExternalInput").ap() for k, x in arrays.items()]
    aps += [nc.dram_tensor(f"out_{k}", s, F32, kind="ExternalOutput").ap() for k, s in outs]
    trunk_step(nc, *aps)
    got = run_bass_kernel_spmd(nc, [arrays], core_ids=[0]).results[0]
    o = {k: got[f"out_{k}"] for k, _ in outs}
    win = (2, HD, DH)
    return (o["y_prompt"].reshape(1, S, D), o["y_sample"].reshape(NB, 1, D), o["rows_p"].reshape(1, 1, S, CW),
            o["win0_p"].reshape(1, 1, P, *win), o["win1_p"].reshape(1, 1, S, *win), o["win2_p"].reshape(1, 1, S, *win),
            o["rows_s"].reshape(1, NB, 1, CW), o["win0_s"].reshape(1, NB, 1, *win),
            o["win1_s"].reshape(1, NB, 1, *win), o["win2_s"].reshape(1, NB, 1, *win))
```

```python
from contextlib import ExitStack

import numpy as np

import concourse.bass as bass
from concourse import mybir

P = 128
F32 = mybir.dt.float32
F32R = mybir.dt.float32r
I32 = mybir.dt.int32
ALU = mybir.AluOpType
ACT = mybir.ActivationFunctionType
AX = mybir.AxisListType.X

D = 1024
S = 512
NT = S // P
TS = NT
NB = 8
PAST = 4096
NPAGE = PAST // P
HM, NOPE, ROPE = 8, 64, 32
QK = NOPE + ROPE
QR, KVR = 384, 256
CW = KVR + ROPE
ND, HD, DH = 3, 4, 64
BW = HD * DH
AW = HM * 64
PATTERNS = ((128, 1), (512, 4), (2048, 16))
MLA_SCALE = QK ** -0.5
DIL_SCALE = DH ** -0.5
EPS = 1e-6
NEG = -1e30
RSQRT_MAGIC = float(0x5F3759DF)
KD = D // P
LO = 64

C_Q, C_KV, C_D = 0, QR, QR + CW
C_GA = C_D + ND * 3 * BW
C_GB = C_GA + AW
C_MA = C_GB + BW
C_MB = C_MA + D

G_KV, G_KR, G_QN, G_KN, G_QR, G_DQ, G_DK = 0, 256, 288, 352, 416, 448, 640
G_ALL = 832

M_CAUSAL = 3 * P
M_R4, M_R16, M_PREV = 4 * P, 8 * P, 12 * P
M_ALL = 14 * P

BLOCKS = ([(f"ada{n}", "w_ada", 0, KD, n * 512, 512) for n in range(6)]
          + [("Q", "w_in", 0, KD, C_Q, QR), ("KV", "w_in", 0, KD, C_KV, CW)]
          + [(f"QB{i}", "w_qb", 0, QR // P, i * 384, 384) for i in range(2)]
          + [("V", "w_uv", 0, KVR // P, 0, AW)])
for _g in range(ND):
    BLOCKS += [(f"D{_g}QK", "w_in", 0, KD, C_D + _g * 3 * BW, 2 * BW),
               (f"D{_g}V", "w_in", 0, KD, C_D + _g * 3 * BW + 2 * BW, BW)]
BLOCKS += [("GA", "w_in", 0, KD, C_GA, AW), ("GB", "w_in", 0, KD, C_GB, BW)]
BLOCKS += [(f"P{_b}{n}", f"w_p{_b.lower()}", 0, k, n * 512, 512)
           for n in range(2) for _b, k in (("A", AW // P), ("B", BW // P))]
BLOCKS += [(f"M{_b}{n}", "w_in", 0, KD, c + n * 512, 512)
           for n in range(2) for _b, c in (("A", C_MA), ("B", C_MB))]
BLOCKS += [(f"WO{n}", "w_out", 0, KD, n * 512, 512) for n in range(2)]
BLOCKS += [(f"P{_b}s{n}", f"w_p{_b.lower()}", 0, k, n * 512, 512)
           for n in range(2) for _b, k in (("A", AW // P), ("B", BW // P))]
BLOCKS += [(f"WOs{n}", "w_out", 0, KD, n * 512, 512) for n in range(2)]
CHUNKS = []
FIRST = {}
COUNT = {}
WIDTH = {}
for _name, _w, _k0, _nk, _c, _width in BLOCKS:
    FIRST[_name], COUNT[_name], WIDTH[_name] = len(CHUNKS), _nk, _width
    CHUNKS += [(_w, k, _c, _width) for k in range(_nk)]

STAGES = ([("ada0", 1, "A"), ("ada1", 1, "A"), ("wukT", 2, "A"), ("xT", KD, "A")]
          + [(f"ada{n}", 1, "A") for n in range(2, 6)]
          + [("gate", 2, "A"), ("Q", 5, "A"), ("KV", 5, "A"), ("Tq", 3, "D"), ("QB0", 5, "A"), ("QB1", 5, "A"),
             ("Tr", 2, "D"), ("K", 5, "A"), ("V", 4, "A"), ("TqM", 8, "A"), ("TkM", 8, "A")])
for _g in range(ND):
    STAGES += [(f"D{_g}QK", 5, "A"), (f"D{_g}V", 5, "A")]
STAGES += [("TD", 4 * ND, "A"), ("GA", 4, "D"), ("GAs", 1, "A"), ("GB", 4, "D"), ("GBs", 1, "A"), ("To", 6, "D")]
STAGES += [(f"P{b}{n}", 4, "A") for n in range(2) for b in "AB"]
STAGES += [(f"M{b}{n}", 5, "A") for n in range(2) for b in "AB"]
STAGES += [("Tm", KD, "D"), ("WO0", 4, "A"), ("WO1", 4, "A")]
STAGES += [(f"P{b}s{n}", 1, "A") for n in range(2) for b in "AB"] + [("WOs0", 1, "A"), ("WOs1", 1, "A")]
ITEM = {}
READER = []
_seen = {"A": 0, "D": 0}
for _name, _n, _e in STAGES:
    ITEM[_name] = len(READER)
    for _ in range(_n):
        _seen[_e] += 1
        READER.append((_e, _seen[_e]))
BANKS = 7
LAST_ITEM = {n: ITEM[n] + c - 1 for n, c, _ in STAGES}
LAST_ITEM["GA"], LAST_ITEM["GB"] = ITEM["GAs"], ITEM["GBs"]
END_ITEM = {}
for _name, *_ in BLOCKS:
    END_ITEM[FIRST[_name] + COUNT[_name] - 1] = LAST_ITEM[_name]
NRAW, NHL = 4, 3
NSTAGE = 5

MLA_JOBS = [(i, h, i + 1) for i in range(NT) for h in range(HM)]
DIL_JOBS = [(i, h, (1 if i == 0 else 2) + 2 * (i + 1)) for i in range(NT) for h in range(HD)]


def widths(nb):
    return [min(4, nb - c) for c in range(0, nb, 4)]


CHUNK_END = [int(n) for n in np.cumsum([len(widths(j[2])) for j in MLA_JOBS + DIL_JOBS])]
N_MLA_CHUNKS = CHUNK_END[len(MLA_JOBS) - 1]

SMP_Q, SMP_R, SMP_KV = 1, 2, 3
F_MAX, F_DIAG, F_SUB, F_SUM, F_OBT, F_OG, F_OST, F_MS, F_MST, F_Y = range(1, 11)
LSTEPS = 32


def trunk_step(nc, x_prompt, x_sample, cache_mla, cw0, cw1, cw2, page_table, c_prompt, c_sample, b_ada,
               w_ada, w_in, w_qb, w_uk, w_uv, w_pa, w_pb, w_out, gains, cols, tables, rope,
               y_prompt, y_sample, rows_p, win0_p, win1_p, win2_p, rows_s, win0_s, win1_s, win2_s):
    weights = dict(w_ada=w_ada, w_in=w_in, w_qb=w_qb, w_uv=w_uv, w_pa=w_pa, w_pb=w_pb, w_out=w_out)
    ctx = ExitStack()
    with ctx:
        def sem(name):
            return ctx.enter_context(nc.semaphore(name))

        at = [16512]

        def region(nbytes):
            at[0] += nbytes
            assert at[0] <= 229344, at[0]
            return at[0] - nbytes

        def put(name, shape, offset, dt=F32):
            return nc.alloc_sbuf_tensor_at(name, [shape[0], int(np.prod(shape[1:]))], dt, offset=offset)

        def new(name, shape, dt=F32):
            n = int(np.prod(shape[1:])) * 4
            return put(name, shape, region((n + 31) // 32 * 32), dt)

        def v3(t, a, b):
            return t[:, :].rearrange("p (a b) -> p a b", a=a, b=b)

        def v4(t, a, b, c):
            return t[:, :].rearrange("p (a b c) -> p a b c", a=a, b=b, c=c)

        tab = new("tab", [P, P + M_ALL + 8])
        ident = tab[:, 0:P]
        masks = tab[:, P:P + M_ALL]
        newmask = tab[0:NB, P + M_ALL:P + M_ALL + 8]
        ones = new("ones", [P, P])
        dead = at[0]
        ropes_t = new("ropes", [P, 5 * 192])
        ropes = v3(ropes_t, 5, 192)
        gn = new("gn", [P, G_ALL])
        g96 = new("g96", [P, QK])
        q_s = new("q_s", [NB, HM * QK])
        assert at[0] - dead >= NB * KVR * 4
        lat_h = put("lat_h", [NB, NB * KVR], dead)
        colt = new("colt", [P, 11])
        raw_t = new("raw", [P, NRAW * 512])
        raw = v3(raw_t, NRAW, 512)
        whi_t = new("whi", [P, NHL * 512], F32R)
        whi = v3(whi_t, NHL, 512)
        wlo_t = new("wlo", [P, NHL * 512], F32R)
        wlo = v3(wlo_t, NHL, 512)
        wq_hi_t = new("wq_hi", [P, 2 * 2 * 264], F32R)
        wq_hi = v4(wq_hi_t, 2, 2, 264)
        wq_lo_t = new("wq_lo", [P, 2 * 2 * 264], F32R)
        wq_lo = v4(wq_lo_t, 2, 2, 264)
        wuk_hi, wuk_lo = wq_hi[:, :, :, 4:260], wq_lo[:, :, :, 4:260]
        hTs_t = new("hTs", [P, KD * P], F32R)
        hTs = v3(hTs_t, KD, P)
        rows_t = new("rows", [P, 5 * CW])
        rows = v3(rows_t, 5, CW)
        gate_bc = new("gate_bc", [P, D])
        gate_s = new("gate_s", [NB, D])
        kv_s_t = new("kv_s", [NB, ND * 512])
        kv_s = v3(kv_s_t, ND, 512)
        dq_s_t = new("dq_s", [NB, ND * BW])
        dq_s = v3(dq_s_t, ND, BW)
        small = region(4096)
        ms = put("ms", [P, 40], small)
        rsx = put("rsx", [P, 40], small + 160)
        rsa = put("rsa", [P, 40], small + 320)
        rsy = put("rsy", [P, 40], small + 480)
        pe1 = put("pe1", [P, 128], small + 640)
        pe2 = put("pe2", [P, 128], small + 1152)
        amax = put("amax", [P, 16], small + 2624)
        flag = put("flag", [1, 8], small + 2848)
        mx1 = put("mx1", [32, 1], small + 2880)
        dgm = put("dgm", [32, 32], small + 2944)
        dns = put("dns", [NB, 8], small + 2816)
        qsT = put("qsT", [P, 32], small + 1920)
        lsum = put("lsum", [P, 8], small + 2688)
        snew = put("snew", [NB, NB * HM], small + 1664)
        qabs = put("qabs", [P, (NB + 1) * 2 * HM], small + 2048)
        qpe = put("qpe", [P, NB * 4 * HM], small + 3072)

        W = region(22 * 1024)
        stage_t = put("stage", [P, NSTAGE * 512], W)
        stage = v3(stage_t, NSTAGE, 512)
        sqt = put("sqt", [P, 512], W + 10240)
        tmp_t = put("tmp", [P, 5 * 512], W + 12288)
        tmp = v3(tmp_t, 5, 512)
        PT_t = put("PT", [P, 3 * 512], W + 12288)
        PT = v3(PT_t, 3, 512)
        wukT_t = put("wukT", [P, 4 * KVR], W + 12288)
        wukT = v3(wukT_t, 4, KVR)
        qn_s = put("qn_s", [NB, HM * NOPE], W + 12288 + 4 * 1792)
        k_s = put("k_s", [NB, HM * QK], W + 16384)
        low_s = new("low_s", [NB + 1, 512])

        ON = region(12 * 1024)
        HT = region(32 * 1024)
        V = region(229344 - at[0])
        K1 = 1024
        assert 229344 - V >= 62 * K1, 229344 - V
        oN = v3(put("oN", [P, NT * 768], ON), NT, 768)
        hThi = v3(put("hT_hi", [P, KD * S], HT, F32R), KD, S)
        hTlo = v3(put("hT_lo", [P, KD * S], HT + 16 * K1, F32R), KD, S)
        wukr = v3(put("wuk_raw", [P, 2 * 512], ON), 2, 512)
        xsq = put("xsq", [P, D], ON + 4 * K1)
        xT = v3(put("xT", [P, KD * S], HT + 16 * K1), KD, S)
        xt = v3(put("x_tiles", [P, NT * D], V), NT, D)
        xs1 = put("x_s1", [NB, D], V + 16 * K1)
        cs = v3(put("c_split", [P, KD * P], V + 20 * K1, F32R), KD, P)
        c9 = put("c9", [NB + 1, D], V + 24 * K1)
        c9b = put("c9b", [NB + 1, D], V + 28 * K1)
        ada = put("ada", [NB + 1, 3 * D], V + 32 * K1)
        bada = put("bada", [NB + 1, 3 * D], V + 44 * K1)
        xTs = put("xTs", [P, KD * NB], V + 56 * K1)
        G1 = v3(put("G1", [P, KD * 9], V + 57 * K1), KD, 9)
        SH = v3(put("SH", [P, KD * 9], V + 57 * K1 + 512), KD, 9)
        hs_f = v3(put("hs_f", [P, KD * NB], V + 58 * K1), KD, NB)
        qh = v3(put("qh", [P, 8 * 384], ON), 8, 384)
        qan = v3(put("qan", [P, 5 * QR], V), 5, QR)
        qTm = v3(put("qTm", [QK, HM * S], V), HM, S)
        kTm = v3(put("kTm", [QK, HM * S], V + 16 * K1), HM, S)
        vm = v3(put("v_mla", [P, NT * AW], V + 32 * K1), NT, AW)
        qaThi = v3(put("qaT_hi", [P, 3 * S], V + 16 * K1, F32R), 3, S)
        qaTlo = v3(put("qaT_lo", [P, 3 * S], V + 22 * K1, F32R), 3, S)
        qaTs = v3(put("qaTs", [P, 3 * P], V + 28 * K1, F32R), 3, P)
        rTs = v3(put("rTs", [P, 2 * P], V + 30 * K1, F32R), 2, P)
        rThi = v3(put("rT_hi", [P, 2 * S], V + 40 * K1, F32R), 2, S)
        rTlo = v3(put("rT_lo", [P, 2 * S], V + 44 * K1, F32R), 2, S)
        kc = v3(put("kc", [P, NT * HM * QK], V + 48 * K1), NT, HM * QK)
        Pm_t = put("probs", [P, 2 * 1280], V + 48 * K1)
        Pm = {4: v3(Pm_t, 4, 640), 2: v3(Pm_t, 2, 1280)}
        kvo = v4(put("kvo", [P, ND * NT * 512], V), ND, NT, 512)
        dqT = v4(put("dqT", [P, ND * 2 * S], V + 24 * K1), ND, 2, S)
        dkT = v4(put("dkT", [P, ND * 2 * S], V + 36 * K1), ND, 2, S)
        dqn = v4(put("dqn", [P, ND * NT * BW], V + 48 * K1), ND, NT, BW)
        oThi = v3(put("oT_hi", [P, 6 * S], V, F32R), 6, S)
        oTlo = v3(put("oT_lo", [P, 6 * S], V + 12 * K1, F32R), 6, S)
        ya = v3(put("ya", [P, NT * D], V + 24 * K1), NT, D)
        yb = v3(put("yb", [P, NT * D], V + 40 * K1), NT, D)
        merge_s = put("merge_gates_s", [NB, 2 * D], V)
        mix_s = put("mix_gates_s", [NB, 768], V + 59 * K1)
        xr = [v3(put("x_again0", [P, NT * 512], V + 44 * K1), NT, 512),
              v3(put("x_again1", [P, NT * 512], ON), NT, 512)]
        cn = [v3(put(f"cn{p}", [P, NPAGE * CW], (V + 8 * K1, ON)[p]), NPAGE, CW) for p in range(2)]
        cThi = v3(put("cT_hi", [P, 2 * 1024], W, F32R), 2, 1024)
        cTlo = v3(put("cT_lo", [P, 2 * 1024], W + 8 * K1, F32R), 2, 1024)
        sq4 = v3(put("sq4", [P, 4 * 512], V + 44 * K1), 4, 512)
        kpT = v3(put("kpT", [P, 2 * P], V + 52 * K1), 2, P)
        kpn = v3(put("kpn", [P, 2 * P], V + 53 * K1), 2, P)
        HE = HT + 24 * K1
        Sq = v3(put("s_latent", [P, NPAGE * HM], HE), NPAGE, HM)
        Sk = v3(put("s_rotary", [P, NPAGE * HM], HE + K1), NPAGE, HM)
        ssq = put("ssq", [P, NPAGE * HM], HE + 3 * K1)
        lx = put("lx", [P, 128], HE + 4 * K1)
        lax = put("lax", [P, 128], HE + 4 * K1 + 512)
        ly = put("ly", [P, 128], HE + 5 * K1)
        Sc_t = put("scores", [P, 33 * HM], HE + 5 * K1 + 512)
        Sc = v3(Sc_t, 33, HM)
        Ex_t = put("expd", [P, 33 * HM], HE + 6 * K1 + 768)
        Ex = v3(Ex_t, 33, HM)
        latT = put("latT", [P, NB * 16], V + 56 * K1)
        pmx = put("pmx", [P, 8], V + 57 * K1)
        pt = put("pt", [1, NB * NPAGE], V + 58 * K1, I32)
        esm = put("esm", [P, 8], V + 57 * K1 + 256)
        rdn = put("rdn", [P, 8], V + 57 * K1 + 288)
        sdk0 = v3(put("sdk0", [P, 18 * 512], V + 8 * K1), 18, 512)
        sdk1 = v3(put("sdk1", [P, 6 * 512], V + 44 * K1), 6, 512)
        wuvr = v3(put("wuv_raw", [P, 2 * 512], ON), 2, 512)
        prod = v3(put("prod", [P, 2 * 768], ON + 4 * K1), 2, 768)
        SD_t = put("sd", [P, NB * 24], ON + 10 * K1)
        SD = v3(SD_t, NB, 24)
        ED_t = put("ed", [P, NB * 24], ON + 11 * K1)
        dn = put("dn", [NB, 16], ON + 12 * K1)
        dpm = put("dpm", [P, 32], ON + 12 * K1 + 64)
        dsm = put("dsm", [P, 32], ON + 12 * K1 + 192)
        rl = put("rl", [P, 32], ON + 12 * K1 + 320)
        obT = put("obT", [P, 2 * NB], ON + 12 * K1 + 448)
        osT = v3(put("osT", [P, 6 * P], ON + 13 * K1, F32R), 6, P)
        og = put("og", [NB, 768], ON + 16 * K1)
        sgm = put("sgm", [NB, 768], ON + 19 * K1)
        mgm = put("mgm", [NB, 2 * D], ON + 22 * K1)
        yab = v3(put("yab", [NB, 2 * D], ON + 30 * K1), 2, D)
        xs2 = put("x_s2", [NB, D], ON + 38 * K1)

        ps = ctx.enter_context(nc.psum_tensor("ps", [P, 8, 512], F32))

        def psw(bank, w):
            return ps[:, :, :].rearrange("p b c -> p (b c)")[:, bank * 512:bank * 512 + w]

        consts_in, c_in, wuk_in, bada_in = sem("consts_in"), sem("c_in"), sem("wuk_in"), sem("bada_in")
        x_in = [sem(f"x_in{t}") for t in range(5)]
        raw_in = [sem(f"raw_in{i}") for i in range(NRAW)]
        w_hi_ready, w_lo_ready, w_used = sem("w_hi_ready"), sem("w_lo_ready"), sem("w_used")
        z_done = sem("z_done")
        evac_a, evac_d = sem("evac_a"), sem("evac_d")
        act_half = sem("act_half")
        stage_free = sem("stage_free")
        even_done = sem("even_done")
        misc_done, misc_free = sem("misc_done"), sem("misc_free")
        dve_step = sem("dve_step")
        pool_step = sem("pool_step")
        zeroed, sigm_c, csilu, cs_ready, wuk_h, wuk_split = (
            sem("zeroed"), sem("sigm_c"), sem("csilu"), sem("cs_ready"), sem("wuk_h"), sem("wuk_split"))
        xn_ready, ada_ready, h_f, h_hi, h_ready = (
            sem("xn_ready"), sem("ada_ready"), sem("h_f"), sem("h_hi"), sem("h_ready"))
        qan_ready, rows_ready, qh_ready, kc_ready = (
            sem("qan_ready"), sem("rows_ready"), sem("qh_ready"), sem("kc_ready"))
        smp_ready = sem("smp_ready")
        y_roped, rope_done = sem("y_roped"), sem("rope_done")
        qk_done, masked, exp_done, tr_done, trp_done, pt_a, pt_d, pv_chunk, o_done = (
            sem("qk_done"), sem("masked"), sem("exp_done"), sem("tr_done"), sem("trp_done"), sem("pt_a"),
            sem("pt_d"), sem("pv_chunk"), sem("o_done"))
        rows_out, win_out, y_rdy, pt_in = sem("rows_out"), sem("win_out"), sem("y_rdy"), sem("pt_in")
        gated, merged = sem("gated"), sem("merged")
        xr_in = [sem(f"xr_in{n}") for n in range(2)]
        y_out = [sem(f"y_out{n}") for n in range(2)]
        cn_in = [[sem(f"cn_in{p}{q}") for q in range(4)] for p in range(2)]
        ct_done, ct_hi, ct_ready, k_done, sq_done, red_done, s_done, s_read = (
            sem("ct_done"), sem("ct_hi"), sem("ct_ready"), sem("k_done"), sem("sq_done"), sem("red_done"),
            sem("s_done"), sem("s_read"))
        pm_ready, pmT_done, dg_ready, mx_done, sub_done, ex_done, es_ready, pv_done, lat_done, lstep = (
            sem("pm_ready"), sem("pmT_done"), sem("dg_ready"), sem("mx_done"), sem("sub_done"), sem("ex_done"),
            sem("es_ready"), sem("pv_done"), sem("lat_done"), sem("lstep"))
        kpn_ready, lt_done, lt_ready = sem("kpn_ready"), sem("lt_done"), sem("lt_ready")
        sdk_in = [sem("sdk_in0"), sem("sdk_in1")]
        late_in = sem("late_in")
        qb_done, qb_read, f_pe, f_dve, f_act = (
            sem("qb_done"), sem("qb_read"), sem("f_pe"), sem("f_dve"), sem("f_act"))
        s_out = sem("s_out")

        def rep(ap, axis, n):
            u = ap.unsqueeze(axis)
            shape = list(u.shape)
            shape[axis] = n
            return u.to_broadcast(shape)

        def wait_used(eng, j):
            if j in END_ITEM:
                eng.wait_ge(z_done, END_ITEM[j] + 1)
            else:
                eng.wait_ge(w_used, sum(1 for i in range(j + 1) if i not in END_ITEM))

        def wait_evac(eng, idx):
            e, n = READER[idx]
            eng.wait_ge(evac_a if e == "A" else evac_d, n)

        def pt_copy(eng, fn, chunk, w, signal, extra):
            eng.wait_ge(trp_done, chunk + 1)
            if chunk >= 3:
                eng.wait_ge(pv_chunk, chunk - 2)
            fn(PT[:, chunk % 3, 0:w * P], ps[:, 6 + chunk % 2, 0:w * P], *extra).then_inc(signal, 1)

        def wait_pt(eng, c):
            if c % 2 == 0:
                eng.wait_ge(pt_d, c // 2 + 1)
            else:
                eng.wait_ge(pt_a, (c + 1) // 2)

        def lanes(t):
            return NB if t == TS else P

        block = ctx.enter_context(nc.Block())

        @block.sync
        def _(sp):
            done = [0]

            def stream_to(last):
                while done[0] < min(last, len(CHUNKS)):
                    j = done[0]
                    w, k, c, width = CHUNKS[j]
                    if j >= NRAW:
                        sp.wait_ge(w_lo_ready, j - NRAW + 1)
                    sp.dma_start(raw[:, j % NRAW, 0:width], weights[w][k * P:(k + 1) * P, c:c + width])\
                      .then_inc(raw_in[j % NRAW], 16)
                    done[0] += 1

            def load_page(p, quarter, index, tile, summed=None):
                page = sp.value_load(pt[0:1, bass.ds(index, 1)], min_val=0, max_val=cache_mla.shape[0] - 1)
                if summed is not None:
                    sp.wait_ge(pv_done, summed + 1)
                sp.dma_start(cn[p][:, bass.ds(tile, 1), :],
                             cache_mla[bass.ds(page, 1), :, :].rearrange("a p c -> p a c"))\
                  .then_inc(cn_in[p][quarter], 16)

            sp.dma_start(c9[0:NB, :], c_sample).then_inc(c_in, 16)
            sp.dma_start(c9[NB:NB + 1, :], c_prompt).then_inc(c_in, 16)
            sp.dma_start(tab[:, :], tables).then_inc(consts_in, 16)
            sp.dma_start(colt[:, :], cols).then_inc(consts_in, 16)
            stream_to(NRAW)
            sp.dma_start(wukr[:, :, :], w_uk.rearrange("(k p) n -> p k n", p=P)).then_inc(wuk_in, 16)
            sp.dma_start(bada[:, :], b_ada.rearrange("(a n) -> a n", a=1).to_broadcast([NB + 1, 3 * D]))\
              .then_inc(bada_in, 16)
            sp.dma_start(ropes[:, 0:NT, :], rope[0:S, :].rearrange("(t p) c -> p t c", p=P)).then_inc(consts_in, 16)
            sp.dma_start(ropes[0:NB, TS, :], rope[S:S + NB, :]).then_inc(consts_in, 16)
            sp.dma_start(gn[:, :], gains.rearrange("(a n) -> a n", a=1).to_broadcast([P, G_ALL]))\
              .then_inc(consts_in, 16)
            stream_to(FIRST["WO0"])
            sp.wait_ge(z_done, ITEM["To"] + 1)
            sp.dma_start(pt[:, :], page_table.rearrange("b n -> (b n)").rearrange("(a n) -> a n", a=1))\
              .then_inc(pt_in, 16)
            stream_to(FIRST["WO0"] + NRAW)
            sp.wait_ge(pt_in, 16)
            sp.wait_ge(z_done, LAST_ITEM["Tm"] + 1)
            n = 0
            for j in range(FIRST["WO0"] + NRAW, FIRST["PAs0"]):
                stream_to(j + 1)
                for _ in range(3):
                    if n < NPAGE:
                        load_page(0, n // 8, n, n)
                        n += 1
            stream_to(FIRST["PAs0"] + NRAW)
            sp.wait_ge(z_done, LAST_ITEM["WO1"] + 1)
            sp.wait_ge(y_out[1], 16)
            for quarter in range(4):
                with sp.Fori(0, 8) as u:
                    load_page(1, quarter, NPAGE + 8 * quarter + u, 8 * quarter + u)
            with sp.Fori(0, (NB - 2) // 2) as i:
                for p in range(2):
                    for quarter in range(4):
                        with sp.Fori(0, 8) as u:
                            load_page(p, quarter, 2 * NPAGE * i + (2 + p) * NPAGE + 8 * quarter + u, 8 * quarter + u,
                                      2 * i + p)
            wins = [cw[:, :, :].rearrange("b (r s) c -> r b s c", s=dil)[:, :, 0, :]
                    for cw, (_, dil) in zip((cw0, cw1, cw2), PATTERNS)]
            sp.wait_ge(pv_done, NB - 1)
            for g in range(ND):
                sp.dma_start(sdk0[:, :, :].rearrange("p (b g) c -> p b g c", g=ND)[:, :, g, :],
                             wins[g][:, 0:6, :]).then_inc(sdk_in[0], 16)
            sp.wait_ge(pv_done, NB)
            sp.wait_ge(red_done, NB * NPAGE)
            sp.wait_ge(ct_ready, NB * 8)
            for g in range(ND):
                sp.dma_start(sdk1[:, :, :].rearrange("p (b g) c -> p b g c", g=ND)[:, :, g, :],
                             wins[g][:, 6:8, :]).then_inc(sdk_in[1], 16)
            sp.dma_start(wuvr[:, :, :], w_uv.rearrange("(k p) n -> p k n", p=P)).then_inc(late_in, 16)
            sp.dma_start(xs2[:, :], x_sample).then_inc(late_in, 16)
            stream_to(len(CHUNKS))
            sp.wait_ge(f_dve, F_Y)
            sp.dma_start(y_sample, xs2[:, :]).then_inc(s_out, 16)
            sp.wait_ge(s_out, 16)
            sp.wait_ge(rows_out, 32)
            sp.wait_ge(win_out, 16 * 6)
            for n in range(2):
                sp.wait_ge(y_out[n], 16)

        @block.scalar
        def _(act):
            split = [0]
            staged = [0]
            lows = [0]

            def split_to(last):
                while split[0] < min(last, len(CHUNKS)):
                    j = split[0]
                    width = CHUNKS[j][3]
                    act.wait_ge(raw_in[j % NRAW], 16 * (j // NRAW + 1))
                    if j >= NHL:
                        wait_used(act, j - NHL)
                    nc.scalar.activation(whi[:, j % NHL, 0:width], raw[:, j % NRAW, 0:width], ACT.Copy)\
                      .then_inc(w_hi_ready, 1)
                    split[0] += 1

            def split_for(name):
                split_to(FIRST[name] + COUNT[name] + NHL)

            def bank(idx, w, n=P, start=0):
                return ps[start:start + n, idx % BANKS, 0:w]

            def copy_out(idx, out, w, n=P, func=ACT.Copy):
                act.wait_ge(z_done, idx + 1)
                nc.scalar.activation(out, bank(idx, w, n), func).then_inc(evac_a, 1)

            def next_stage():
                k = staged[0]
                staged[0] += 1
                if k >= NSTAGE:
                    act.wait_ge(stage_free, k - NSTAGE + 1)
                return stage[:, k % NSTAGE, :]

            def to_stage(idx, w, func=ACT.Copy):
                copy_out(idx, next_stage()[:, 0:w], w, func=func)

            def to_stage_small(idx, w, n=NB):
                out = next_stage()
                if lows[0]:
                    act.wait_ge(stage_free, lows[0])
                lows[0] = staged[0]
                act.wait_ge(z_done, idx + 1)
                nc.scalar.activation(out[0:n, 0:w], bank(idx, w, n), ACT.Copy)
                nc.scalar.activation(low_s[0:n, 0:w], bank(idx, w, n, LO), ACT.Copy).then_inc(evac_a, 1)

            def half(idx, out, func=ACT.Copy, scale=1.0):
                act.wait_ge(z_done, idx + 1)
                nc.scalar.activation(out, bank(idx, 512), func, scale=scale).then_inc(act_half, 1)

            def attention(jobs, n0, c0, slots, ahead, scale):
                def exp(n):
                    s = n % slots
                    w = jobs[n - n0][2] * P
                    act.wait_ge(masked, n + 1)
                    p = Pm[slots][:, s, 0:w]
                    nc.scalar.activation(p, p, ACT.Exp, bias=amax[:, 4 * s + 2:4 * s + 3],
                                         scale=scale, accum_out=lsum[:, s:s + 1]).then_inc(exp_done, 1)

                chunk = c0
                for n in range(n0, n0 + ahead):
                    exp(n)
                for n in range(n0, n0 + len(jobs)):
                    if n + ahead < n0 + len(jobs):
                        exp(n + ahead)
                    for w in widths(jobs[n - n0][2]):
                        if chunk % 2:
                            pt_copy(act, nc.scalar.activation, chunk, w, pt_a, (ACT.Copy,))
                        chunk += 1

            for t in range(NT):
                act.dma_start(xt[:, t, :], x_prompt[t * P:(t + 1) * P, :]).then_inc(x_in[t], 16)
            act.dma_start(xs1[:, :], x_sample).then_inc(x_in[TS], 16)
            act.wait_ge(c_in, 32)
            nc.scalar.activation(c9b[:, :], c9[:, :], ACT.Sigmoid).then_inc(sigm_c, 1)
            split_to(NHL)
            act.wait_ge(wuk_in, 16)
            nc.scalar.activation(wuk_hi, wukr[:, :, :].rearrange("p c (f n) -> p c f n", f=2), ACT.Copy)\
              .then_inc(wuk_h, 1)
            for n in range(2):
                split_for(f"ada{n}")
                to_stage_small(ITEM[f"ada{n}"], 512, NB + 1)
            for i in range(2):
                copy_out(ITEM["wukT"] + i, wukT_t[:, i * 512:(i + 1) * 512], 512)
            for k in range(KD):
                copy_out(ITEM["xT"] + k, xT[:, k, :], 512)
            for n in range(2, 6):
                split_for(f"ada{n}")
                to_stage_small(ITEM[f"ada{n}"], 512, NB + 1)
            for n in range(2):
                copy_out(ITEM["gate"] + n, gate_bc[:, n * 512:(n + 1) * 512], 512)
            for k in range(KD):
                act.wait_ge(h_f, k + 1)
                nc.scalar.activation(hThi[:, k, :], xT[:, k, :], ACT.Copy).then_inc(h_hi, 1)
            for name, w in (("Q", QR), ("KV", CW)):
                split_for(name)
                for t in range(NT):
                    to_stage(ITEM[name] + t, w)
                to_stage_small(ITEM[name] + TS, w)
            for c in range(3):
                half(ITEM["Tq"] + c, qaThi[:, c, :], scale=colt[:, KD + c:KD + c + 1])
            for i in range(2):
                split_for(f"QB{i}")
                for t in range(NT):
                    to_stage(ITEM[f"QB{i}"] + t, 384)
                to_stage_small(ITEM[f"QB{i}"] + TS, 384)
            for c in range(2):
                half(ITEM["Tr"] + c, rThi[:, c, :])
            for t in range(NT):
                to_stage(ITEM["K"] + t, 512)
            to_stage_small(ITEM["K"] + TS, 512)
            split_for("V")
            for t in range(NT):
                copy_out(ITEM["V"] + t, vm[:, t, :], 512)
            for i in range(2):
                for t in range(NT):
                    idx = ITEM["TqM"] + i * NT + t
                    copy_out(idx, qTm[:, 4 * i:4 * i + 4, t * P:(t + 1) * P], 512, QK)
            for t in range(NT):
                for i in range(2):
                    idx = ITEM["TkM"] + 2 * t + i
                    copy_out(idx, kTm[:, 4 * i:4 * i + 4, t * P:(t + 1) * P], 512, QK)
            attention(MLA_JOBS, 0, 0, 4, 2, MLA_SCALE)
            for g in range(ND):
                split_for(f"D{g}QK")
                for t in range(NT):
                    to_stage(ITEM[f"D{g}QK"] + t, 512)
                to_stage_small(ITEM[f"D{g}QK"] + TS, 512)
                split_for(f"D{g}V")
                for t in range(NT):
                    copy_out(ITEM[f"D{g}V"] + t, kvo[:, g, t, BW:2 * BW], BW)
                to_stage_small(ITEM[f"D{g}V"] + TS, BW)
            for i in range(4 * ND):
                g, is_k, p = i // 4, i // 2 % 2, i % 2
                copy_out(ITEM["TD"] + i, (dkT if is_k else dqT)[:, g, p, :], 512)
            attention(DIL_JOBS, len(MLA_JOBS), N_MLA_CHUNKS, 2, 1, DIL_SCALE)
            for name, w in (("GA", AW), ("GB", BW)):
                split_for(name)
                for t in range(NT):
                    act.wait_ge(z_done, ITEM[name] + t + 1)
                    out = next_stage()
                    nc.scalar.activation(out[:, 0:w], bank(ITEM[name] + t, w), ACT.Sigmoid).then_inc(act_half, 1)
                to_stage_small(ITEM[name + "s"], w)
            act.wait_ge(win_out, 16 * 3)
            for c in range(6):
                half(ITEM["To"] + c, oThi[:, c, :])
            for n in range(2):
                for b, out in (("A", ya), ("B", yb)):
                    split_for(f"P{b}{n}")
                    for t in range(NT):
                        copy_out(ITEM[f"P{b}{n}"] + t, out[:, t, n * 512:(n + 1) * 512], 512)
            act.dma_start(xr[1][:, :, :], x_prompt[:, 512:1024].rearrange("(t p) c -> p t c", p=P))\
               .then_inc(xr_in[1], 16)
            for n in range(2):
                for b in "AB":
                    split_for(f"M{b}{n}")
                    for t in range(NT):
                        to_stage(ITEM[f"M{b}{n}"] + t, 512, ACT.Sigmoid)
                    to_stage_small(ITEM[f"M{b}{n}"] + TS, 512)
            for k in range(KD):
                half(ITEM["Tm"] + k, hThi[:, k, :])
            act.wait_ge(merged, 2 * NT)
            act.dma_start(xr[0][:, :, :], x_prompt[:, 0:512].rearrange("(t p) c -> p t c", p=P))\
               .then_inc(xr_in[0], 16)
            for n in range(2):
                split_for(f"WO{n}")
                for t in range(NT):
                    to_stage(ITEM[f"WO{n}"] + t, 512)
            act.wait_ge(stage_free, staged[0])
            act.wait_ge(y_out[0], 16)

            def hi_rows(G, q):
                act.wait_ge(ct_done, G + 1)
                if not (isinstance(G, int) and G < 2):
                    act.wait_ge(k_done, 4 * G - 4)
                nc.scalar.activation(cThi[:, q % 2, :], psw(0, 1024), ACT.Copy).then_inc(ct_hi, 1)

            def rotary_keys(G, g, p, turn):
                if g % 2 == 0:
                    act.wait_ge(cn_in[p][g // 2], 128 * turn + 128)
                if not (isinstance(G, int) and G < 2):
                    act.wait_ge(ct_done, G - 1)
                nc.scalar.activation(kpn[:, g % 2, :].rearrange("p (u e) -> p u e", u=4),
                                     cn[p][:, 4 * g:4 * g + 4, KVR:CW], ACT.Copy).then_inc(kpn_ready, 1)

            def batch(b, p, turn, next_turn, first, last):
                k0 = 4 - 4 * p
                s0 = 256 * p
                for g in range(8):
                    if g == 0 and first:
                        rotary_keys(8 * b, 0, p, turn)
                        rotary_keys(8 * b + 1, 1, p, turn)
                        hi_rows(b * 8, 0)
                    if not (last and g == 7):
                        hi_rows(b * 8 + g + 1, g + 1)
                    for u in range(4):
                        U = b * NPAGE + 4 * g + u
                        act.wait_ge(k_done, U + 1)
                        if not (first and 4 * g + u < 4):
                            act.wait_ge(red_done, U - 3)
                        kb = ps[:, 3 + 2 * (u % 2):5 + 2 * (u % 2), :]
                        nc.scalar.activation(Sq[:, 4 * g + u, :].rearrange("p (f h) -> p f h", f=2),
                                             kb[:, :, s0:s0 + 4], ACT.Copy)
                        nc.scalar.activation(sq4[:, u, :].rearrange("p (f n) -> p f n", f=2),
                                             kb[:, :, k0:k0 + 256], ACT.Square).then_inc(sq_done, 1)
                        if u == 2 and g < 6:
                            rotary_keys(8 * b + g + 2, g + 2, p, turn)
                        elif u == 2 and not last:
                            rotary_keys(8 * b + g + 2, g - 6, 1 - p, next_turn)
                        if g == 4 and u == 0 and not first:
                            expo(b - 1)

            def expo(b):
                act.wait_ge(sub_done, b + 1)
                nc.scalar.activation(Ex_t[:, :], Sc_t[:, :], ACT.Exp, scale=MLA_SCALE).then_inc(ex_done, 1)

            batch(0, 0, 0, 0, True, False)
            with act.Fori(0, (NB - 2) // 2) as i:
                batch(2 * i + 1, 1, i, i + 1, False, False)
                batch(2 * i + 2, 0, i + 1, i + 1, False, False)
            batch(NB - 1, 1, (NB - 1) // 2, 0, False, True)
            expo(NB - 1)
            act.wait_ge(f_dve, F_SUB)
            nc.scalar.activation(ED_t[:, :], SD_t[:, :], ACT.Exp, scale=DIL_SCALE).then_inc(f_act, 1)
            nc.scalar.activation(sgm[:, :], mix_s[:, :], ACT.Sigmoid).then_inc(f_act, 1)
            nc.scalar.activation(mgm[:, :], merge_s[:, :], ACT.Sigmoid).then_inc(f_act, 1)
            for n in range(2):
                for b in "AB":
                    split_for(f"P{b}s{n}")
                    to_stage_small(ITEM[f"P{b}s{n}"], 512)
            for n in range(2):
                split_for(f"WOs{n}")
                to_stage_small(ITEM[f"WOs{n}"], 512)

        @block.gpsimd
        def _(pool):
            low = [0]
            steps = [0]

            def link(ins):
                steps[0] += 1
                ins.then_inc(pool_step, 1)
                pool.wait_ge(pool_step, steps[0])

            def low_to(last):
                while low[0] < min(last, len(CHUNKS)):
                    j = low[0]
                    width = CHUNKS[j][3]
                    pool.wait_ge(w_hi_ready, j + 1)
                    nc.gpsimd.tensor_tensor(out=wlo[:, j % NHL, 0:width], in0=raw[:, j % NRAW, 0:width],
                                            in1=whi[:, j % NHL, 0:width].bitcast(F32), op=ALU.subtract)\
                      .then_inc(w_lo_ready, 1)
                    low[0] += 1

            def rotate(g, t, c):
                n = lanes(t)
                y = tmp[0:n, c % 2, :].rearrange("p (h e) -> p h e", e=DH)
                t1 = tmp[0:n, 2, :]
                t2 = tmp[0:n, 3, :].rearrange("p (h e) -> p h e", e=DH)
                sin = ropes[0:n, t, 64:128]
                pool.wait_ge(y_roped, 2 * c + 1)
                if c:
                    pool.wait_ge(rope_done, c)
                nc.gpsimd.tensor_tensor(out=t2[:, :, 0:32], in0=y[:, :, 32:64], in1=rep(sin[:, 0:32], 1, 8), op=ALU.mult)
                link(nc.gpsimd.tensor_tensor(out=t2[:, :, 32:64], in0=y[:, :, 0:32], in1=rep(sin[:, 32:64], 1, 8),
                                             op=ALU.mult))
                pool.wait_ge(y_roped, 2 * c + 2)
                q_out = dq_s[:, g, :] if t == TS else dqn[:, g, t, :]
                k_out = kv_s[:, g, 0:BW] if t == TS else kvo[:, g, t, 0:BW]
                t2f = tmp[0:n, 3, :]
                nc.gpsimd.tensor_tensor(out=q_out, in0=t1[:, 0:BW], in1=t2f[:, 0:BW], op=ALU.add)
                nc.gpsimd.tensor_tensor(out=k_out, in0=t1[:, BW:2 * BW], in1=t2f[:, BW:2 * BW], op=ALU.add)\
                  .then_inc(rope_done, 1)

            nc.gpsimd.memset(ones[:, :], 1.0).then_inc(zeroed, 1)
            nc.gpsimd.memset(cs[:, :, :].bitcast(F32), 0.0).then_inc(zeroed, 1)
            nc.gpsimd.memset(hTs[:, :, :].bitcast(F32), 0.0).then_inc(zeroed, 1)
            low_to(NHL)
            pool.wait_ge(cs_ready, 1)
            nc.gpsimd.memset(qaTs[:, :, :].bitcast(F32), 0.0).then_inc(zeroed, 1)
            nc.gpsimd.memset(rTs[:, :, :].bitcast(F32), 0.0).then_inc(zeroed, 1)
            low_to(FIRST["D0QK"] + NHL)
            pool.wait_ge(rows_ready, 5)
            pool.dma_start(rows_p.rearrange("(t p) c -> p t c", p=P), rows[:, 0:NT, :]).then_inc(rows_out, 16)
            pool.dma_start(rows_s, rows[0:NB, TS, :]).then_inc(rows_out, 16)
            for g in range(ND):
                low_to(FIRST[f"D{g}QK"] + COUNT[f"D{g}QK"] + NHL)
                for t in range(5):
                    rotate(g, t, 5 * g + t)
                    low_to(low[0] + 1)
                low_to(FIRST[f"D{g}V"] + COUNT[f"D{g}V"] + NHL)
            wait_evac(pool, ITEM[f"D{ND - 1}V"] + TS)
            pool.dma_start(win0_p, kvo[:, 0, NT - 1, :]).then_inc(win_out, 16)
            for g, out in ((1, win1_p), (2, win2_p)):
                pool.dma_start(out.rearrange("(t p) c -> p t c", p=P), kvo[:, g, :, :]).then_inc(win_out, 16)
            low_to(FIRST["WO0"])
            pool.wait_ge(smp_ready, SMP_KV)
            for g, out in enumerate((win0_s, win1_s, win2_s)):
                pool.dma_start(out, kv_s[:, g, :]).then_inc(win_out, 16)
            for n in range(2):
                low_to(FIRST[f"WO{n}"] + COUNT[f"WO{n}"] + NHL)
                pool.wait_ge(y_rdy, NT * (n + 1))
                pool.dma_start(y_prompt[:, n * 512:(n + 1) * 512].rearrange("(t p) c -> p t c", p=P), xr[n][:, :, :])\
                    .then_inc(y_out[n], 16)
            pool.wait_ge(pv_done, NB)
            nc.gpsimd.memset(osT[:, :, :].bitcast(F32), 0.0).then_inc(zeroed, 1)
            low_to(len(CHUNKS))

        @block.tensor
        def _(pe):
            mm = nc.tensor.matmul
            miscs = [0]

            def wait_bank(idx):
                if idx >= BANKS:
                    wait_evac(pe, idx - BANKS)

            def misc_begin():
                if miscs[0]:
                    pe.wait_ge(misc_free, miscs[0])
                miscs[0] += 1

            def block_of(name, first, tiles, hi=None, lo=None, small=None):
                f, nk, w = FIRST[name], COUNT[name], WIDTH[name]
                for k in range(nk):
                    j = f + k
                    pe.wait_ge(w_lo_ready, j + 1)
                    bh, bl = whi[:, j % NHL, 0:w], wlo[:, j % NHL, 0:w]
                    for n, t in enumerate(tiles):
                        idx = first + n
                        if k == 0:
                            wait_bank(idx)
                        out = ps[:, idx % BANKS, 0:w]
                        st, en = k == 0, k == nk - 1
                        if t == TS:
                            mm(out, small[:, k, :], bh, start=st, stop=False)
                            last = mm(out, small[:, k, :], bl, start=False, stop=en)
                        else:
                            c = slice(t * P, (t + 1) * P)
                            mm(out, hi[:, k, c], bh, start=st, stop=False)
                            mm(out, hi[:, k, c], bl, start=False, stop=False)
                            last = mm(out, lo[:, k, c], bh, start=False, stop=en)
                        if en:
                            last.then_inc(z_done, 1)
                    if k < nk - 1:
                        last.then_inc(w_used, 1)

            def transposes(idx, parts, n_in=P):
                wait_bank(idx)
                for col, rows_out_, src in parts:
                    last = nc.tensor.transpose(ps[0:rows_out_, idx % BANKS, col:col + n_in], src, ident[0:n_in, 0:n_in])
                last.then_inc(z_done, 1)

            def misc_transposes(parts, n_in):
                misc_begin()
                for col, rows_out_, src in parts:
                    last = nc.tensor.transpose(ps[0:rows_out_, 7, col:col + n_in], src, ident[0:n_in, 0:n_in])
                last.then_inc(misc_done, 1)

            pe.wait_ge(consts_in, 80)
            pe.wait_ge(csilu, 1)
            misc_transposes([(9 * k, P, c9b[0:9, k * P:(k + 1) * P]) for k in range(KD)], NB + 1)
            pe.wait_ge(cs_ready, 1)
            for n in range(2):
                block_of(f"ada{n}", ITEM[f"ada{n}"], [TS], small=cs)
            pe.wait_ge(wuk_in, 16)
            for i in range(2):
                transposes(ITEM["wukT"] + i, [(2 * P * q + P * r, P, wukr[:, r, (2 * i + q) * P:(2 * i + q + 1) * P])
                                              for q in range(2) for r in range(2)])
            pe.wait_ge(xn_ready, 5)
            for k in range(KD):
                transposes(ITEM["xT"] + k, [(t * P, P, xt[:, t, k * P:(k + 1) * P]) for t in range(NT)])
            misc_transposes([(NB * k, P, xs1[:, k * P:(k + 1) * P]) for k in range(KD)], NB)
            for n in range(2, 6):
                block_of(f"ada{n}", ITEM[f"ada{n}"], [TS], small=cs)
            pe.wait_ge(ada_ready, 6)
            misc_transposes([(9 * k, P, ada[:, k * P:(k + 1) * P]) for k in range(2 * KD)], NB + 1)
            for n in range(2):
                idx = ITEM["gate"] + n
                wait_bank(idx)
                mm(ps[:, idx % BANKS, :], ident[0:NB + 1, NB:NB + 1].to_broadcast([NB + 1, P]),
                   ada[:, 2 * D + n * 512:2 * D + (n + 1) * 512], start=True, stop=True).then_inc(z_done, 1)
            pe.wait_ge(h_ready, KD + 1)
            for name in ("Q", "KV"):
                block_of(name, ITEM[name], range(5), hThi, hTlo, hTs)
            pe.wait_ge(qan_ready, 1)
            for c in range(3):
                transposes(ITEM["Tq"] + c, [(t * P, P, qan[:, t, c * P:(c + 1) * P]) for t in range(NT)])
            misc_transposes([(NB * c, P, qan[0:NB, TS, c * P:(c + 1) * P]) for c in range(3)], NB)
            wait_evac(pe, ITEM["Tq"] + 2)
            pe.wait_ge(smp_ready, SMP_Q)
            for i in range(2):
                block_of(f"QB{i}", ITEM[f"QB{i}"], range(5), qaThi, qaTlo, qaTs)
            pe.wait_ge(rows_ready, 5)
            for c in range(2):
                transposes(ITEM["Tr"] + c, [(t * P, P, rows[:, t, c * P:(c + 1) * P]) for t in range(NT)])
            misc_transposes([(NB * c, P, rows[0:NB, TS, c * P:(c + 1) * P]) for c in range(2)], NB)
            wait_evac(pe, ITEM["Tr"] + 1)
            pe.wait_ge(smp_ready, SMP_R)
            for t in range(5):
                idx = ITEM["K"] + t
                wait_bank(idx)
                for k in range(2):
                    if t == TS:
                        pairs = [(rTs[:, k, :], wuk_hi[:, k, :]), (rTs[:, k, :], wuk_lo[:, k, :])]
                    else:
                        c = slice(t * P, (t + 1) * P)
                        pairs = [(rThi[:, k, c], wuk_hi[:, k, :]), (rThi[:, k, c], wuk_lo[:, k, :]),
                                 (rTlo[:, k, c], wuk_hi[:, k, :])]
                    for m, (a, b) in enumerate(pairs):
                        last = mm(ps[:, idx % BANKS, :].rearrange("p (f n) -> p f n", f=2), a, b, start=k == 0 and m == 0,
                                  stop=k == 1 and m == len(pairs) - 1)
                last.then_inc(z_done, 1)
            block_of("V", ITEM["V"], range(NT), rThi, rTlo)
            for i in range(2):
                for t in range(NT):
                    pe.wait_ge(qh_ready, 5 * i + t + 1)
                    transposes(ITEM["TqM"] + i * NT + t,
                               [(m * P, QK, qh[:, i * NT + t, m * QK:(m + 1) * QK]) for m in range(4)])
            pe.wait_ge(qh_ready, 10)
            misc_begin()
            for p in range(4):
                nc.tensor.transpose(ps[:, 7, NB * p:NB * p + NB],
                                    qn_s[:, p * P:(p + 1) * P],
                                    ident[0:NB, 0:NB])
            for h in range(HM):
                last = nc.tensor.transpose(ps[0:ROPE, 7, 32 + NB * h:32 + NB * h + NB],
                                           q_s[:, h * QK + NOPE:(h + 1) * QK], ident[0:NB, 0:NB])
            last.then_inc(misc_done, 1)
            misc_begin()
            for odd in range(2):
                o = 64 * odd
                for c in range(2):
                    for h in range(odd, HM, 2):
                        last = mm(ps[:, 7, c * 64 + h * NB:c * 64 + (h + 1) * NB],
                                  wukT[o:o + 64, h // 2, c * P:(c + 1) * P],
                                  qsT[o:o + 64, h // 2 * NB:(h // 2 + 1) * NB], start=True, stop=True)
                if odd == 0:
                    last.then_inc(even_done, 1)
                    pe.wait_ge(even_done, 1)
            last.then_inc(misc_done, 1)
            for t in range(NT):
                pe.wait_ge(kc_ready, t + 1)
                for i in range(2):
                    transposes(ITEM["TkM"] + 2 * t + i,
                               [(m * P, QK, kc[:, t, (4 * i + m) * QK:(4 * i + m + 1) * QK]) for m in range(4)])

            def attention(jobs, n0, c0, first_idx, slots, outs, scores, values):
                wait_evac(pe, first_idx)
                pe.wait_ge(misc_free, miscs[0])
                end = n0 + len(jobs)

                def qk(n):
                    if n - n0 >= slots:
                        pe.wait_ge(masked, n - slots + 1)
                    scores(jobs[n - n0], n).then_inc(qk_done, 1)

                chunk = c0
                for n in range(n0, n0 + slots):
                    qk(n)
                for n in range(n0, end):
                    s = n % slots
                    pe.wait_ge(exp_done, n + 1)
                    ws = widths(jobs[n - n0][2])

                    def tr(m):
                        c = chunk + m
                        if c - c0 >= 2:
                            wait_pt(pe, c - 2)
                        for q in range(ws[m]):
                            last = nc.tensor.transpose(ps[:, 6 + c % 2, q * P:(q + 1) * P],
                                                       Pm[slots][:, s, (4 * m + q) * P:(4 * m + q + 1) * P], ident)
                        last.then_inc(trp_done, 1)

                    tr(0)
                    if n + slots < end:
                        qk(n + slots)
                    out, vals = values(jobs[n - n0], n)
                    if n - n0 >= outs:
                        pe.wait_ge(o_done, n - outs + 1)
                    for m in range(len(ws)):
                        if m + 1 < len(ws):
                            tr(m + 1)
                        c = chunk + m
                        wait_pt(pe, c)
                        for q in range(ws[m]):
                            b = 4 * m + q
                            last = mm(out, PT[:, c % 3, q * P:(q + 1) * P], vals[b], start=b == 0,
                                      stop=b == len(vals) - 1)
                        last.then_inc(pv_chunk, 1)
                    chunk += len(ws)
                pe.wait_ge(o_done, end)

            def mla_scores(job, n):
                i, h, nb = job
                return mm(ps[:, n % 4, 0:nb * P], qTm[:, h, i * P:(i + 1) * P], kTm[:, h, 0:nb * P],
                          start=True, stop=True)

            def mla_values(job, n):
                i, h, nb = job
                return ps[:, 4 + n % 2, 0:64], [vm[:, b, h * 64:(h + 1) * 64] for b in range(nb)]

            attention(MLA_JOBS, 0, 0, LAST_ITEM["TkM"], 4, 2, mla_scores, mla_values)
            for g in range(ND):
                block_of(f"D{g}QK", ITEM[f"D{g}QK"], range(5), hThi, hTlo, hTs)
                block_of(f"D{g}V", ITEM[f"D{g}V"], range(5), hThi, hTlo, hTs)
            for i in range(4 * ND):
                g, is_k, p = i // 4, i // 2 % 2, i % 2
                pe.wait_ge(rope_done, 5 * g + NT)
                transposes(ITEM["TD"] + i,
                           [(t * P, P, (kvo if is_k else dqn)[:, g, t, p * P:(p + 1) * P]) for t in range(NT)])

            def dil_scores(job, n):
                i, h, nb = job
                r = slice(64 * (h % 2), 64 * (h % 2) + 64)
                for g in (1, 2, 0):
                    lo = max(0, i - 1) if g == 0 else 0
                    if g == 0 and n > len(MLA_JOBS):
                        pe.wait_ge(masked, n)
                    bank, c = (2 * (n % 2) + g - 1, 0) if g else (4, 256 * (n % 2))
                    last = mm(ps[:, bank, c:c + (i + 1 - lo) * P], dqT[r, g, h // 2, i * P:(i + 1) * P],
                              dkT[r, g, h // 2, lo * P:(i + 1) * P], start=True, stop=True)
                return last

            def dil_values(job, n):
                i, h, nb = job
                blocks = [(g, b) for g in range(ND) for b in range(max(0, i - 1) if g == 0 else 0, i + 1)]
                return ps[:, 5, 0:64], [kvo[:, g, b, BW + h * 64:BW + (h + 1) * 64] for g, b in blocks]

            attention(DIL_JOBS, len(MLA_JOBS), N_MLA_CHUNKS, LAST_ITEM["TD"], 2, 1, dil_scores, dil_values)
            for name in ("GA", "GB"):
                block_of(name, ITEM[name], range(5), hThi, hTlo, hTs)
            pe.wait_ge(gated, 2 * NT)
            for c in range(6):
                transposes(ITEM["To"] + c, [(t * P, P, oN[:, t, c * P:(c + 1) * P]) for t in range(NT)])
            wait_evac(pe, ITEM["To"] + 5)
            for n in range(2):
                block_of(f"PA{n}", ITEM[f"PA{n}"], range(NT), oThi, oTlo)
                block_of(f"PB{n}", ITEM[f"PB{n}"], range(NT), oThi[:, 4:6, :], oTlo[:, 4:6, :])
            for n in range(2):
                for b in "AB":
                    block_of(f"M{b}{n}", ITEM[f"M{b}{n}"], range(5), hThi, hTlo, hTs)
            pe.wait_ge(merged, 2 * NT)
            for k in range(KD):
                transposes(ITEM["Tm"] + k, [(t * P, P, ya[:, t, k * P:(k + 1) * P]) for t in range(NT)])
            wait_evac(pe, ITEM["Tm"] + KD - 1)
            for n in range(2):
                block_of(f"WO{n}", ITEM[f"WO{n}"], range(NT), hThi, hTlo)
            wait_evac(pe, LAST_ITEM["WO1"])

            def group_in(b, g, p, turn):
                G = 8 * b + g
                if g % 2 == 0:
                    pe.wait_ge(cn_in[p][g // 2], 128 * turn + 128)
                if not (isinstance(G, int) and G == 0):
                    pe.wait_ge(ct_ready, G)
                if not (isinstance(G, int) and G < 2):
                    pe.wait_ge(s_read, G - 1)
                for u in range(4):
                    src = cn[p][:, 4 * g + u, :]
                    for c in range(2):
                        nc.tensor.transpose(ps[:, c, u * P:(u + 1) * P], src[:, c * P:(c + 1) * P], ident)
                pe.wait_ge(kpn_ready, G + 1)
                nc.tensor.transpose(ps[:, 2, 0:P], kpn[:, g % 2, :], ident).then_inc(ct_done, 1)

            def group_products(b, g, p, last_group):
                w = slice(4 * p, 4 * p + 260)
                G = 8 * b + g
                q = g % 2
                pe.wait_ge(ct_ready, G + 1)
                for u in range(4):
                    U = 4 * G + u
                    if not (isinstance(U, int) and U < 2):
                        pe.wait_ge(sq_done, U - 1)
                    hi = [cThi[:, q, c * 512 + u * P:c * 512 + (u + 1) * P] for c in range(2)]
                    lo = [cTlo[:, q, c * 512 + u * P:c * 512 + (u + 1) * P] for c in range(2)]
                    for c in range(2):
                        for a, wq in ((hi, wq_hi), (hi, wq_lo), (lo, wq_hi)):
                            for f in range(2):
                                last = mm(ps[:, 3 + 2 * (u % 2) + f, 0:260], a[c], wq[:, c, f, w],
                                          start=c == 0 and a is hi and wq is wq_hi, stop=c == 1 and a is lo)
                    last.then_inc(k_done, 1)
                    if u == 2:
                        if last_group:
                            pe.wait_ge(s_read, G)
                        else:
                            pe.wait_ge(ct_ready, G + 2)
                        mm(ps[:, 2, P:P + 32], kpT[:, q, :], qpe[:, bass.ds(32 * b, 32)], start=True, stop=True)\
                            .then_inc(s_done, 1)

            def softmax_max(b):
                pe.wait_ge(pm_ready, b + 1)
                nc.tensor.transpose(ps[0:HM, 7, 0:P], pmx[:, :], ident).then_inc(pmT_done, 1)

            def softmax_spread(b):
                pe.wait_ge(dg_ready, b + 1)
                mm(ps[:, 7, P:P + HM], ones[0:HM, :], dgm[0:HM, 0:HM], start=True, stop=True).then_inc(mx_done, 1)

            def weighted_sum(b, p):
                pe.wait_ge(es_ready, b + 1)
                mm(ps[0:HM, 7, P + 8:P + 9], esm[:, :], ones[:, 0:1], start=True, stop=True)
                if not (isinstance(b, int) and b == 0):
                    pe.wait_ge(lat_done, b)
                for t in range(NPAGE):
                    mm(ps[0:HM, 7, 256:512], Ex[:, t, :], cn[p][:, t, 0:KVR], start=t == 0, stop=False)
                mm(ps[0:HM, 7, 256:512], Ex[0:NB, NPAGE, :], rows[0:NB, TS, 0:KVR], start=False, stop=True)\
                    .then_inc(pv_done, 1)

            def batch(b, p, turn, next_turn, first, last):
                if first:
                    group_in(b, 0, p, turn)
                for g in range(8):
                    if g < 7:
                        group_in(b, g + 1, p, turn)
                    elif not last:
                        group_in(b + 1, 0, 1 - p, next_turn)
                    group_products(b, g, p, last and g == 7)
                    if not first:
                        if g == 2:
                            softmax_max(b - 1)
                        elif g == 3:
                            softmax_spread(b - 1)
                        elif g == 4:
                            weighted_sum(b - 1, 1 - p)

            batch(0, 0, 0, 0, True, False)
            with pe.Fori(0, (NB - 2) // 2) as i:
                batch(2 * i + 1, 1, i, i + 1, False, False)
                batch(2 * i + 2, 0, i + 1, i + 1, False, False)
            batch(NB - 1, 1, (NB - 1) // 2, 0, False, True)
            softmax_max(NB - 1)
            softmax_spread(NB - 1)
            weighted_sum(NB - 1, 1)
            pe.wait_ge(lat_done, NB)
            for b in range(NB):
                for c in range(2):
                    o = (2 * b + c) * NB
                    last = nc.tensor.transpose(ps[:, 7, o:o + NB], lat_h[:, b * KVR + c * P:b * KVR + (c + 1) * P],
                                               ident[0:NB, 0:NB])
            last.then_inc(lt_done, 1)
            pe.wait_ge(late_in, 32)
            pe.wait_ge(lt_ready, 1)
            lat = latT[:, :].rearrange("p (b c h) -> p b c h", b=NB, c=2)
            for h in range(HM):
                for c in range(2):
                    last = mm(ps[0:NB, 0, h * 64:(h + 1) * 64], lat[:, :, c, h], wuvr[:, c, h * 64:(h + 1) * 64],
                              start=c == 0, stop=c == 1)
            last.then_inc(f_pe, 1)
            for b in range(NB):
                if b >= 2:
                    pe.wait_ge(qb_read, b - 1)
                for g in range(ND):
                    q0 = (1 + 2 * (b % 2)) * 512 + g * BW
                    last = mm(psw(0, 8 * 512)[:, q0:q0 + BW], ident[0:NB, b:b + 1].to_broadcast([NB, P]),
                              dq_s[:, g, :], start=True, stop=True)
                last.then_inc(qb_done, 1)
            pe.wait_ge(f_dve, F_MAX)
            nc.tensor.transpose(ps[0:32, 5, 0:P], dpm[:, :], ident).then_inc(f_pe, 1)
            pe.wait_ge(f_dve, F_DIAG)
            mm(ps[:, 5, 128:160], ones[0:32, :], dgm[:, :], start=True, stop=True).then_inc(f_pe, 1)
            pe.wait_ge(f_dve, F_SUM)
            mm(ps[:, 5, 160:192], ones[:, :], dsm[:, :], start=True, stop=True).then_inc(f_pe, 1)
            ED = ED_t[:, :].rearrange("p (b s h) -> p b s h", b=NB, h=HD)
            for b in range(NB):
                kv = [(sdk0 if b < 6 else sdk1)[:, (b if b < 6 else b - 6) * ND + g, :] for g in range(ND)]
                for p in range(2):
                    c = BW + p * P
                    for g in range(ND):
                        mm(ps[:, 6, 4 * b + 2 * p:4 * b + 2 * p + 2], kv[g][:, c:c + P], ED[:, b, g, 2 * p:2 * p + 2],
                           start=g == 0, stop=False)
                    for g in range(ND):
                        last = mm(ps[:, 6, 4 * b + 2 * p:4 * b + 2 * p + 2], kv_s[:, g, c:c + P],
                                  ED[0:NB, b, ND + g, 2 * p:2 * p + 2], start=False, stop=g == ND - 1)
            last.then_inc(f_pe, 1)
            pe.wait_ge(f_dve, F_OBT)
            for p in range(2):
                last = nc.tensor.transpose(ps[0:NB, 7, p * P:(p + 1) * P], obT[:, p * NB:(p + 1) * NB], ident)
            last.then_inc(f_pe, 1)
            pe.wait_ge(f_dve, F_OG)
            for c in range(6):
                last = nc.tensor.transpose(ps[:, 7, 256 + NB * c:256 + NB * (c + 1)], og[:, c * P:(c + 1) * P],
                                           ident[0:NB, 0:NB])
            last.then_inc(f_pe, 1)
            pe.wait_ge(zeroed, 6)
            pe.wait_ge(f_dve, F_OST)
            for n in range(2):
                block_of(f"PAs{n}", ITEM[f"PAs{n}"], [TS], small=osT)
                block_of(f"PBs{n}", ITEM[f"PBs{n}"], [TS], small=osT[:, 4:6, :])
            pe.wait_ge(f_dve, F_MS)
            for c in range(KD):
                last = nc.tensor.transpose(ps[:, 7, 320 + NB * c:320 + NB * (c + 1)], yab[:, 0, c * P:(c + 1) * P],
                                           ident[0:NB, 0:NB])
            last.then_inc(f_pe, 1)
            pe.wait_ge(f_dve, F_MST)
            for n in range(2):
                block_of(f"WOs{n}", ITEM[f"WOs{n}"], [TS], small=hTs)

        @block.vector
        def _(dve):
            v = nc.vector
            steps = [0]
            staged = [0]
            freed = [0]
            miscs = [0]
            fcount = [0]

            def link(ins):
                steps[0] += 1
                ins.then_inc(dve_step, 1)
                dve.wait_ge(dve_step, steps[0])

            def rsqrt_seed(x, a, y, step):
                step(v.tensor_scalar(out=a.bitcast(I32), in0=x.bitcast(I32), scalar1=1, scalar2=None,
                                     op0=ALU.logical_shift_right))
                step(v.tensor_scalar(out=y.bitcast(I32), in0=a.bitcast(I32), scalar1=-1.0, scalar2=RSQRT_MAGIC,
                                     op0=ALU.mult, op1=ALU.add))

            def rsqrt_newton(x, a, y, step):
                step(v.tensor_tensor(out=a, in0=y, in1=y, op=ALU.mult))
                step(v.scalar_tensor_tensor(out=a, in0=a, scalar=-0.5, in1=x, op0=ALU.mult, op1=ALU.mult))
                step(v.scalar_tensor_tensor(out=y, in0=a, scalar=1.5, in1=y, op0=ALU.add, op1=ALU.mult))

            def rsqrt(x, a, y, step):
                rsqrt_seed(x, a, y, step)
                for _ in range(3):
                    rsqrt_newton(x, a, y, step)

            def inv_rms(cols_, *scales):
                w = cols_ // len(scales)
                for m, scale in enumerate(scales):
                    last = v.tensor_scalar(out=rsx[:, m * w:(m + 1) * w], in0=ms[:, m * w:(m + 1) * w], scalar1=scale,
                                           scalar2=EPS, op0=ALU.mult, op1=ALU.add)
                link(last)
                rsqrt(rsx[:, 0:cols_], rsa[:, 0:cols_], rsy[:, 0:cols_], link)

            def take(idx, n, w, small):
                wait_evac(dve, idx)
                z = stage[0:n, staged[0] % NSTAGE, 0:w]
                staged[0] += 1
                if small:
                    link(v.tensor_tensor(out=z, in0=z, in1=low_s[0:n, 0:w], op=ALU.add))
                return z

            def free_stage(ins):
                ins.then_inc(stage_free, 1)
                freed[0] += 1
                dve.wait_ge(stage_free, freed[0])

            def mean_square(z, w, col):
                n = z.shape[0]
                link(v.tensor_tensor_reduce(out=sqt[0:n, 0:w], in0=z, in1=z, scale=1.0 / w, scalar=0.0,
                                            op0=ALU.mult, op1=ALU.add, accum_out=ms[0:n, col:col + 1]))

            def rotate(x, out, sin_cos, heads):
                n = x.shape[0]
                a = pe1[0:n, 0:heads * ROPE].rearrange("p (h e) -> p h e", e=ROPE)
                b = pe2[0:n, 0:heads * ROPE].rearrange("p (h e) -> p h e", e=ROPE)
                v.tensor_tensor(out=a, in0=x, in1=rep(sin_cos[:, 0:32], 1, heads), op=ALU.mult)
                v.tensor_tensor(out=b[:, :, 0:16], in0=x[:, :, 16:32], in1=rep(sin_cos[:, 32:48], 1, heads), op=ALU.mult)
                link(v.tensor_tensor(out=b[:, :, 16:32], in0=x[:, :, 0:16], in1=rep(sin_cos[:, 48:64], 1, heads),
                                     op=ALU.mult))
                return v.tensor_tensor(out=out, in0=a, in1=b, op=ALU.add)

            def misc_wait():
                miscs[0] += 1
                dve.wait_ge(misc_done, miscs[0])

            def misc_read(ins):
                ins.then_inc(misc_free, 1)
                dve.wait_ge(misc_free, miscs[0])

            def split_small(src, dst, count, n=NB):
                link(v.tensor_copy(dst[:, 0:count, 0:n], src))
                return v.tensor_tensor(out=dst[:, 0:count, LO:LO + n], in0=src,
                                       in1=dst[:, 0:count, 0:n].bitcast(F32), op=ALU.subtract)

            def low_half(idx, out, hi, scale=None):
                dve.wait_ge(act_half, READER[idx][1])
                src = ps[:, idx % BANKS, :]
                if scale is None:
                    ins = v.tensor_tensor(out=out, in0=src, in1=hi.bitcast(F32), op=ALU.subtract)
                else:
                    ins = v.scalar_tensor_tensor(out=out, in0=src, scalar=scale, in1=hi.bitcast(F32), op0=ALU.mult,
                                                 op1=ALU.subtract)
                ins.then_inc(evac_d, 1)

            dve.wait_ge(sigm_c, 1)
            v.tensor_tensor(out=c9b[:, :], in0=c9[:, :], in1=c9b[:, :], op=ALU.mult).then_inc(csilu, 1)
            dve.wait_ge(zeroed, 3)
            misc_wait()
            csf = ps[:, 7, 0:72].rearrange("p (k n) -> p k n", n=9)
            link(v.tensor_copy(cs[:, :, 0:9], csf))
            misc_read(v.tensor_tensor(out=cs[:, :, LO:LO + 9], in0=csf, in1=cs[:, :, 0:9].bitcast(F32), op=ALU.subtract))
            v.memset(flag[:, :], 0.0).then_inc(cs_ready, 1)
            dve.wait_ge(wuk_h, 1)
            v.tensor_tensor(out=wuk_lo, in0=wukr[:, :, :].rearrange("p c (f n) -> p c f n", f=2),
                            in1=wuk_hi.bitcast(F32), op=ALU.subtract)\
             .then_inc(wuk_split, 1)

            def ada_item(n):
                z = take(ITEM[f"ada{n}"], NB + 1, 512, True)
                if n == 0:
                    dve.wait_ge(bada_in, 16)
                free_stage(v.tensor_tensor(out=ada[:, n * 512:(n + 1) * 512], in0=z,
                                           in1=bada[:, n * 512:(n + 1) * 512], op=ALU.add))
                if n >= 4:
                    v.tensor_copy(gate_s[:, (n - 4) * 512:(n - 3) * 512], ada[0:NB, n * 512:(n + 1) * 512])\
                     .then_inc(ada_ready, 1)
                else:
                    v.memset(flag[:, :], 0.0).then_inc(ada_ready, 1)

            link(v.memset(ms[:, :], 1.0))
            for t in range(5):
                n = lanes(t)
                x = xs1[:, :] if t == TS else xt[:, t, :]
                dve.wait_ge(x_in[t], 16)
                link(v.tensor_tensor_reduce(out=xsq[0:n, :], in0=x, in1=x, scale=1.0 / D, scalar=0.0,
                                            op0=ALU.mult, op1=ALU.add, accum_out=ms[0:n, t:t + 1]))
            inv_rms(5, 1.0)
            for t in range(5):
                n = lanes(t)
                x = xs1[:, :] if t == TS else xt[:, t, :]
                v.tensor_scalar(out=x, in0=x, scalar1=rsy[0:n, t:t + 1], scalar2=None, op0=ALU.mult)\
                 .then_inc(xn_ready, 1)
            for n in range(2):
                ada_item(n)
            misc_wait()
            misc_read(v.tensor_copy(xTs[:, :], ps[:, 7, 0:64]))
            for n in range(2, 6):
                ada_item(n)
            misc_wait()
            adaT = ps[:, 7, 0:144].rearrange("p (k n) -> p k n", n=9)
            dve.wait_ge(consts_in, 80)
            v.scalar_tensor_tensor(out=G1[:, :, :], in0=adaT[:, KD:2 * KD, :], scalar=1.0,
                                   in1=rep(colt[:, 0:KD], 2, 9), op0=ALU.add, op1=ALU.mult)
            misc_read(v.tensor_copy(SH[:, :, :], adaT[:, 0:KD, :]))
            xTs3 = xTs[:, :].rearrange("p (k n) -> p k n", n=NB)
            link(v.tensor_tensor(out=hs_f[:, :, :], in0=xTs3, in1=G1[:, :, 0:NB], op=ALU.mult))
            link(v.tensor_tensor(out=hs_f[:, :, :], in0=hs_f[:, :, :], in1=SH[:, :, 0:NB], op=ALU.add))
            split_small(hs_f[:, :, :], hTs, KD).then_inc(h_ready, 1)

            def low_h(k):
                dve.wait_ge(h_hi, k + 1)
                v.tensor_tensor(out=hTlo[:, k, :], in0=xT[:, k, :], in1=hThi[:, k, :].bitcast(F32), op=ALU.subtract)\
                 .then_inc(h_ready, 1)

            for k in range(KD):
                wait_evac(dve, ITEM["xT"] + k)
                v.tensor_scalar(out=xT[:, k, :], in0=xT[:, k, :], scalar1=G1[:, k, NB:NB + 1],
                                scalar2=SH[:, k, NB:NB + 1], op0=ALU.mult, op1=ALU.add).then_inc(h_f, 1)
                if k:
                    low_h(k - 1)
            low_h(KD - 1)
            v.tensor_tensor(out=g96[:, 0:NOPE], in0=gn[:, G_QN:G_QN + 64], in1=gn[:, G_KN:G_KN + 64], op=ALU.mult)
            link(v.tensor_copy(g96[:, NOPE:QK], gn[:, G_QR:G_QR + 32]))
            zs = []
            for t in range(5):
                zs.append(take(ITEM["Q"] + t, lanes(t), QR, t == TS))
                mean_square(zs[t], QR, t)
            inv_rms(5, 1.0)
            for t in range(5):
                n = lanes(t)
                free_stage(v.tensor_scalar(out=qan[0:n, t, :], in0=zs[t], scalar1=rsy[0:n, t:t + 1], scalar2=None,
                                           op0=ALU.mult))
            v.memset(flag[:, :], 0.0).then_inc(qan_ready, 1)
            for c in range(3):
                low_half(ITEM["Tq"] + c, qaTlo[:, c, :], qaThi[:, c, :], colt[:, KD + c:KD + c + 1])
            dve.wait_ge(zeroed, 5)
            misc_wait()
            qaf = pe1[:, 0:24].rearrange("p (k n) -> p k n", n=NB)
            misc_read(v.tensor_tensor(out=qaf, in0=ps[:, 7, 0:24].rearrange("p (k n) -> p k n", n=NB),
                                      in1=rep(colt[:, KD:KD + 3], 2, NB), op=ALU.mult))
            split_small(qaf, qaTs, 3).then_inc(smp_ready, 1)
            zs = []
            for t in range(5):
                zs.append(take(ITEM["KV"] + t, lanes(t), CW, t == TS))
                mean_square(zs[t][:, 0:KVR], KVR, t)
                mean_square(zs[t][:, KVR:CW], ROPE, 5 + t)
            inv_rms(10, 1.0)
            for t in range(5):
                n, z = lanes(t), zs[t]
                v.scalar_tensor_tensor(out=rows[0:n, t, 0:KVR], in0=z[:, 0:KVR], scalar=rsy[0:n, t:t + 1],
                                       in1=gn[0:n, G_KV:G_KV + KVR], op0=ALU.mult, op1=ALU.mult)
                free_stage(v.scalar_tensor_tensor(out=rows[0:n, t, KVR:CW], in0=z[:, KVR:CW],
                                                  scalar=rsy[0:n, 5 + t:6 + t], in1=gn[0:n, G_KR:G_KR + ROPE],
                                                  op0=ALU.mult, op1=ALU.mult))
                kp = rows[0:n, t, KVR:CW].unsqueeze(1)
                rotate(kp, kp, ropes[0:n, t, 128:192], 1).then_inc(rows_ready, 1)
                dve.wait_ge(rows_ready, t + 1)

            def q_squares(i, t):
                n = lanes(t)
                z = take(ITEM[f"QB{i}"] + t, n, 384, t == TS)
                z3 = z.rearrange("p (h e) -> p h e", e=QK)
                sq3 = sqt[0:n, 0:384].rearrange("p (h e) -> p h e", e=QK)
                link(v.tensor_tensor(out=sq3, in0=z3, in1=z3, op=ALU.mult))
                v.tensor_reduce(out=ms[0:n, 4 * t:4 * t + 4], in_=sq3[:, :, 0:NOPE], axis=AX, op=ALU.add)
                link(v.tensor_reduce(out=ms[0:n, 20 + 4 * t:24 + 4 * t], in_=sq3[:, :, NOPE:QK], axis=AX, op=ALU.add))
                return z3

            def q_item(i, t, z3):
                n = lanes(t)
                out = q_s[:, i * 384:(i + 1) * 384] if t == TS else qh[:, i * NT + t, :]
                o3 = out.rearrange("p (h e) -> p h e", e=QK)
                v.tensor_tensor(out=o3[:, :, 0:NOPE], in0=z3[:, :, 0:NOPE], in1=rep(rsy[0:n, 4 * t:4 * t + 4], 2, NOPE),
                                op=ALU.mult)
                free_stage(v.tensor_tensor(out=o3[:, :, NOPE:QK], in0=z3[:, :, NOPE:QK],
                                           in1=rep(rsy[0:n, 20 + 4 * t:24 + 4 * t], 2, ROPE), op=ALU.mult))
                link(v.tensor_tensor(out=o3, in0=o3, in1=rep(g96[0:n, :], 1, 4), op=ALU.mult))
                if t == TS:
                    v.tensor_copy(qn_s[:, i * 256:(i + 1) * 256].rearrange("p (h e) -> p h e", e=NOPE), o3[:, :, 0:NOPE])
                rotate(o3[:, :, NOPE:QK], o3[:, :, NOPE:QK], ropes[0:n, t, 128:192], 4).then_inc(qh_ready, 1)
                dve.wait_ge(qh_ready, 5 * i + t + 1)

            def q_block(i):
                zs = [q_squares(i, t) for t in range(5)]
                inv_rms(40, 1.0 / NOPE, 1.0 / ROPE)
                for t in range(5):
                    q_item(i, t, zs[t])

            q_block(0)
            for c in range(2):
                low_half(ITEM["Tr"] + c, rTlo[:, c, :], rThi[:, c, :])
            misc_wait()
            rf = pe1[:, 0:16].rearrange("p (k n) -> p k n", n=NB)
            misc_read(v.tensor_copy(rf, ps[:, 7, 0:16].rearrange("p (k n) -> p k n", n=NB)))
            split_small(rf, rTs, 2).then_inc(smp_ready, 1)
            q_block(1)

            def head_squares(name, t):
                n = lanes(t)
                z = take(ITEM[name] + t, n, 512, t == TS)
                link(v.tensor_tensor(out=sqt[0:n, :], in0=z, in1=z, op=ALU.mult))
                link(v.tensor_reduce(out=ms[0:n, 8 * t:8 * t + 8], in_=sqt[0:n, :].rearrange("p (h e) -> p h e", e=64),
                                     axis=AX, op=ALU.add))
                return z.rearrange("p (h e) -> p h e", e=64)

            zs = [head_squares("K", t) for t in range(5)]
            inv_rms(40, 1.0 / NOPE)
            for t in range(5):
                n, z3 = lanes(t), zs[t]
                out = (k_s[:, :] if t == TS else kc[:, t, :]).rearrange("p (h e) -> p h e", e=QK)
                free_stage(v.tensor_tensor(out=out[:, :, 0:NOPE], in0=z3, in1=rep(rsy[0:n, 8 * t:8 * t + 8], 2, NOPE),
                                           op=ALU.mult))
                v.tensor_copy(out[:, :, NOPE:QK], rep(rows[0:n, t, KVR:CW], 1, HM)).then_inc(kc_ready, 1)
            misc_wait()
            v.tensor_copy(qsT[:, :], ps[:, 7, 0:32])
            link(v.memset(qpe[:, :], 0.0))
            for u in range(4):
                last = v.tensor_copy(qpe[32 * u:32 * u + 32, :].rearrange("p (b u h) -> p u h b", b=NB, u=4)[:, u],
                                     ps[0:ROPE, 7, 32:96].rearrange("p (h b) -> p h b", b=NB))
            misc_read(last)
            misc_wait()
            misc_read(v.tensor_copy(qabs[:, 0:NB * 16].rearrange("p (b c h) -> p c h b", c=2, b=NB),
                                    ps[:, 7, 0:128].rearrange("p (c h b) -> p c h b", c=2, b=NB)))
            link(v.memset(qabs[:, NB * 16:(NB + 1) * 16], 0.0))

            def set_q(b, p, step):
                q3 = qabs[:, bass.ds(16 * b, 16)].rearrange("p (c f h) -> p c f h", c=2, f=2)
                cols_ = slice(260 * p, 260 * p + 4)
                step(v.tensor_copy(wq_hi[:, :, :, cols_], q3))
                return v.tensor_tensor(out=wq_lo[:, :, :, cols_], in0=q3, in1=wq_hi[:, :, :, cols_].bitcast(F32),
                                       op=ALU.subtract)

            for b in range(2):
                link(set_q(b, b, link))
            dve.wait_ge(kc_ready, 5)
            own = tmp_t[0:NB, 1792:2560]
            link(v.tensor_tensor(out=own, in0=q_s[:, :], in1=k_s[:, :], op=ALU.mult))
            link(v.tensor_reduce(out=dns[:, :], in_=own.rearrange("p (h e) -> p h e", e=QK), axis=AX, op=ALU.add))
            link(v.tensor_tensor(out=snew[:, :].rearrange("p (b h) -> p b h", b=NB), in0=rep(dns[:, :], 1, NB),
                                 in1=rep(newmask, 2, HM), op=ALU.add))

            def attention(jobs, n0, c0, slots, ahead, mask, place, scale):
                def masks_max(n):
                    s = n % slots
                    dve.wait_ge(qk_done, n + 1)
                    if n - n0 >= slots:
                        dve.wait_ge(trp_done, CHUNK_END[n - slots])
                    a = amax[:, 4 * s:4 * s + 4]
                    parts = mask(jobs[n - n0], n, Pm[slots][:, s, :])
                    for m, (out, src, msk) in enumerate(parts):
                        link(v.tensor_tensor_reduce(out=out, in0=src, in1=msk, scale=1.0,
                                                    scalar=NEG if m == 0 else a[:, 0:1], op0=ALU.add, op1=ALU.max,
                                                    accum_out=a[:, m:m + 1]))
                    m = len(parts) - 1
                    v.tensor_scalar(out=a[:, 2:3], in0=a[:, m:m + 1], scalar1=-scale, scalar2=None, op0=ALU.mult)\
                     .then_inc(masked, 1)

                chunk = c0
                for n in range(n0, n0 + ahead):
                    masks_max(n)
                for n in range(n0, n0 + len(jobs)):
                    s = n % slots
                    if n + ahead < n0 + len(jobs):
                        masks_max(n + ahead)
                    for w in widths(jobs[n - n0][2]):
                        if chunk % 2 == 0:
                            pt_copy(dve, v.tensor_copy, chunk, w, pt_d, ())
                        chunk += 1
                    dve.wait_ge(exp_done, n + 1)
                    link(v.reciprocal(lsum[:, 4 + s:5 + s], lsum[:, s:s + 1]))
                    dve.wait_ge(pv_chunk, chunk)
                    out, src = place(jobs[n - n0], n)
                    v.tensor_scalar(out=out, in0=src, scalar1=lsum[:, 4 + s:5 + s], scalar2=None, op0=ALU.mult)\
                     .then_inc(o_done, 1)

            def mla_mask(job, n, p):
                w = job[2] * P
                return [(p[:, 0:w], ps[:, n % 4, 0:w], masks[:, M_R4 - w:M_R4])]

            def mla_place(job, n):
                i, h, nb = job
                return oN[:, i, h * 64:(h + 1) * 64], ps[:, 4 + n % 2, 0:64]

            dve.wait_ge(z_done, LAST_ITEM["TkM"] + 1)
            attention(MLA_JOBS, 0, 0, 4, 2, mla_mask, mla_place, MLA_SCALE)
            for g in range(ND):
                zs = [head_squares(f"D{g}QK", t) for t in range(5)]
                inv_rms(40, 1.0 / DH)
                for t in range(5):
                    c = 5 * g + t
                    n, z3 = lanes(t), zs[t]
                    y = tmp[0:n, c % 2, :]
                    if c >= 2:
                        dve.wait_ge(rope_done, c - 1)
                    free_stage(v.tensor_tensor(out=y.rearrange("p (h e) -> p h e", e=DH), in0=z3,
                                               in1=rep(rsy[0:n, 8 * t:8 * t + 8], 2, DH), op=ALU.mult))
                    for m, o in enumerate((G_DQ, G_DK)):
                        yh = y[:, m * BW:(m + 1) * BW].rearrange("p (h e) -> p h e", e=DH)
                        last = v.tensor_tensor(out=yh, in0=yh, in1=rep(gn[0:n, o + g * DH:o + (g + 1) * DH], 1, HD),
                                               op=ALU.mult)
                    last.then_inc(y_roped, 1)
                    dve.wait_ge(y_roped, 2 * c + 1)
                    if c >= 1:
                        dve.wait_ge(rope_done, c)
                    v.tensor_tensor(out=tmp[0:n, 2, :].rearrange("p (h e) -> p h e", e=DH),
                                    in0=y.rearrange("p (h e) -> p h e", e=DH),
                                    in1=rep(ropes[0:n, t, 0:64], 1, 2 * HD), op=ALU.mult).then_inc(y_roped, 1)
                wait_evac(dve, ITEM[f"D{g}V"] + TS)
                z = stage[0:NB, staged[0] % NSTAGE, 0:BW]
                staged[0] += 1
                free_stage(v.tensor_tensor(out=kv_s[:, g, BW:2 * BW], in0=z, in1=low_s[0:NB, 0:BW], op=ALU.add))
            dve.wait_ge(rope_done, 5 * ND)
            v.memset(flag[:, :], 0.0).then_inc(smp_ready, 1)

            def dil_mask(job, n, p):
                i = job[0]
                w0 = P if i == 0 else 2 * P
                w = (i + 1) * P
                both = masks[:, M_R4:M_R4 + 1024].rearrange("p (g c) -> p g c", g=2)[:, :, 512 - w:512]
                s = n % 2
                return [(p[:, 0:w0], ps[:, 4, 256 * s:256 * s + w0], masks[:, M_ALL - w0:M_ALL]),
                        (p[:, w0:w0 + 2 * w].rearrange("p (g c) -> p g c", g=2), ps[:, 2 * s:2 * s + 2, 0:w], both)]

            def dil_place(job, n):
                i, h, nb = job
                return oN[:, i, AW + h * 64:AW + (h + 1) * 64], ps[:, 5, 0:64]

            dve.wait_ge(z_done, LAST_ITEM["TD"] + 1)
            attention(DIL_JOBS, len(MLA_JOBS), N_MLA_CHUNKS, 2, 1, dil_mask, dil_place, DIL_SCALE)
            for name, c0, w in (("GA", 0, AW), ("GB", AW, BW)):
                for t in range(NT):
                    idx = ITEM[name] + t
                    dve.wait_ge(act_half, READER[idx][1])
                    sg = stage[:, staged[0] % NSTAGE, 0:w]
                    staged[0] += 1
                    v.tensor_tensor(out=sg, in0=sg, in1=ps[:, idx % BANKS, 0:w], op=ALU.mult).then_inc(evac_d, 1)
                    dve.wait_ge(evac_d, READER[idx][1])
                    free_stage(v.tensor_tensor(out=oN[:, t, c0:c0 + w], in0=oN[:, t, c0:c0 + w], in1=sg, op=ALU.mult))
                    v.memset(flag[:, :], 0.0).then_inc(gated, 1)
                wait_evac(dve, ITEM[name + "s"])
                z = stage[0:NB, staged[0] % NSTAGE, 0:w]
                staged[0] += 1
                free_stage(v.tensor_tensor(out=mix_s[:, c0:c0 + w], in0=z, in1=low_s[0:NB, 0:w], op=ALU.add))
            dve.wait_ge(win_out, 16 * 3)
            for c in range(6):
                low_half(ITEM["To"] + c, oTlo[:, c, :], oThi[:, c, :])
            for n in range(2):
                for b, y in (("A", ya), ("B", yb)):
                    for t in range(NT):
                        z = take(ITEM[f"M{b}{n}"] + t, P, 512, False)
                        yt = y[:, t, n * 512:(n + 1) * 512]
                        free_stage(v.tensor_tensor(out=yt, in0=yt, in1=z, op=ALU.mult))
                        if b == "B":
                            yt2 = ya[:, t, n * 512:(n + 1) * 512]
                            v.tensor_tensor(out=yt2, in0=yt2, in1=yt, op=ALU.add).then_inc(merged, 1)
                    idx = ITEM[f"M{b}{n}"] + TS
                    wait_evac(dve, idx)
                    z = stage[0:NB, staged[0] % NSTAGE, 0:512]
                    staged[0] += 1
                    c0 = (0 if b == "A" else D) + n * 512
                    free_stage(v.tensor_tensor(out=merge_s[:, c0:c0 + 512], in0=z, in1=low_s[0:NB, :], op=ALU.add))
            for k in range(KD):
                low_half(ITEM["Tm"] + k, hTlo[:, k, :], hThi[:, k, :])
            for n in range(2):
                dve.wait_ge(xr_in[n], 16)
                for t in range(NT):
                    z = take(ITEM[f"WO{n}"] + t, P, 512, False)
                    link(v.tensor_tensor(out=z, in0=z, in1=gate_bc[:, n * 512:(n + 1) * 512], op=ALU.mult))
                    free_stage(v.tensor_tensor(out=xr[n][:, t, :], in0=xr[n][:, t, :], in1=z, op=ALU.add))
                    v.memset(flag[:, :], 0.0).then_inc(y_rdy, 1)
            dve.wait_ge(z_done, LAST_ITEM["WO1"] + 1)
            dve.wait_ge(y_out[0], 16)
            v.memset(Sc[:, NPAGE, :], NEG)
            base = [0]
            within = [0]

            def lstep_link(ins):
                within[0] += 1
                ins.then_inc(lstep, 1)
                dve.wait_ge(lstep, base[0] + within[0])

            def lat_rows(G, q):
                dve.wait_ge(ct_hi, G + 1)
                v.tensor_tensor(out=cTlo[:, q % 2, :], in0=psw(0, 1024), in1=cThi[:, q % 2, :].bitcast(F32),
                                op=ALU.subtract)
                v.tensor_copy(kpT[:, q % 2, :], ps[:, 2, 0:P]).then_inc(ct_ready, 1)

            def half_scores(h, part):
                t0 = 16 * h
                if part == 0:
                    lstep_link(v.tensor_scalar(out=lx[:, :], in0=ssq[:, t0 * 8:t0 * 8 + 128], scalar1=1.0 / NOPE,
                                               scalar2=EPS, op0=ALU.mult, op1=ALU.add))
                    rsqrt_seed(lx[:, :], lax[:, :], ly[:, :], lstep_link)
                else:
                    rsqrt_newton(lx[:, :], lax[:, :], ly[:, :], lstep_link)
                if part < 3:
                    return
                s3 = Sc[:, t0:t0 + 16, :]
                lstep_link(v.tensor_tensor(out=s3, in0=Sq[:, t0:t0 + 16, :],
                                           in1=ly[:, :].rearrange("p (t h) -> p t h", h=8), op=ALU.mult))
                lstep_link(v.tensor_tensor(out=s3, in0=s3, in1=Sk[:, t0:t0 + 16, :], op=ALU.add))

            def softmax_diag(b):
                dve.wait_ge(pmT_done, b + 1)
                lstep_link(v.tensor_reduce(out=mx1[0:HM, :], in_=ps[0:HM, 7, 0:P], axis=AX, op=ALU.max))
                v.tensor_scalar(out=dgm[0:HM, 0:HM], in0=ident[0:HM, 0:HM], scalar1=mx1[0:HM, :], scalar2=None,
                                op0=ALU.mult).then_inc(dg_ready, 1)

            def softmax_shift(b):
                dve.wait_ge(mx_done, b + 1)
                v.tensor_tensor(out=Sc[:, :, :], in0=Sc[:, :, :], in1=rep(ps[:, 7, P:P + HM], 1, 33), op=ALU.subtract)\
                 .then_inc(sub_done, 1)

            def softmax_sum(b):
                dve.wait_ge(ex_done, b + 1)
                v.tensor_reduce(out=esm[:, :], in_=Ex[:, :, :].rearrange("p t h -> p h t"), axis=AX, op=ALU.add)\
                 .then_inc(es_ready, 1)

            def latent(b):
                dve.wait_ge(pv_done, b + 1)
                lstep_link(v.reciprocal(rdn[0:HM, 0:1], ps[0:HM, 7, P + 8:P + 9]))
                v.tensor_scalar(out=lat_h[:, bass.ds(KVR * b, KVR)], in0=ps[0:HM, 7, 256:512], scalar1=rdn[0:HM, 0:1],
                                scalar2=None, op0=ALU.mult).then_inc(lat_done, 1)

            def maxima(b):
                lstep_link(v.tensor_copy(Sc[0:NB, NPAGE, :], snew[:, bass.ds(8 * b, 8)]))
                v.tensor_reduce(out=pmx[:, :], in_=Sc[:, :, :].rearrange("p t h -> p h t"), axis=AX, op=ALU.max)\
                 .then_inc(pm_ready, 1)

            def batch(b, p, first, last):
                within[0] = 0
                base[0] = b * LSTEPS if first is False else 0
                for g in range(8):
                    if g == 0 and first:
                        lat_rows(8 * b, 0)
                    if not (last and g == 7):
                        lat_rows(8 * b + g + 1, g + 1)
                    if g == 0 and not first or g == 4:
                        dve.wait_ge(red_done, NPAGE * b + 4 * g)
                    for u in range(4):
                        if u % 2 == 0 and g < 2 and not first:
                            half_scores(1, 2 * g + u // 2)
                        if u % 2 == 0 and g in (4, 5):
                            half_scores(0, 2 * (g - 4) + u // 2)
                        if g == 4 and u == 2 and not first:
                            softmax_sum(b - 1)
                        if u == 3:
                            dve.wait_ge(s_done, 8 * b + g + 1)
                            v.tensor_copy(Sk[:, 4 * g:4 * g + 4, :],
                                          ps[:, 2, P:P + 32].rearrange("p (u n) -> p u n", u=4)).then_inc(s_read, 1)
                        dve.wait_ge(sq_done, NPAGE * b + 4 * g + u + 1)
                        v.tensor_reduce(out=ssq[:, (4 * g + u) * 8:(4 * g + u + 1) * 8],
                                        in_=sq4[:, u, :].rearrange("p (h e) -> p h e", e=NOPE), axis=AX, op=ALU.add)\
                         .then_inc(red_done, 1)
                    if not first:
                        if g == 1:
                            maxima(b - 1)
                        elif g == 2:
                            softmax_diag(b - 1)
                        elif g == 3:
                            softmax_shift(b - 1)
                        elif g == 5:
                            latent(b - 1)
                if not last:
                    set_q(b + 2, p, lstep_link)
                return within[0]

            n0 = batch(0, 0, True, False)
            for _ in range(LSTEPS - n0):
                lstep_link(v.memset(flag[:, :], 0.0))
            with dve.Fori(0, (NB - 2) // 2) as i:
                assert batch(2 * i + 1, 1, False, False) == LSTEPS
                assert batch(2 * i + 2, 0, False, False) == LSTEPS
            batch(NB - 1, 1, False, True)
            dve.wait_ge(red_done, NPAGE * NB)
            for part in range(4):
                half_scores(1, part)
            maxima(NB - 1)
            softmax_diag(NB - 1)
            softmax_shift(NB - 1)
            softmax_sum(NB - 1)
            latent(NB - 1)
            dve.wait_ge(lt_done, 1)
            v.tensor_copy(latT[:, :], ps[:, 7, 0:NB * 16]).then_inc(lt_ready, 1)
            def signal(ins, want):
                fcount[0] += 1
                assert fcount[0] == want, (fcount[0], want)
                ins.then_inc(f_dve, 1)
                dve.wait_ge(f_dve, want)

            dve.wait_ge(pv_done, NB)
            v.memset(SD_t[:, :], NEG)
            for b in range(NB):
                if b == 0:
                    dve.wait_ge(sdk_in[0], 48)
                if b == 6:
                    dve.wait_ge(sdk_in[1], 48)
                kv = (sdk0 if b < 6 else sdk1)[:, (b if b < 6 else b - 6) * ND:(b if b < 6 else b - 6) * ND + ND, 0:BW]
                dve.wait_ge(qb_done, b + 1)
                q0 = (1 + 2 * (b % 2)) * 512
                pr = prod[:, b % 2, :]
                v.tensor_tensor(out=pr.rearrange("p (g c) -> p g c", g=ND), in0=kv,
                                in1=psw(0, 4096)[:, q0:q0 + 768].rearrange("p (g c) -> p g c", g=ND), op=ALU.mult)\
                 .then_inc(qb_read, 1)
                dve.wait_ge(qb_read, b + 1)
                link(v.tensor_reduce(out=SD[:, b, 0:12], in_=pr.rearrange("p (n e) -> p n e", e=DH), axis=AX, op=ALU.add))
            pr = prod[0:NB, 0, :]
            link(v.tensor_tensor(out=pr.rearrange("p (g c) -> p g c", g=ND), in0=dq_s[:, :, :], in1=kv_s[:, :, 0:BW],
                                 op=ALU.mult))
            link(v.tensor_reduce(out=dn[:, 0:12], in_=pr.rearrange("p (n e) -> p n e", e=DH), axis=AX, op=ALU.add))
            link(v.tensor_tensor(out=SD[0:NB, :, 12:24], in0=rep(dn[:, 0:12], 1, NB), in1=rep(newmask, 2, 12), op=ALU.add))
            sd4 = SD_t[:, :].rearrange("p (b s h) -> p b h s", b=NB, h=HD)
            signal(v.tensor_reduce(out=dpm[:, :].rearrange("p (b h) -> p b h", b=NB), in_=sd4, axis=AX, op=ALU.max), F_MAX)
            dve.wait_ge(f_pe, 2)
            link(v.tensor_reduce(out=mx1[:, :], in_=ps[0:32, 5, 0:P], axis=AX, op=ALU.max))
            signal(v.tensor_scalar(out=dgm[:, :], in0=ident[0:32, 0:32], scalar1=mx1[:, :], scalar2=None, op0=ALU.mult),
                   F_DIAG)
            dve.wait_ge(f_pe, 3)
            signal(v.tensor_tensor(out=sd4, in0=sd4,
                                   in1=rep(ps[:, 5, 128:160].rearrange("p (b h) -> p b h", b=NB), 3, 6),
                                   op=ALU.subtract), F_SUB)
            dve.wait_ge(f_act, 1)
            ed4 = ED_t[:, :].rearrange("p (b s h) -> p b h s", b=NB, h=HD)
            signal(v.tensor_reduce(out=dsm[:, :].rearrange("p (b h) -> p b h", b=NB), in_=ed4, axis=AX, op=ALU.add), F_SUM)
            dve.wait_ge(f_pe, 4)
            link(v.reciprocal(rl[:, :], ps[:, 5, 160:192]))
            dve.wait_ge(f_pe, 5)
            for r in range(2):
                q = slice(64 * r, 64 * r + 64)
                last = v.tensor_tensor(out=obT[q, :].rearrange("p (a b) -> p b a", a=2),
                                       in0=ps[q, 6, 0:32].rearrange("p (b a r) -> p b a r", b=NB, a=2)[:, :, :, r],
                                       in1=rl[q, :].rearrange("p (b a r) -> p b a r", b=NB, a=2)[:, :, :, r], op=ALU.mult)
            signal(last, F_OBT)
            dve.wait_ge(f_act, 2)
            link(v.tensor_tensor(out=sgm[:, :], in0=sgm[:, :], in1=mix_s[:, :], op=ALU.mult))
            v.tensor_tensor(out=og[:, 0:AW], in0=sgm[:, 0:AW], in1=ps[0:NB, 0, 0:AW], op=ALU.mult)
            dve.wait_ge(f_pe, 6)
            signal(v.tensor_tensor(out=og[:, AW:768], in0=sgm[:, AW:768], in1=ps[0:NB, 7, 0:BW], op=ALU.mult), F_OG)
            dve.wait_ge(f_pe, 7)
            dve.wait_ge(zeroed, 6)
            osf = prod[:, 1, 0:48].rearrange("p (k n) -> p k n", n=NB)
            link(v.tensor_copy(osf, ps[:, 7, 256:304].rearrange("p (k n) -> p k n", n=NB)))
            signal(split_small(osf, osT, 6), F_OST)
            dve.wait_ge(f_act, 3)
            for n in range(2):
                for m, b in enumerate("AB"):
                    z = take(ITEM[f"P{b}s{n}"], NB, 512, True)
                    out = yab[:, m, n * 512:(n + 1) * 512]
                    free_stage(v.tensor_tensor(out=out, in0=z, in1=mgm[:, m * D + n * 512:m * D + (n + 1) * 512],
                                               op=ALU.mult))
            signal(v.tensor_tensor(out=yab[:, 0, :], in0=yab[:, 0, :], in1=yab[:, 1, :], op=ALU.add), F_MS)
            dve.wait_ge(f_pe, 8)
            msf = prod[:, 0, 0:64].rearrange("p (k n) -> p k n", n=NB)
            link(v.tensor_copy(msf, ps[:, 7, 320:384].rearrange("p (k n) -> p k n", n=NB)))
            signal(split_small(msf, hTs, KD), F_MST)
            dve.wait_ge(late_in, 32)
            for n in range(2):
                z = take(ITEM[f"WOs{n}"], NB, 512, True)
                c = slice(n * 512, (n + 1) * 512)
                link(v.tensor_tensor(out=z, in0=z, in1=gate_s[:, c], op=ALU.mult))
                free_stage(v.tensor_tensor(out=xs2[:, c], in0=xs2[:, c], in1=z, op=ALU.add))
            signal(v.memset(flag[:, :], 0.0), F_Y)


def _tables():
    q, k = np.arange(P)[:, None], np.arange(P)[None, :]
    none = np.zeros((P, P), bool)
    parts = [none] * 3 + [k > q]
    for d in (4, 16):
        r = (q - k) % d != 0
        parts += [r] * 3 + [r | (k > q)]
    parts += [k < q, k > q]
    masks = np.where(np.concatenate(parts, 1), np.float32(NEG), np.float32(0))
    own = np.zeros((P, 8), np.float32)
    own[:NB] = np.where(np.eye(NB, dtype=bool), 0, np.float32(NEG))
    tab = np.concatenate([np.eye(P, dtype=np.float32), masks, own], 1).astype(np.float32)
    pos = np.concatenate([np.arange(S), np.full(NB, PAST)]).astype(np.float32)
    cols = []
    for half in (DH // 2, ROPE // 2):
        inv = (10000.0 ** (-np.arange(half, dtype=np.float64) / half)).astype(np.float32)
        ang = (pos[:, None] * inv[None, :]).astype(np.float32)
        c, s = np.cos(ang.astype(np.float64)), np.sin(ang.astype(np.float64))
        cols += [c, c, -s, s]
    return tab, np.concatenate(cols, 1).astype(np.float32)


def kernel(**a):
    import concourse.bacc as bacc
    from concourse.bass_utils import run_bass_kernel_spmd

    a = {k: np.asarray(v) for k, v in a.items()}
    nc = bacc.Bacc("TRN2", target_bir_lowering=False, num_devices=1)
    tab, rope = _tables()
    arrays = {
        "x_prompt": a["x_prompt"][0], "x_sample": a["x_sample"][:, 0], "cache_mla": a["cache_mla"][0],
        "cw0": a["cache_win0"][0].reshape(NB, -1, 2 * BW), "cw1": a["cache_win1"][0].reshape(NB, -1, 2 * BW),
        "cw2": a["cache_win2"][0].reshape(NB, -1, 2 * BW), "page_table": a["page_table"],
        "c_prompt": a["c_prompt"], "c_sample": a["c_sample"], "b_ada": a["b_ada"][0],
        "w_ada": a["w_ada"][0], "w_in": a["w_in"][0], "w_qb": a["w_qb"][0],
        "w_uk": a["w_uk"][0].reshape(KVR, -1), "w_uv": a["w_uv"][0].reshape(KVR, -1),
        "w_pa": a["w_pa"][0], "w_pb": a["w_pb"][0], "w_out": a["w_out"][0],
        "gains": np.concatenate([a[n][0].reshape(-1) for n in (
            "mla_kv_norm", "mla_kr_g", "mla_qn_g", "mla_kn_g", "mla_qr_g", "dil_q_g", "dil_k_g")]),
        "cols": np.concatenate([a["norm_w"][0].reshape(KD, P).T, a["mla_qa_norm"][0].reshape(3, P).T], 1),
        "tables": tab, "rope": rope,
    }
    outs = [("y_prompt", (S, D)), ("y_sample", (NB, D)), ("rows_p", (S, CW)), ("win0_p", (P, 512)),
            ("win1_p", (S, 512)), ("win2_p", (S, 512)), ("rows_s", (NB, CW)), ("win0_s", (NB, 512)),
            ("win1_s", (NB, 512)), ("win2_s", (NB, 512))]
    arrays = {f"in_{k}": np.ascontiguousarray(x) for k, x in arrays.items()}
    aps = [nc.dram_tensor(k, x.shape, mybir.dt.from_np(x.dtype), kind="ExternalInput").ap() for k, x in arrays.items()]
    aps += [nc.dram_tensor(f"out_{k}", s, F32, kind="ExternalOutput").ap() for k, s in outs]
    trunk_step(nc, *aps)
    got = run_bass_kernel_spmd(nc, [arrays], core_ids=[0]).results[0]
    o = {k: got[f"out_{k}"] for k, _ in outs}
    win = (2, HD, DH)
    return (o["y_prompt"].reshape(1, S, D), o["y_sample"].reshape(NB, 1, D), o["rows_p"].reshape(1, 1, S, CW),
            o["win0_p"].reshape(1, 1, P, *win), o["win1_p"].reshape(1, 1, S, *win), o["win2_p"].reshape(1, 1, S, *win),
            o["rows_s"].reshape(1, NB, 1, CW), o["win0_s"].reshape(1, NB, 1, *win),
            o["win1_s"].reshape(1, NB, 1, *win), o["win2_s"].reshape(1, NB, 1, *win))
```

```python
from contextlib import ExitStack

import numpy as np

import concourse.bass as bass
from concourse import mybir

P = 128
F32 = mybir.dt.float32
F32R = mybir.dt.float32r
I32 = mybir.dt.int32
ALU = mybir.AluOpType
ACT = mybir.ActivationFunctionType
AX = mybir.AxisListType.X

D = 1024
S = 512
NT = S // P
TS = NT
NB = 8
PAST = 4096
NPAGE = PAST // P
HM, NOPE, ROPE = 8, 64, 32
QK = NOPE + ROPE
QR, KVR = 384, 256
CW = KVR + ROPE
ND, HD, DH = 3, 4, 64
BW = HD * DH
AW = HM * 64
PATTERNS = ((128, 1), (512, 4), (2048, 16))
MLA_SCALE = QK ** -0.5
DIL_SCALE = DH ** -0.5
EPS = 1e-6
NEG = -1e30
RSQRT_MAGIC = float(0x5F3759DF)
KD = D // P
LO = 64

C_Q, C_KV, C_D = 0, QR, QR + CW
C_GA = C_D + ND * 3 * BW
C_GB = C_GA + AW
C_MA = C_GB + BW
C_MB = C_MA + D

G_KV, G_KR, G_QN, G_KN, G_QR, G_DQ, G_DK = 0, 256, 288, 352, 416, 448, 640
G_ALL = 832

M_CAUSAL = 3 * P
M_R4, M_R16, M_PREV = 4 * P, 8 * P, 12 * P
M_ALL = 14 * P

BLOCKS = ([(f"ada{n}", "w_ada", 0, KD, n * 512, 512) for n in range(6)]
          + [("Q", "w_in", 0, KD, C_Q, QR), ("KV", "w_in", 0, KD, C_KV, CW)]
          + [("QB0", "w_qb", 0, QR // P, 0, 384), ("V", "w_uv", 0, KVR // P, 0, AW),
             ("QB1", "w_qb", 0, QR // P, 384, 384)])
for _g in range(ND):
    BLOCKS += [(f"D{_g}QK", "w_in", 0, KD, C_D + _g * 3 * BW, 2 * BW),
               (f"D{_g}V", "w_in", 0, KD, C_D + _g * 3 * BW + 2 * BW, BW)]
BLOCKS += [("GA", "w_in", 0, KD, C_GA, AW), ("GB", "w_in", 0, KD, C_GB, BW)]
BLOCKS += [(f"P{_b}{n}", f"w_p{_b.lower()}", 0, k, n * 512, 512)
           for n in range(2) for _b, k in (("A", AW // P), ("B", BW // P))]
BLOCKS += [(f"M{_b}{n}", "w_in", 0, KD, c + n * 512, 512)
           for n in range(2) for _b, c in (("A", C_MA), ("B", C_MB))]
BLOCKS += [(f"WO{n}", "w_out", 0, KD, n * 512, 512) for n in range(2)]
BLOCKS += [(f"P{_b}s{n}", f"w_p{_b.lower()}", 0, k, n * 512, 512)
           for n in range(2) for _b, k in (("A", AW // P), ("B", BW // P))]
BLOCKS += [(f"WOs{n}", "w_out", 0, KD, n * 512, 512) for n in range(2)]
CHUNKS = []
SPLITS = []
SPLIT_NO = []
FIRST = {}
COUNT = {}
WIDTH = {}
for _name, _w, _k0, _nk, _c, _width in BLOCKS:
    FIRST[_name], COUNT[_name], WIDTH[_name] = len(CHUNKS), _nk, _width
    for _k in range(_nk):
        if not (_name.startswith("ada") or "s" in _name):
            SPLITS.append(len(CHUNKS))
        SPLIT_NO.append(len(SPLITS))
        CHUNKS.append((_w, _k, _c, _width))

STAGES = ([("ada0", 1, "A"), ("ada1", 1, "A"), ("wukT", 2, "A"), ("xT", KD, "A")]
          + [(f"ada{n}", 1, "A") for n in range(2, 6)]
          + [("gate", 2, "A"), ("Q", 5, "A"), ("KV", 5, "A"), ("Tq", 3, "D"), ("QB0", 5, "A"),
             ("Tr", 2, "D"), ("K", 5, "A"), ("V", 4, "A"), ("QB1", 5, "A"), ("TkM", 8, "A"), ("TqM", 8, "A")])
for _g in range(ND):
    STAGES += [(f"D{_g}QK", 5, "A"), (f"D{_g}V", 5, "A")]
STAGES += [("TD", 4 * ND, "A"), ("GA", 4, "D"), ("GAs", 1, "A"), ("GB", 4, "D"), ("GBs", 1, "A"), ("To", 6, "D")]
STAGES += [(f"P{b}{n}", 4, "A") for n in range(2) for b in "AB"]
STAGES += [(f"M{b}{n}", 5, "A") for n in range(2) for b in "AB"]
STAGES += [("Tm", KD, "D"), ("WO0", 4, "A"), ("WO1", 4, "A")]
STAGES += [(f"P{b}s{n}", 1, "A") for n in range(2) for b in "AB"] + [("WOs0", 1, "A"), ("WOs1", 1, "A")]
ITEM = {}
READER = []
_seen = {"A": 0, "D": 0}
for _name, _n, _e in STAGES:
    ITEM[_name] = len(READER)
    for _ in range(_n):
        _seen[_e] += 1
        READER.append((_e, _seen[_e]))
BANKS = 7
LAST_ITEM = {n: ITEM[n] + c - 1 for n, c, _ in STAGES}
LAST_ITEM["GA"], LAST_ITEM["GB"] = ITEM["GAs"], ITEM["GBs"]
END_ITEM = {}
for _name, *_ in BLOCKS:
    END_ITEM[FIRST[_name] + COUNT[_name] - 1] = LAST_ITEM[_name]
NRAW, NHL = 4, 3
NSTAGE = 5

MLA_JOBS = [(i, h, i + 1) for i in range(NT) for h in range(HM)]
DIL_JOBS = [(i, h, (1 if i == 0 else 2) + 2 * (i + 1)) for i in range(NT) for h in range(HD)]


def widths(nb):
    return [min(4, nb - c) for c in range(0, nb, 4)]


CHUNK_END = [int(n) for n in np.cumsum([len(widths(j[2])) for j in MLA_JOBS + DIL_JOBS])]
N_MLA_CHUNKS = CHUNK_END[len(MLA_JOBS) - 1]

SMP_Q, SMP_R, SMP_KV = 1, 2, 3
F_MAX, F_DIAG, F_SUB, F_SUM, F_OBT, F_OG, F_OST, F_MS, F_MST, F_Y = range(1, 11)
Q_FREED = 6 + 5 + 5
LSTEPS = 32


def trunk_step(nc, x_prompt, x_sample, cache_mla, cw0, cw1, cw2, page_table, c_prompt, c_sample, b_ada,
               w_ada, w_in, w_qb, w_uk, w_uv, w_pa, w_pb, w_out, gains, cols, tables, rope,
               y_prompt, y_sample, rows_p, win0_p, win1_p, win2_p, rows_s, win0_s, win1_s, win2_s):
    weights = dict(w_ada=w_ada, w_in=w_in, w_qb=w_qb, w_uv=w_uv, w_pa=w_pa, w_pb=w_pb, w_out=w_out)
    ctx = ExitStack()
    with ctx:
        def sem(name):
            return ctx.enter_context(nc.semaphore(name))

        at = [16512]

        def region(nbytes):
            at[0] += nbytes
            assert at[0] <= 229344, at[0]
            return at[0] - nbytes

        def put(name, shape, offset, dt=F32):
            return nc.alloc_sbuf_tensor_at(name, [shape[0], int(np.prod(shape[1:]))], dt, offset=offset)

        def new(name, shape, dt=F32):
            n = int(np.prod(shape[1:])) * 4
            return put(name, shape, region((n + 31) // 32 * 32), dt)

        def v3(t, a, b):
            return t[:, :].rearrange("p (a b) -> p a b", a=a, b=b)

        def v4(t, a, b, c):
            return t[:, :].rearrange("p (a b c) -> p a b c", a=a, b=b, c=c)

        tab = new("tab", [P, P + M_ALL + 20])
        ident = tab[:, 0:P]
        masks = tab[:, P:P + M_ALL]
        newmask = tab[0:NB, P + M_ALL:P + M_ALL + 8]
        head_of = tab[0:NB * HD, P + M_ALL + 8:P + M_ALL + 12]
        sample_of = tab[0:NB * HD, P + M_ALL + 12:P + M_ALL + 20]
        ones = new("ones", [P, P])
        dead = at[0]
        ropes_t = new("ropes", [P, 5 * 192])
        ropes = v3(ropes_t, 5, 192)
        gn = new("gn", [P, G_ALL])
        g96 = new("g96", [P, QK])
        q_s = new("q_s", [NB, HM * QK])
        assert at[0] - dead >= NB * KVR * 4
        lat_h = put("lat_h", [NB, NB * KVR], dead)
        colt = new("colt", [P, 11])
        raw_t = new("raw", [P, NRAW * 512])
        raw = v3(raw_t, NRAW, 512)
        whi_t = new("whi", [P, NHL * 512], F32R)
        whi = v3(whi_t, NHL, 512)
        wlo_t = new("wlo", [P, NHL * 512], F32R)
        wlo = v3(wlo_t, NHL, 512)
        wq_hi_t = new("wq_hi", [P, 2 * 2 * 264], F32R)
        wq_hi = v4(wq_hi_t, 2, 2, 264)
        wq_lo_t = new("wq_lo", [P, 2 * 2 * 264], F32R)
        wq_lo = v4(wq_lo_t, 2, 2, 264)
        wuk_hi, wuk_lo = wq_hi[:, :, :, 4:260], wq_lo[:, :, :, 4:260]
        hTs_t = new("hTs", [P, KD * P], F32R)
        hTs = v3(hTs_t, KD, P)
        rows_t = new("rows", [P, 5 * CW])
        rows = v3(rows_t, 5, CW)
        gate_bc = new("gate_bc", [P, D])
        gate_s = new("gate_s", [NB, D])
        kv_s_t = new("kv_s", [NB, ND * 512])
        kv_s = v3(kv_s_t, ND, 512)
        dq_s_t = new("dq_s", [NB, ND * BW])
        dq_s = v3(dq_s_t, ND, BW)
        small = region(4096)
        ms = put("ms", [P, 40], small)
        rsx = put("rsx", [P, 40], small + 160)
        rsa = put("rsa", [P, 40], small + 320)
        rsy = put("rsy", [P, 40], small + 480)
        pe1 = put("pe1", [P, 128], small + 640)
        pe2 = put("pe2", [P, 128], small + 1152)
        amax = put("amax", [P, 16], small + 2624)
        flag = put("flag", [1, 8], small + 2848)
        mx1 = put("mx1", [32, 1], small + 2880)
        dgm = put("dgm", [32, 32], small + 2944)
        dns = put("dns", [NB, 8], small + 2816)
        qsT = put("qsT", [P, 32], small + 1920)
        lsum = put("lsum", [P, 8], small + 2688)
        snew = put("snew", [NB, NB * HM], small + 1664)
        qabs = put("qabs", [P, (NB + 1) * 2 * HM], small + 2048)
        qpe = put("qpe", [P, NB * 4 * HM], small + 3072)

        W = region(22 * 1024)
        stage_t = put("stage", [P, NSTAGE * 512], W)
        stage = v3(stage_t, NSTAGE, 512)
        sqt = put("sqt", [P, 512], W + 10240)
        tmp_t = put("tmp", [P, 5 * 512], W + 12288)
        tmp = v3(tmp_t, 5, 512)
        PT_t = put("PT", [P, 3 * 512], W + 12288)
        PT = v3(PT_t, 3, 512)
        wukT_t = put("wukT", [P, 4 * KVR], W + 12288)
        wukT = v3(wukT_t, 4, KVR)
        qn_s = put("qn_s", [NB, HM * NOPE], W + 12288 + 4 * 1792)
        k_s = put("k_s", [NB, HM * QK], W + 16384)
        low_s = new("low_s", [NB + 1, 512])

        ON = region(12 * 1024)
        HT = region(32 * 1024)
        V = region(229344 - at[0])
        K1 = 1024
        assert 229344 - V >= 62 * K1, 229344 - V
        oN = v3(put("oN", [P, NT * 768], ON), NT, 768)
        hThi = v3(put("hT_hi", [P, KD * S], HT, F32R), KD, S)
        hTlo = v3(put("hT_lo", [P, KD * S], HT + 16 * K1, F32R), KD, S)
        wukr = v3(put("wuk_raw", [P, 2 * 512], ON), 2, 512)
        xsq = put("xsq", [P, D], ON + 4 * K1)
        xT = v3(put("xT", [P, KD * S], HT + 16 * K1), KD, S)
        xt = v3(put("x_tiles", [P, NT * D], V), NT, D)
        xs1 = put("x_s1", [NB, D], V + 16 * K1)
        cs = v3(put("silu_cT", [P, KD * 9], V + 20 * K1), KD, 9)
        c9 = put("c9", [NB + 1, D], V + 24 * K1)
        c9b = put("c9b", [NB + 1, D], V + 28 * K1)
        ada = put("ada", [NB + 1, 3 * D], V + 32 * K1)
        bada = put("bada", [NB + 1, 3 * D], V + 44 * K1)
        xTs = put("xTs", [P, KD * NB], V + 56 * K1)
        G1 = v3(put("G1", [P, KD * 9], V + 57 * K1), KD, 9)
        SH = v3(put("SH", [P, KD * 9], V + 57 * K1 + 512), KD, 9)
        hs_f = v3(put("hs_f", [P, KD * NB], V + 58 * K1), KD, NB)
        qh = v3(put("qh", [P, 8 * 384], ON), 8, 384)
        qan = v3(put("qan", [P, 5 * QR], V), 5, QR)
        qTm = v3(put("qTm", [QK, HM * S], V), HM, S)
        kTm = v3(put("kTm", [QK, HM * S], V + 16 * K1), HM, S)
        vm = v3(put("v_mla", [P, NT * AW], V + 32 * K1), NT, AW)
        qaThi = v3(put("qaT_hi", [P, 3 * S], V + 16 * K1, F32R), 3, S)
        qaTlo = v3(put("qaT_lo", [P, 3 * S], V + 22 * K1, F32R), 3, S)
        qaTs = v3(put("qaTs", [P, 3 * P], V + 28 * K1, F32R), 3, P)
        rTs = v3(put("rTs", [P, 2 * P], V + 30 * K1, F32R), 2, P)
        rThi = v3(put("rT_hi", [P, 2 * S], V + 40 * K1, F32R), 2, S)
        rTlo = v3(put("rT_lo", [P, 2 * S], V + 44 * K1, F32R), 2, S)
        pq1 = put("pq1", [P, 128], V + 60 * K1)
        pq2 = put("pq2", [P, 128], V + 60 * K1 + 512)
        kc = v3(put("kc", [P, NT * HM * QK], V + 48 * K1), NT, HM * QK)
        Pm_t = put("probs", [P, 2 * 1280], V + 48 * K1)
        Pm = {4: v3(Pm_t, 4, 640), 2: v3(Pm_t, 2, 1280)}
        kvo = v4(put("kvo", [P, ND * NT * 512], V), ND, NT, 512)
        dqT = v4(put("dqT", [P, ND * 2 * S], V + 24 * K1), ND, 2, S)
        dkT = v4(put("dkT", [P, ND * 2 * S], V + 36 * K1), ND, 2, S)
        dqn = v4(put("dqn", [P, ND * NT * BW], V + 48 * K1), ND, NT, BW)
        oThi = v3(put("oT_hi", [P, 6 * S], V, F32R), 6, S)
        oTlo = v3(put("oT_lo", [P, 6 * S], V + 12 * K1, F32R), 6, S)
        ya = v3(put("ya", [P, NT * D], V + 24 * K1), NT, D)
        yb = v3(put("yb", [P, NT * D], V + 40 * K1), NT, D)
        merge_s = put("merge_gates_s", [NB, 2 * D], V)
        mix_s = put("mix_gates_s", [NB, 768], V + 59 * K1)
        xr = [v3(put("x_again0", [P, NT * 512], V + 44 * K1), NT, 512),
              v3(put("x_again1", [P, NT * 512], ON), NT, 512)]
        cn = [v3(put(f"cn{p}", [P, NPAGE * CW], (V + 8 * K1, ON)[p]), NPAGE, CW) for p in range(2)]
        cThi = v3(put("cT_hi", [P, 2 * 1024], W, F32R), 2, 1024)
        cTlo = v3(put("cT_lo", [P, 2 * 1024], W + 8 * K1, F32R), 2, 1024)
        sq4 = v3(put("sq4", [P, 4 * 512], V + 44 * K1), 4, 512)
        kpT = v3(put("kpT", [P, 2 * P], V + 52 * K1), 2, P)
        kpn = v3(put("kpn", [P, 2 * P], V + 53 * K1), 2, P)
        HE = HT + 24 * K1
        Sq = v3(put("s_latent", [P, NPAGE * HM], HE), NPAGE, HM)
        Sk = v3(put("s_rotary", [P, NPAGE * HM], HE + K1), NPAGE, HM)
        ssq = put("ssq", [P, NPAGE * HM], HE + 3 * K1)
        lx = put("lx", [P, 128], HE + 4 * K1)
        lax = put("lax", [P, 128], HE + 4 * K1 + 512)
        ly = put("ly", [P, 128], HE + 5 * K1)
        Sc_t = put("scores", [P, 33 * HM], HE + 5 * K1 + 512)
        Sc = v3(Sc_t, 33, HM)
        Ex_t = put("expd", [P, 33 * HM], HE + 6 * K1 + 768)
        Ex = v3(Ex_t, 33, HM)
        latT = put("latT", [P, NB * 16], V + 56 * K1)
        pmx = put("pmx", [P, 8], V + 57 * K1)
        pt = put("pt", [1, NB * NPAGE], V + 58 * K1, I32)
        esm = put("esm", [P, 8], V + 57 * K1 + 256)
        rdn = put("rdn", [P, 8], V + 57 * K1 + 288)
        sdk0 = v3(put("sdk0", [P, 18 * 512], V + 8 * K1), 18, 512)
        sdk1 = v3(put("sdk1", [P, 6 * 512], V + 44 * K1), 6, 512)
        prod = v3(put("prod", [P, 2 * 768], W + 10 * K1), 2, 768)
        wuvr = v3(put("wuv_raw", [P, 2 * 512], W + 16 * K1), 2, 512)
        SD_t = put("sd", [P, NB * 24], W + 20 * K1)
        SD = v3(SD_t, NB, 24)
        ED_t = put("ed", [P, NB * 24], W + 20 * K1 + 768)
        own_ed = v3(put("own_ed", [NB, ND * NB * HD], ON + 7 * K1 + 512), ND, NB * HD)
        WS = W + 21 * K1 + 512
        dn = put("dn", [NB, 16], WS)
        dpm = put("dpm", [P, 32], WS + 64)
        dsm = put("dsm", [P, 32], WS + 192)
        rl = put("rl", [P, 32], WS + 320)
        EZ_t = put("ed_padded", [P, NB * 100], ON + 4 * K1)
        ob = put("ob", [NB * HD, BW], ON + 8 * K1)
        osT = v3(put("osT", [P, 6 * NB], ON + 13 * K1), 6, NB)
        msT = v3(put("msT", [P, KD * NB], ON + 14 * K1), KD, NB)
        og = put("og", [NB, 768], ON + 16 * K1)
        sgm = put("sgm", [NB, 768], ON + 19 * K1)
        mgm = put("mgm", [NB, 2 * D], ON + 22 * K1)
        yab = v3(put("yab", [NB, 2 * D], ON + 30 * K1), 2, D)
        xs2 = put("x_s2", [NB, D], ON + 38 * K1)

        ps = ctx.enter_context(nc.psum_tensor("ps", [P, 8, 512], F32))

        def psw(bank, w):
            return ps[:, :, :].rearrange("p b c -> p (b c)")[:, bank * 512:bank * 512 + w]

        tab_in = sem("tab_in")
        consts_in, c_in, wuk_in, bada_in = sem("consts_in"), sem("c_in"), sem("wuk_in"), sem("bada_in")
        x_in = [sem(f"x_in{t}") for t in range(5)]
        raw_in = [sem(f"raw_in{i}") for i in range(NRAW)]
        w_hi_ready, w_lo_ready, w_used = sem("w_hi_ready"), sem("w_lo_ready"), sem("w_used")
        z_done = sem("z_done")
        evac_a, evac_d = sem("evac_a"), sem("evac_d")
        act_half = sem("act_half")
        low_added = sem("low_added")
        stage_free = sem("stage_free")
        even_done = sem("even_done")
        misc_done, misc_free = sem("misc_done"), sem("misc_free")
        dve_step = sem("dve_step")
        pool_step = sem("pool_step")
        zeroed, sigm_c, csilu, cs_ready, wuk_h, wuk_split = (
            sem("zeroed"), sem("sigm_c"), sem("csilu"), sem("cs_ready"), sem("wuk_h"), sem("wuk_split"))
        xn_ready, ada_ready, h_f, h_hi, h_ready = (
            sem("xn_ready"), sem("ada_ready"), sem("h_f"), sem("h_hi"), sem("h_ready"))
        qan_ready, rows_ready, qh0_ready, qh1_ready, kc_ready = (
            sem("qan_ready"), sem("rows_ready"), sem("qh0_ready"), sem("qh1_ready"), sem("kc_ready"))
        smp_ready = sem("smp_ready")
        y_roped, rope_done = sem("y_roped"), sem("rope_done")
        qk_done, masked, exp_done, tr_done, trp_done, pt_a, pt_d, pv_chunk, o_done = (
            sem("qk_done"), sem("masked"), sem("exp_done"), sem("tr_done"), sem("trp_done"), sem("pt_a"),
            sem("pt_d"), sem("pv_chunk"), sem("o_done"))
        rows_out, win_out, y_rdy, pt_in = sem("rows_out"), sem("win_out"), sem("y_rdy"), sem("pt_in")
        gated, merged = sem("gated"), sem("merged")
        xr_in = [sem(f"xr_in{n}") for n in range(2)]
        y_out = [sem(f"y_out{n}") for n in range(2)]
        cn_in = [[sem(f"cn_in{p}{q}") for q in range(4)] for p in range(2)]
        ct_done, ct_hi, ct_ready, k_done, sq_done, red_done, s_done, s_read = (
            sem("ct_done"), sem("ct_hi"), sem("ct_ready"), sem("k_done"), sem("sq_done"), sem("red_done"),
            sem("s_done"), sem("s_read"))
        pm_ready, pmT_done, dg_ready, mx_done, sub_done, ex_done, es_ready, pv_done, lat_done, lstep = (
            sem("pm_ready"), sem("pmT_done"), sem("dg_ready"), sem("mx_done"), sem("sub_done"), sem("ex_done"),
            sem("es_ready"), sem("pv_done"), sem("lat_done"), sem("lstep"))
        kpn_ready, lt_done, lt_ready = sem("kpn_ready"), sem("lt_done"), sem("lt_ready")
        sdk_in = [sem("sdk_in0"), sem("sdk_in1")]
        wuv_in, late_in = sem("wuv_in"), sem("late_in")
        qb_done, qb_read, f_pe, f_dve, f_act = (
            sem("qb_done"), sem("qb_read"), sem("f_pe"), sem("f_dve"), sem("f_act"))
        s_out = sem("s_out")

        def rep(ap, axis, n):
            u = ap.unsqueeze(axis)
            shape = list(u.shape)
            shape[axis] = n
            return u.to_broadcast(shape)

        def wait_used(eng, j):
            if j in END_ITEM:
                eng.wait_ge(z_done, END_ITEM[j] + 1)
            else:
                eng.wait_ge(w_used, sum(1 for i in range(j + 1) if i not in END_ITEM))

        def wait_evac(eng, idx):
            e, n = READER[idx]
            eng.wait_ge(evac_a if e == "A" else evac_d, n)

        def pt_copy(eng, fn, chunk, w, signal, extra):
            eng.wait_ge(trp_done, chunk + 1)
            if chunk >= 3:
                eng.wait_ge(pv_chunk, chunk - 2)
            fn(PT[:, chunk % 3, 0:w * P], ps[:, 6 + chunk % 2, 0:w * P], *extra).then_inc(signal, 1)

        def wait_pt(eng, c):
            if c % 2 == 0:
                eng.wait_ge(pt_d, c // 2 + 1)
            else:
                eng.wait_ge(pt_a, (c + 1) // 2)

        def q_heads(i, t):
            out = q_s[:, i * 384:(i + 1) * 384] if t == TS else qh[:, i * NT + t, :]
            return out.rearrange("p (h e) -> p h e", e=QK)

        def lanes(t):
            return NB if t == TS else P

        block = ctx.enter_context(nc.Block())

        @block.sync
        def _(sp):
            done = [0]

            def stream_to(last):
                while done[0] < min(last, len(CHUNKS)):
                    j = done[0]
                    w, k, c, width = CHUNKS[j]
                    if j >= NRAW:
                        if j - NRAW in SPLITS:
                            sp.wait_ge(w_lo_ready, SPLIT_NO[j - NRAW])
                        else:
                            wait_used(sp, j - NRAW)
                    sp.dma_start(raw[:, j % NRAW, 0:width], weights[w][k * P:(k + 1) * P, c:c + width])\
                      .then_inc(raw_in[j % NRAW], 16)
                    done[0] += 1

            def load_page(p, quarter, index, tile, summed=None):
                page = sp.value_load(pt[0:1, bass.ds(index, 1)], min_val=0, max_val=cache_mla.shape[0] - 1)
                if summed is not None:
                    sp.wait_ge(pv_done, summed + 1)
                sp.dma_start(cn[p][:, bass.ds(tile, 1), :],
                             cache_mla[bass.ds(page, 1), :, :].rearrange("a p c -> p a c"))\
                  .then_inc(cn_in[p][quarter], 16)

            sp.dma_start(c9[0:NB, :], c_sample).then_inc(c_in, 16)
            sp.dma_start(c9[NB:NB + 1, :], c_prompt).then_inc(c_in, 16)
            sp.dma_start(tab[:, :], tables).then_inc(tab_in, 16)
            sp.dma_start(colt[:, :], cols).then_inc(tab_in, 16)
            stream_to(NRAW)
            sp.dma_start(wukr[:, :, :], w_uk.rearrange("(k p) n -> p k n", p=P)).then_inc(wuk_in, 16)
            sp.dma_start(bada[:, :], b_ada.rearrange("(a n) -> a n", a=1).to_broadcast([NB + 1, 3 * D]))\
              .then_inc(bada_in, 16)
            sp.dma_start(ropes[:, 0:NT, :], rope[0:S, :].rearrange("(t p) c -> p t c", p=P)).then_inc(consts_in, 16)
            sp.dma_start(ropes[0:NB, TS, :], rope[S:S + NB, :]).then_inc(consts_in, 16)
            sp.dma_start(gn[:, :], gains.rearrange("(a n) -> a n", a=1).to_broadcast([P, G_ALL]))\
              .then_inc(consts_in, 16)
            stream_to(FIRST["WO0"])
            sp.wait_ge(z_done, ITEM["To"] + 1)
            sp.dma_start(pt[:, :], page_table.rearrange("b n -> (b n)").rearrange("(a n) -> a n", a=1))\
              .then_inc(pt_in, 16)
            stream_to(FIRST["WO0"] + NRAW)
            sp.wait_ge(pt_in, 16)
            sp.wait_ge(z_done, LAST_ITEM["Tm"] + 1)
            n = 0
            for j in range(FIRST["WO0"] + NRAW, FIRST["PAs0"]):
                stream_to(j + 1)
                for _ in range(3):
                    if n < NPAGE:
                        load_page(0, n // 8, n, n)
                        n += 1
            stream_to(FIRST["PAs0"] + NRAW)
            sp.wait_ge(z_done, LAST_ITEM["WO1"] + 1)
            sp.wait_ge(y_out[1], 16)
            sp.dma_start(wuvr[:, :, :], w_uv.rearrange("(k p) n -> p k n", p=P)).then_inc(wuv_in, 16)
            for quarter in range(4):
                with sp.Fori(0, 8) as u:
                    load_page(1, quarter, NPAGE + 8 * quarter + u, 8 * quarter + u)
            with sp.Fori(0, (NB - 2) // 2) as i:
                for p in range(2):
                    for quarter in range(4):
                        with sp.Fori(0, 8) as u:
                            load_page(p, quarter, 2 * NPAGE * i + (2 + p) * NPAGE + 8 * quarter + u, 8 * quarter + u,
                                      2 * i + p)
            wins = [cw[:, :, :].rearrange("b (r s) c -> r b s c", s=dil)[:, :, 0, :]
                    for cw, (_, dil) in zip((cw0, cw1, cw2), PATTERNS)]
            sp.wait_ge(pv_done, NB - 1)
            for g in range(ND):
                sp.dma_start(sdk0[:, :, :].rearrange("p (b g) c -> p b g c", g=ND)[:, :, g, :],
                             wins[g][:, 0:6, :]).then_inc(sdk_in[0], 16)
            sp.wait_ge(red_done, NB * NPAGE)
            sp.wait_ge(ct_ready, NB * 8)
            sp.wait_ge(s_done, NB * 8)
            for g in range(ND):
                sp.dma_start(sdk1[:, :, :].rearrange("p (b g) c -> p b g c", g=ND)[:, :, g, :],
                             wins[g][:, 6:8, :]).then_inc(sdk_in[1], 16)
            sp.wait_ge(pv_done, NB)
            sp.dma_start(xs2[:, :], x_sample).then_inc(late_in, 16)
            stream_to(len(CHUNKS))
            sp.wait_ge(f_dve, F_Y)
            sp.dma_start(y_sample, xs2[:, :]).then_inc(s_out, 16)
            sp.wait_ge(s_out, 16)
            sp.wait_ge(rows_out, 32)
            sp.wait_ge(win_out, 16 * 6)
            for n in range(2):
                sp.wait_ge(y_out[n], 16)

        @block.scalar
        def _(act):
            split = [0]
            staged = [0]
            lows = [0, 0]

            def split_to(last):
                while split[0] < min(last, len(CHUNKS)):
                    j = split[0]
                    split[0] += 1
                    if j not in SPLITS:
                        continue
                    width = CHUNKS[j][3]
                    s = SPLIT_NO[j] - 1
                    act.wait_ge(raw_in[j % NRAW], 16 * (j // NRAW + 1))
                    if s >= NHL:
                        wait_used(act, SPLITS[s - NHL])
                    nc.scalar.activation(whi[:, s % NHL, 0:width], raw[:, j % NRAW, 0:width], ACT.Copy)\
                      .then_inc(w_hi_ready, 1)

            def split_for(name):
                split_to(FIRST[name] + COUNT[name] + NHL)

            def bank(idx, w, n=P, start=0):
                return ps[start:start + n, idx % BANKS, 0:w]

            def copy_out(idx, out, w, n=P, func=ACT.Copy):
                act.wait_ge(z_done, idx + 1)
                nc.scalar.activation(out, bank(idx, w, n), func).then_inc(evac_a, 1)

            def next_stage():
                k = staged[0]
                staged[0] += 1
                if k >= NSTAGE:
                    act.wait_ge(stage_free, k - NSTAGE + 1)
                return stage[:, k % NSTAGE, :]

            def to_stage(idx, w, func=ACT.Copy, n=P):
                copy_out(idx, next_stage()[0:n, 0:w], w, n, func=func)

            def to_stage_small(idx, w, added_at_once=True, n=NB):
                out = next_stage()
                if lows[0]:
                    act.wait_ge(stage_free, lows[0])
                if lows[1]:
                    act.wait_ge(low_added, lows[1])
                if added_at_once:
                    lows[0], lows[1] = 0, lows[1] + 1
                else:
                    lows[0] = staged[0]
                act.wait_ge(z_done, idx + 1)
                nc.scalar.activation(out[0:n, 0:w], bank(idx, w, n), ACT.Copy)
                nc.scalar.activation(low_s[0:n, 0:w], bank(idx, w, n, LO), ACT.Copy).then_inc(evac_a, 1)

            def half(idx, out, func=ACT.Copy, scale=1.0):
                act.wait_ge(z_done, idx + 1)
                nc.scalar.activation(out, bank(idx, 512), func, scale=scale).then_inc(act_half, 1)

            def attention(jobs, n0, c0, slots, ahead, scale):
                def exp(n):
                    s = n % slots
                    w = jobs[n - n0][2] * P
                    act.wait_ge(masked, n + 1)
                    p = Pm[slots][:, s, 0:w]
                    nc.scalar.activation(p, p, ACT.Exp, bias=amax[:, 4 * s + 2:4 * s + 3],
                                         scale=scale, accum_out=lsum[:, n % 4:n % 4 + 1]).then_inc(exp_done, 1)

                chunk = c0
                for n in range(n0, n0 + ahead):
                    exp(n)
                for n in range(n0, n0 + len(jobs)):
                    if n + ahead < n0 + len(jobs):
                        exp(n + ahead)
                    for w in widths(jobs[n - n0][2]):
                        if chunk % 2:
                            pt_copy(act, nc.scalar.activation, chunk, w, pt_a, (ACT.Copy,))
                        chunk += 1

            for t in range(NT):
                act.dma_start(xt[:, t, :], x_prompt[t * P:(t + 1) * P, :]).then_inc(x_in[t], 16)
            act.dma_start(xs1[:, :], x_sample).then_inc(x_in[TS], 16)
            act.wait_ge(c_in, 32)
            nc.scalar.activation(c9b[:, :], c9[:, :], ACT.Sigmoid).then_inc(sigm_c, 1)
            act.wait_ge(wuk_in, 16)
            nc.scalar.activation(wuk_hi, wukr[:, :, :].rearrange("p c (f n) -> p c f n", f=2), ACT.Copy)\
              .then_inc(wuk_h, 1)
            for n in range(2):
                to_stage(ITEM[f"ada{n}"], 512, n=NB + 1)
            for i in range(2):
                copy_out(ITEM["wukT"] + i, wukT_t[:, i * 512:(i + 1) * 512], 512)
            for k in range(KD):
                copy_out(ITEM["xT"] + k, xT[:, k, :], 512)
            for n in range(2, 6):
                to_stage(ITEM[f"ada{n}"], 512, n=NB + 1)
            split_to(FIRST["Q"] + NHL)
            for n in range(2):
                copy_out(ITEM["gate"] + n, gate_bc[:, n * 512:(n + 1) * 512], 512)
            for k in range(KD):
                act.wait_ge(h_f, k + 1)
                nc.scalar.activation(hThi[:, k, :], xT[:, k, :], ACT.Copy).then_inc(h_hi, 1)
            for name, w in (("Q", QR), ("KV", CW)):
                split_for(name)
                for t in range(NT):
                    to_stage(ITEM[name] + t, w)
                to_stage_small(ITEM[name] + TS, w)
            for c in range(3):
                half(ITEM["Tq"] + c, qaThi[:, c, :], scale=colt[:, KD + c:KD + c + 1])

            def stage_q(i):
                split_for(f"QB{i}")
                for t in range(NT):
                    to_stage(ITEM[f"QB{i}"] + t, 384)
                to_stage_small(ITEM[f"QB{i}"] + TS, 384)

            stage_q(0)
            for c in range(2):
                half(ITEM["Tr"] + c, rThi[:, c, :])
            for t in range(NT):
                to_stage(ITEM["K"] + t, 512)
            to_stage_small(ITEM["K"] + TS, 512)
            split_for("V")
            for t in range(NT):
                copy_out(ITEM["V"] + t, vm[:, t, :], 512)
            stage_q(1)
            for t in range(NT):
                for i in range(2):
                    idx = ITEM["TkM"] + 2 * t + i
                    copy_out(idx, kTm[:, 4 * i:4 * i + 4, t * P:(t + 1) * P], 512, QK)
            for i in range(2):
                for t in range(NT):
                    idx = ITEM["TqM"] + i * NT + t
                    copy_out(idx, qTm[:, 4 * i:4 * i + 4, t * P:(t + 1) * P], 512, QK)
            attention(MLA_JOBS, 0, 0, 4, 2, MLA_SCALE)
            for g in range(ND):
                split_for(f"D{g}QK")
                for t in range(NT):
                    to_stage(ITEM[f"D{g}QK"] + t, 512)
                to_stage_small(ITEM[f"D{g}QK"] + TS, 512)
                split_for(f"D{g}V")
                for t in range(NT):
                    copy_out(ITEM[f"D{g}V"] + t, kvo[:, g, t, BW:2 * BW], BW)
                to_stage_small(ITEM[f"D{g}V"] + TS, BW, False)
            for i in range(4 * ND):
                g, is_k, p = i // 4, i // 2 % 2, i % 2
                copy_out(ITEM["TD"] + i, (dkT if is_k else dqT)[:, g, p, :], 512)
            attention(DIL_JOBS, len(MLA_JOBS), N_MLA_CHUNKS, 2, 1, DIL_SCALE)
            for name, w in (("GA", AW), ("GB", BW)):
                split_for(name)
                for t in range(NT):
                    act.wait_ge(z_done, ITEM[name] + t + 1)
                    out = next_stage()
                    nc.scalar.activation(out[:, 0:w], bank(ITEM[name] + t, w), ACT.Sigmoid).then_inc(act_half, 1)
                to_stage_small(ITEM[name + "s"], w, False)
            act.wait_ge(win_out, 16 * 3)
            for c in range(6):
                half(ITEM["To"] + c, oThi[:, c, :])
            for n in range(2):
                for b, out in (("A", ya), ("B", yb)):
                    split_for(f"P{b}{n}")
                    for t in range(NT):
                        copy_out(ITEM[f"P{b}{n}"] + t, out[:, t, n * 512:(n + 1) * 512], 512)
            act.dma_start(xr[1][:, :, :], x_prompt[:, 512:1024].rearrange("(t p) c -> p t c", p=P))\
               .then_inc(xr_in[1], 16)
            for n in range(2):
                for b in "AB":
                    split_for(f"M{b}{n}")
                    for t in range(NT):
                        to_stage(ITEM[f"M{b}{n}"] + t, 512, ACT.Sigmoid)
                    to_stage_small(ITEM[f"M{b}{n}"] + TS, 512, False)
            for k in range(KD):
                half(ITEM["Tm"] + k, hThi[:, k, :])
            act.wait_ge(merged, 2 * NT)
            act.dma_start(xr[0][:, :, :], x_prompt[:, 0:512].rearrange("(t p) c -> p t c", p=P))\
               .then_inc(xr_in[0], 16)
            for n in range(2):
                split_for(f"WO{n}")
                for t in range(NT):
                    to_stage(ITEM[f"WO{n}"] + t, 512)
            act.wait_ge(stage_free, staged[0])
            act.wait_ge(y_out[0], 16)

            def hi_rows(G, q):
                act.wait_ge(ct_done, G + 1)
                if not (isinstance(G, int) and G < 2):
                    act.wait_ge(k_done, 4 * G - 4)
                nc.scalar.activation(cThi[:, q % 2, :], psw(0, 1024), ACT.Copy).then_inc(ct_hi, 1)

            def rotary_keys(G, g, p, turn):
                if g % 2 == 0:
                    act.wait_ge(cn_in[p][g // 2], 128 * turn + 128)
                if not (isinstance(G, int) and G < 2):
                    act.wait_ge(ct_done, G - 1)
                nc.scalar.activation(kpn[:, g % 2, :].rearrange("p (u e) -> p u e", u=4),
                                     cn[p][:, 4 * g:4 * g + 4, KVR:CW], ACT.Copy).then_inc(kpn_ready, 1)

            def batch(b, p, turn, next_turn, first, last):
                k0 = 4 - 4 * p
                s0 = 256 * p
                for g in range(8):
                    if g == 0 and first:
                        rotary_keys(8 * b, 0, p, turn)
                        rotary_keys(8 * b + 1, 1, p, turn)
                        hi_rows(b * 8, 0)
                    if not (last and g == 7):
                        hi_rows(b * 8 + g + 1, g + 1)
                    for u in range(4):
                        U = b * NPAGE + 4 * g + u
                        act.wait_ge(k_done, U + 1)
                        if not (first and 4 * g + u < 4):
                            act.wait_ge(red_done, U - 3)
                        kb = ps[:, 3 + 2 * (u % 2):5 + 2 * (u % 2), :]
                        nc.scalar.activation(Sq[:, 4 * g + u, :].rearrange("p (f h) -> p f h", f=2),
                                             kb[:, :, s0:s0 + 4], ACT.Copy)
                        nc.scalar.activation(sq4[:, u, :].rearrange("p (f n) -> p f n", f=2),
                                             kb[:, :, k0:k0 + 256], ACT.Square).then_inc(sq_done, 1)
                        if u == 2 and g < 6:
                            rotary_keys(8 * b + g + 2, g + 2, p, turn)
                        elif u == 2 and not last:
                            rotary_keys(8 * b + g + 2, g - 6, 1 - p, next_turn)
                        if g == 4 and u == 0 and not first:
                            expo(b - 1)

            def expo(b):
                act.wait_ge(sub_done, b + 1)
                nc.scalar.activation(Ex_t[:, :], Sc_t[:, :], ACT.Exp, scale=MLA_SCALE).then_inc(ex_done, 1)

            batch(0, 0, 0, 0, True, False)
            with act.Fori(0, (NB - 2) // 2) as i:
                batch(2 * i + 1, 1, i, i + 1, False, False)
                batch(2 * i + 2, 0, i + 1, i + 1, False, False)
            batch(NB - 1, 1, (NB - 1) // 2, 0, False, True)
            expo(NB - 1)
            act.wait_ge(f_dve, F_SUB)
            nc.scalar.activation(ED_t[:, :], SD_t[:, :], ACT.Exp, scale=DIL_SCALE).then_inc(f_act, 1)
            nc.scalar.activation(sgm[:, :], mix_s[:, :], ACT.Sigmoid).then_inc(f_act, 1)
            nc.scalar.activation(mgm[:, :], merge_s[:, :], ACT.Sigmoid).then_inc(f_act, 1)
            for n in range(2):
                for b in "AB":
                    to_stage(ITEM[f"P{b}s{n}"], 512, n=NB)
            for n in range(2):
                to_stage(ITEM[f"WOs{n}"], 512, n=NB)

        @block.gpsimd
        def _(pool):
            low = [0]
            steps = [0]

            def link(ins):
                steps[0] += 1
                ins.then_inc(pool_step, 1)
                pool.wait_ge(pool_step, steps[0])

            def low_to(last):
                while low[0] < min(last, len(CHUNKS)):
                    j = low[0]
                    low[0] += 1
                    if j not in SPLITS:
                        continue
                    width = CHUNKS[j][3]
                    s = SPLIT_NO[j] - 1
                    pool.wait_ge(w_hi_ready, s + 1)
                    nc.gpsimd.tensor_tensor(out=wlo[:, s % NHL, 0:width], in0=raw[:, j % NRAW, 0:width],
                                            in1=whi[:, s % NHL, 0:width].bitcast(F32), op=ALU.subtract)\
                      .then_inc(w_lo_ready, 1)

            def rotate(g, t, c):
                n = lanes(t)
                y = tmp[0:n, c % 2, :].rearrange("p (h e) -> p h e", e=DH)
                t1 = tmp[0:n, 2, :]
                t2 = tmp[0:n, 3, :].rearrange("p (h e) -> p h e", e=DH)
                sin = ropes[0:n, t, 64:128]
                pool.wait_ge(y_roped, 2 * c + 1)
                if c:
                    pool.wait_ge(rope_done, c)
                nc.gpsimd.tensor_tensor(out=t2[:, :, 0:32], in0=y[:, :, 32:64], in1=rep(sin[:, 0:32], 1, 8), op=ALU.mult)
                link(nc.gpsimd.tensor_tensor(out=t2[:, :, 32:64], in0=y[:, :, 0:32], in1=rep(sin[:, 32:64], 1, 8),
                                             op=ALU.mult))
                pool.wait_ge(y_roped, 2 * c + 2)
                q_out = dq_s[:, g, :] if t == TS else dqn[:, g, t, :]
                k_out = kv_s[:, g, 0:BW] if t == TS else kvo[:, g, t, 0:BW]
                t2f = tmp[0:n, 3, :]
                nc.gpsimd.tensor_tensor(out=q_out, in0=t1[:, 0:BW], in1=t2f[:, 0:BW], op=ALU.add)
                nc.gpsimd.tensor_tensor(out=k_out, in0=t1[:, BW:2 * BW], in1=t2f[:, BW:2 * BW], op=ALU.add)\
                  .then_inc(rope_done, 1)

            nc.gpsimd.memset(ones[:, :], 1.0).then_inc(zeroed, 1)
            nc.gpsimd.memset(hTs[:, :, :].bitcast(F32), 0.0).then_inc(zeroed, 1)
            pool.wait_ge(cs_ready, 1)
            nc.gpsimd.memset(qaTs[:, :, :].bitcast(F32), 0.0).then_inc(zeroed, 1)
            nc.gpsimd.memset(rTs[:, :, :].bitcast(F32), 0.0).then_inc(zeroed, 1)

            def finish_q(t):
                n = lanes(t)
                o3 = q_heads(0, t)
                x = o3[:, :, NOPE:QK]
                a = pq1[0:n, :].rearrange("p (h e) -> p h e", e=ROPE)
                b = pq2[0:n, :].rearrange("p (h e) -> p h e", e=ROPE)
                rot = ropes[0:n, t, 128:192]
                pool.wait_ge(stage_free, Q_FREED + t + 1)
                link(nc.gpsimd.tensor_tensor(out=o3, in0=o3, in1=rep(g96[0:n, :], 1, 4), op=ALU.mult))
                if t == TS:
                    nc.gpsimd.tensor_copy(qn_s[:, 0:256].rearrange("p (h e) -> p h e", e=NOPE), o3[:, :, 0:NOPE])
                nc.gpsimd.tensor_tensor(out=a, in0=x, in1=rep(rot[:, 0:32], 1, 4), op=ALU.mult)
                nc.gpsimd.tensor_tensor(out=b[:, :, 0:16], in0=x[:, :, 16:32], in1=rep(rot[:, 32:48], 1, 4), op=ALU.mult)
                link(nc.gpsimd.tensor_tensor(out=b[:, :, 16:32], in0=x[:, :, 0:16], in1=rep(rot[:, 48:64], 1, 4),
                                             op=ALU.mult))
                nc.gpsimd.tensor_tensor(out=x, in0=a, in1=b, op=ALU.add).then_inc(qh0_ready, 1)
                pool.wait_ge(qh0_ready, t + 1)

            low_to(FIRST["QB1"] + COUNT["QB1"])
            for t in range(5):
                finish_q(t)
            low_to(FIRST["D0QK"] + NHL)
            pool.wait_ge(rows_ready, 5)
            pool.dma_start(rows_p.rearrange("(t p) c -> p t c", p=P), rows[:, 0:NT, :]).then_inc(rows_out, 16)
            pool.dma_start(rows_s, rows[0:NB, TS, :]).then_inc(rows_out, 16)
            for g in range(ND):
                low_to(FIRST[f"D{g}V"] + COUNT[f"D{g}V"] + NHL)
                for t in range(5):
                    rotate(g, t, 5 * g + t)
                    low_to(low[0] + (g < ND - 1))
            wait_evac(pool, ITEM[f"D{ND - 1}V"] + TS)
            pool.dma_start(win0_p, kvo[:, 0, NT - 1, :]).then_inc(win_out, 16)
            for g, out in ((1, win1_p), (2, win2_p)):
                pool.dma_start(out.rearrange("(t p) c -> p t c", p=P), kvo[:, g, :, :]).then_inc(win_out, 16)
            low_to(FIRST["WO0"])
            pool.wait_ge(smp_ready, SMP_KV)
            for g, out in enumerate((win0_s, win1_s, win2_s)):
                pool.dma_start(out, kv_s[:, g, :]).then_inc(win_out, 16)
            for n in range(2):
                low_to(FIRST[f"WO{n}"] + COUNT[f"WO{n}"] + NHL)
                pool.wait_ge(y_rdy, NT * (n + 1))
                pool.dma_start(y_prompt[:, n * 512:(n + 1) * 512].rearrange("(t p) c -> p t c", p=P), xr[n][:, :, :])\
                    .then_inc(y_out[n], 16)

        @block.tensor
        def _(pe):
            mm = nc.tensor.matmul
            miscs = [0]

            def wait_bank(idx):
                if idx >= BANKS:
                    wait_evac(pe, idx - BANKS)

            def misc_begin():
                if miscs[0]:
                    pe.wait_ge(misc_free, miscs[0])
                miscs[0] += 1

            def block_of(name, first, tiles, hi=None, lo=None, small=None, wait_h=False):
                f, nk, w = FIRST[name], COUNT[name], WIDTH[name]
                for k in range(nk):
                    j = f + k
                    pe.wait_ge(w_lo_ready, SPLIT_NO[j])
                    if wait_h:
                        pe.wait_ge(h_ready, k + 2)
                    s = (SPLIT_NO[j] - 1) % NHL
                    bh, bl = whi[:, s, 0:w], wlo[:, s, 0:w]
                    for n, t in enumerate(tiles):
                        idx = first + n
                        if k == 0:
                            wait_bank(idx)
                        out = ps[:, idx % BANKS, 0:w]
                        st, en = k == 0, k == nk - 1
                        if t == TS:
                            mm(out, small[:, k, :], bh, start=st, stop=False)
                            last = mm(out, small[:, k, :], bl, start=False, stop=en)
                        else:
                            c = slice(t * P, (t + 1) * P)
                            mm(out, hi[:, k, c], bh, start=st, stop=False)
                            mm(out, hi[:, k, c], bl, start=False, stop=False)
                            last = mm(out, lo[:, k, c], bh, start=False, stop=en)
                        if en:
                            last.then_inc(z_done, 1)
                    if k < nk - 1:
                        last.then_inc(w_used, 1)

            def block_direct(name, small):
                f, nk, w, idx, n = FIRST[name], COUNT[name], WIDTH[name], ITEM[name], small.shape[2]
                wait_bank(idx)
                for k in range(nk):
                    j = f + k
                    pe.wait_ge(raw_in[j % NRAW], 16 * (j // NRAW + 1))
                    mm(ps[0:n, idx % BANKS, 0:w], small[:, k, :], raw[:, j % NRAW, 0:w], start=k == 0,
                       stop=k == nk - 1).then_inc(w_used if k < nk - 1 else z_done, 1)

            def transposes(idx, parts, n_in=P):
                wait_bank(idx)
                for col, rows_out_, src in parts:
                    last = nc.tensor.transpose(ps[0:rows_out_, idx % BANKS, col:col + n_in], src, ident[0:n_in, 0:n_in])
                last.then_inc(z_done, 1)

            def misc_transposes(parts, n_in):
                misc_begin()
                for col, rows_out_, src in parts:
                    last = nc.tensor.transpose(ps[0:rows_out_, 7, col:col + n_in], src, ident[0:n_in, 0:n_in])
                last.then_inc(misc_done, 1)

            pe.wait_ge(tab_in, 32)
            pe.wait_ge(csilu, 1)
            misc_transposes([(9 * k, P, c9b[0:9, k * P:(k + 1) * P]) for k in range(KD)], NB + 1)
            pe.wait_ge(cs_ready, 1)
            for n in range(2):
                block_direct(f"ada{n}", cs)
            pe.wait_ge(wuk_in, 16)
            for i in range(2):
                transposes(ITEM["wukT"] + i, [(2 * P * q + P * r, P, wukr[:, r, (2 * i + q) * P:(2 * i + q + 1) * P])
                                              for q in range(2) for r in range(2)])
            pe.wait_ge(xn_ready, 5)
            for k in range(KD):
                transposes(ITEM["xT"] + k, [(t * P, P, xt[:, t, k * P:(k + 1) * P]) for t in range(NT)])
            misc_transposes([(NB * k, P, xs1[:, k * P:(k + 1) * P]) for k in range(KD)], NB)
            for n in range(2, 6):
                block_direct(f"ada{n}", cs)
            pe.wait_ge(ada_ready, 6)
            misc_transposes([(9 * k, P, ada[:, k * P:(k + 1) * P]) for k in range(2 * KD)], NB + 1)
            for n in range(2):
                idx = ITEM["gate"] + n
                wait_bank(idx)
                mm(ps[:, idx % BANKS, :], ident[0:NB + 1, NB:NB + 1].to_broadcast([NB + 1, P]),
                   ada[:, 2 * D + n * 512:2 * D + (n + 1) * 512], start=True, stop=True).then_inc(z_done, 1)
            for name in ("Q", "KV"):
                block_of(name, ITEM[name], range(5), hThi, hTlo, hTs, wait_h=name == "Q")
            pe.wait_ge(qan_ready, 1)
            for c in range(3):
                transposes(ITEM["Tq"] + c, [(t * P, P, qan[:, t, c * P:(c + 1) * P]) for t in range(NT)])
            misc_transposes([(NB * c, P, qan[0:NB, TS, c * P:(c + 1) * P]) for c in range(3)], NB)
            wait_evac(pe, ITEM["Tq"] + 2)
            pe.wait_ge(smp_ready, SMP_Q)
            block_of("QB0", ITEM["QB0"], range(5), qaThi, qaTlo, qaTs)
            pe.wait_ge(rows_ready, 5)
            for c in range(2):
                transposes(ITEM["Tr"] + c, [(t * P, P, rows[:, t, c * P:(c + 1) * P]) for t in range(NT)])
            misc_transposes([(NB * c, P, rows[0:NB, TS, c * P:(c + 1) * P]) for c in range(2)], NB)
            wait_evac(pe, ITEM["Tr"] + 1)
            pe.wait_ge(smp_ready, SMP_R)
            for t in range(5):
                idx = ITEM["K"] + t
                wait_bank(idx)
                for k in range(2):
                    if t == TS:
                        pairs = [(rTs[:, k, :], wuk_hi[:, k, :]), (rTs[:, k, :], wuk_lo[:, k, :])]
                    else:
                        c = slice(t * P, (t + 1) * P)
                        pairs = [(rThi[:, k, c], wuk_hi[:, k, :]), (rThi[:, k, c], wuk_lo[:, k, :]),
                                 (rTlo[:, k, c], wuk_hi[:, k, :])]
                    for m, (a, b) in enumerate(pairs):
                        last = mm(ps[:, idx % BANKS, :].rearrange("p (f n) -> p f n", f=2), a, b, start=k == 0 and m == 0,
                                  stop=k == 1 and m == len(pairs) - 1)
                last.then_inc(z_done, 1)
            block_of("V", ITEM["V"], range(NT), rThi, rTlo)
            block_of("QB1", ITEM["QB1"], range(5), qaThi, qaTlo, qaTs)
            for t in range(NT):
                pe.wait_ge(kc_ready, t + 1)
                for i in range(2):
                    transposes(ITEM["TkM"] + 2 * t + i,
                               [(m * P, QK, kc[:, t, (4 * i + m) * QK:(4 * i + m + 1) * QK]) for m in range(4)])
            for i in range(2):
                for t in range(NT):
                    pe.wait_ge((qh0_ready, qh1_ready)[i], t + 1)
                    transposes(ITEM["TqM"] + i * NT + t,
                               [(m * P, QK, qh[:, i * NT + t, m * QK:(m + 1) * QK]) for m in range(4)])
            pe.wait_ge(qh0_ready, 5)
            pe.wait_ge(qh1_ready, 5)
            misc_begin()
            for p in range(4):
                nc.tensor.transpose(ps[:, 7, NB * p:NB * p + NB],
                                    qn_s[:, p * P:(p + 1) * P],
                                    ident[0:NB, 0:NB])
            for h in range(HM):
                last = nc.tensor.transpose(ps[0:ROPE, 7, 32 + NB * h:32 + NB * h + NB],
                                           q_s[:, h * QK + NOPE:(h + 1) * QK], ident[0:NB, 0:NB])
            last.then_inc(misc_done, 1)
            misc_begin()
            for odd in range(2):
                o = 64 * odd
                for c in range(2):
                    for h in range(odd, HM, 2):
                        last = mm(ps[:, 7, c * 64 + h * NB:c * 64 + (h + 1) * NB],
                                  wukT[o:o + 64, h // 2, c * P:(c + 1) * P],
                                  qsT[o:o + 64, h // 2 * NB:(h // 2 + 1) * NB], start=True, stop=True)
                if odd == 0:
                    last.then_inc(even_done, 1)
                    pe.wait_ge(even_done, 1)
            last.then_inc(misc_done, 1)

            def attention(jobs, n0, c0, first_idx, slots, outs, scores, values):
                wait_evac(pe, first_idx)
                pe.wait_ge(misc_free, miscs[0])
                end = n0 + len(jobs)

                def qk(n):
                    if n - n0 >= slots:
                        pe.wait_ge(masked, n - slots + 1)
                    scores(jobs[n - n0], n).then_inc(qk_done, 1)

                chunks = [(n, m, w) for n in range(n0, end) for m, w in enumerate(widths(jobs[n - n0][2]))]

                def tr(k):
                    n, m, w = chunks[k]
                    c = c0 + k
                    if m == 0:
                        pe.wait_ge(exp_done, n + 1)
                    if k >= 2:
                        wait_pt(pe, c - 2)
                    for q in range(w):
                        last = nc.tensor.transpose(ps[:, 6 + c % 2, q * P:(q + 1) * P],
                                                   Pm[slots][:, n % slots, (4 * m + q) * P:(4 * m + q + 1) * P], ident)
                    last.then_inc(trp_done, 1)

                for n in range(n0, n0 + slots):
                    qk(n)
                tr(0)
                for k, (n, m, w) in enumerate(chunks):
                    if k + 1 < len(chunks):
                        tr(k + 1)
                    out, vals = values(jobs[n - n0], n)
                    if m == 0 and n + slots < end:
                        qk(n + slots)
                    if m == 0 and n - n0 >= outs:
                        pe.wait_ge(o_done, n - outs + 1)
                    c = c0 + k
                    wait_pt(pe, c)
                    for q in range(w):
                        b = 4 * m + q
                        last = mm(out, PT[:, c % 3, q * P:(q + 1) * P], vals[b], start=b == 0, stop=b == len(vals) - 1)
                    last.then_inc(pv_chunk, 1)
                pe.wait_ge(o_done, end)

            def mla_scores(job, n):
                i, h, nb = job
                return mm(ps[:, n % 4, 0:nb * P], qTm[:, h, i * P:(i + 1) * P], kTm[:, h, 0:nb * P],
                          start=True, stop=True)

            def mla_values(job, n):
                i, h, nb = job
                return ps[:, 4 + n % 2, 0:64], [vm[:, b, h * 64:(h + 1) * 64] for b in range(nb)]

            attention(MLA_JOBS, 0, 0, LAST_ITEM["TqM"], 4, 2, mla_scores, mla_values)
            for g in range(ND):
                block_of(f"D{g}QK", ITEM[f"D{g}QK"], range(5), hThi, hTlo, hTs)
                block_of(f"D{g}V", ITEM[f"D{g}V"], range(5), hThi, hTlo, hTs)
            for i in range(4 * ND):
                g, is_k, p = i // 4, i // 2 % 2, i % 2
                pe.wait_ge(rope_done, 5 * g + NT)
                transposes(ITEM["TD"] + i,
                           [(t * P, P, (kvo if is_k else dqn)[:, g, t, p * P:(p + 1) * P]) for t in range(NT)])

            def dil_scores(job, n):
                i, h, nb = job
                r = slice(64 * (h % 2), 64 * (h % 2) + 64)
                for g in (1, 2, 0):
                    lo = max(0, i - 1) if g == 0 else 0
                    if g == 0 and n > len(MLA_JOBS):
                        pe.wait_ge(masked, n)
                    bank, c = (2 * (n % 2) + g - 1, 0) if g else (4, 256 * (n % 2))
                    last = mm(ps[:, bank, c:c + (i + 1 - lo) * P], dqT[r, g, h // 2, i * P:(i + 1) * P],
                              dkT[r, g, h // 2, lo * P:(i + 1) * P], start=True, stop=True)
                return last

            def dil_values(job, n):
                i, h, nb = job
                blocks = [(g, b) for g in range(ND) for b in range(max(0, i - 1) if g == 0 else 0, i + 1)]
                return ps[:, 5, 0:64], [kvo[:, g, b, BW + h * 64:BW + (h + 1) * 64] for g, b in blocks]

            attention(DIL_JOBS, len(MLA_JOBS), N_MLA_CHUNKS, LAST_ITEM["TD"], 2, 1, dil_scores, dil_values)
            for name in ("GA", "GB"):
                block_of(name, ITEM[name], range(5), hThi, hTlo, hTs)
            pe.wait_ge(gated, 2 * NT)
            for c in range(6):
                transposes(ITEM["To"] + c, [(t * P, P, oN[:, t, c * P:(c + 1) * P]) for t in range(NT)])
            wait_evac(pe, ITEM["To"] + 5)
            for n in range(2):
                block_of(f"PA{n}", ITEM[f"PA{n}"], range(NT), oThi, oTlo)
                block_of(f"PB{n}", ITEM[f"PB{n}"], range(NT), oThi[:, 4:6, :], oTlo[:, 4:6, :])
            for n in range(2):
                for b in "AB":
                    block_of(f"M{b}{n}", ITEM[f"M{b}{n}"], range(5), hThi, hTlo, hTs)
            pe.wait_ge(merged, 2 * NT)
            for k in range(KD):
                transposes(ITEM["Tm"] + k, [(t * P, P, ya[:, t, k * P:(k + 1) * P]) for t in range(NT)])
            wait_evac(pe, ITEM["Tm"] + KD - 1)
            for n in range(2):
                block_of(f"WO{n}", ITEM[f"WO{n}"], range(NT), hThi, hTlo)
            wait_evac(pe, LAST_ITEM["WO1"])

            def group_in(b, g, p, turn):
                G = 8 * b + g
                if g % 2 == 0:
                    pe.wait_ge(cn_in[p][g // 2], 128 * turn + 128)
                if not (isinstance(G, int) and G == 0):
                    pe.wait_ge(ct_ready, G)
                if not (isinstance(G, int) and G < 2):
                    pe.wait_ge(s_read, G - 1)
                for u in range(4):
                    src = cn[p][:, 4 * g + u, :]
                    for c in range(2):
                        nc.tensor.transpose(ps[:, c, u * P:(u + 1) * P], src[:, c * P:(c + 1) * P], ident)
                pe.wait_ge(kpn_ready, G + 1)
                nc.tensor.transpose(ps[:, 2, 0:P], kpn[:, g % 2, :], ident).then_inc(ct_done, 1)

            def group_products(b, g, p, last_group):
                w = slice(4 * p, 4 * p + 260)
                G = 8 * b + g
                q = g % 2
                pe.wait_ge(ct_ready, G + 1)
                for u in range(4):
                    U = 4 * G + u
                    if not (isinstance(U, int) and U < 2):
                        pe.wait_ge(sq_done, U - 1)
                    hi = [cThi[:, q, c * 512 + u * P:c * 512 + (u + 1) * P] for c in range(2)]
                    lo = [cTlo[:, q, c * 512 + u * P:c * 512 + (u + 1) * P] for c in range(2)]
                    for c in range(2):
                        for a, wq in ((hi, wq_hi), (hi, wq_lo), (lo, wq_hi)):
                            for f in range(2):
                                last = mm(ps[:, 3 + 2 * (u % 2) + f, 0:260], a[c], wq[:, c, f, w],
                                          start=c == 0 and a is hi and wq is wq_hi, stop=c == 1 and a is lo)
                    last.then_inc(k_done, 1)
                    if u == 2:
                        if last_group:
                            pe.wait_ge(s_read, G)
                        else:
                            pe.wait_ge(ct_ready, G + 2)
                        mm(ps[:, 2, P:P + 32], kpT[:, q, :], qpe[:, bass.ds(32 * b, 32)], start=True, stop=True)\
                            .then_inc(s_done, 1)

            def softmax_max(b):
                pe.wait_ge(pm_ready, b + 1)
                nc.tensor.transpose(ps[0:HM, 7, 0:P], pmx[:, :], ident).then_inc(pmT_done, 1)

            def softmax_spread(b):
                pe.wait_ge(dg_ready, b + 1)
                mm(ps[:, 7, P:P + HM], ones[0:HM, :], dgm[0:HM, 0:HM], start=True, stop=True).then_inc(mx_done, 1)

            def weighted_sum(b, p, spread=False):
                pe.wait_ge(es_ready, b + 1)
                mm(ps[0:HM, 7, P + 8:P + 9], esm[:, :], ones[:, 0:1], start=True, stop=True)
                if not (isinstance(b, int) and b == 0):
                    pe.wait_ge(lat_done, b)
                for t in range(NPAGE):
                    mm(ps[0:HM, 7, 256:512], Ex[:, t, :], cn[p][:, t, 0:KVR], start=t == 0, stop=False)
                    if spread and t % 5 == 4:
                        spread_q(2 + t // 5)
                mm(ps[0:HM, 7, 256:512], Ex[0:NB, NPAGE, :], rows[0:NB, TS, 0:KVR], start=False, stop=True)\
                    .then_inc(pv_done, 1)

            def spread_q(b):
                if b >= 2:
                    pe.wait_ge(qb_read, b - 1)
                for g in range(ND):
                    q0 = (1 + 2 * (b % 2)) * 512 + g * BW
                    last = mm(psw(0, 8 * 512)[:, q0:q0 + BW], ident[0:NB, b:b + 1].to_broadcast([NB, P]),
                              dq_s[:, g, :], start=True, stop=True)
                last.then_inc(qb_done, 1)

            def batch(b, p, turn, next_turn, first, last):
                if first:
                    group_in(b, 0, p, turn)
                for g in range(8):
                    if g < 7:
                        group_in(b, g + 1, p, turn)
                    elif not last:
                        group_in(b + 1, 0, 1 - p, next_turn)
                    group_products(b, g, p, last and g == 7)
                    if not first:
                        if g == 2:
                            softmax_max(b - 1)
                        elif g == 3:
                            softmax_spread(b - 1)
                        elif g == 4:
                            weighted_sum(b - 1, 1 - p)

            batch(0, 0, 0, 0, True, False)
            with pe.Fori(0, (NB - 2) // 2) as i:
                batch(2 * i + 1, 1, i, i + 1, False, False)
                batch(2 * i + 2, 0, i + 1, i + 1, False, False)
            batch(NB - 1, 1, (NB - 1) // 2, 0, False, True)
            softmax_max(NB - 1)
            softmax_spread(NB - 1)
            pe.wait_ge(s_read, NB * 8)
            pe.wait_ge(sq_done, NB * NPAGE)
            spread_q(0)
            spread_q(1)
            weighted_sum(NB - 1, 1, spread=True)
            pe.wait_ge(lat_done, NB)
            for b in range(NB):
                for c in range(2):
                    o = (2 * b + c) * NB
                    last = nc.tensor.transpose(ps[:, 7, o:o + NB], lat_h[:, b * KVR + c * P:b * KVR + (c + 1) * P],
                                               ident[0:NB, 0:NB])
            last.then_inc(lt_done, 1)
            pe.wait_ge(wuv_in, 16)
            pe.wait_ge(lt_ready, 1)
            lat = latT[:, :].rearrange("p (b c h) -> p b c h", b=NB, c=2)
            for h in range(HM):
                for c in range(2):
                    last = mm(ps[0:NB, 0, h * 64:(h + 1) * 64], lat[:, :, c, h], wuvr[:, c, h * 64:(h + 1) * 64],
                              start=c == 0, stop=c == 1)
            last.then_inc(f_pe, 1)
            pe.wait_ge(f_dve, F_MAX)
            nc.tensor.transpose(ps[0:32, 5, 0:P], dpm[:, :], ident).then_inc(f_pe, 1)
            pe.wait_ge(f_dve, F_DIAG)
            mm(ps[:, 5, 128:160], ones[0:32, :], dgm[:, :], start=True, stop=True).then_inc(f_pe, 1)
            pe.wait_ge(f_dve, F_SUM)
            mm(ps[0:32, 5, 160:161], dsm[:, :], ones[:, 0:1], start=True, stop=True).then_inc(f_pe, 1)
            for b in range(NB):
                for g in range(ND):
                    kv = (sdk0 if b < 6 else sdk1)[:, (b if b < 6 else b - 6) * ND + g, BW:2 * BW]
                    mm(ps[0:32, 6, 0:BW], EZ_t[:, (b * ND + g) * 32:(b * ND + g + 1) * 32], kv,
                       start=b == 0 and g == 0, stop=False)
            for g in range(ND):
                last = mm(ps[0:32, 6, 0:BW], own_ed[:, g, :], kv_s[:, g, BW:2 * BW], start=False, stop=g == ND - 1)
            last.then_inc(f_pe, 1)
            pe.wait_ge(f_dve, F_OBT)
            mm(ps[0:NB, 7, 0:BW], sample_of, ob[:, :], start=True, stop=True).then_inc(f_pe, 1)
            pe.wait_ge(f_dve, F_OG)
            for c in range(6):
                last = nc.tensor.transpose(ps[:, 7, 256 + NB * c:256 + NB * (c + 1)], og[:, c * P:(c + 1) * P],
                                           ident[0:NB, 0:NB])
            last.then_inc(f_pe, 1)
            pe.wait_ge(f_dve, F_OST)
            for n in range(2):
                block_direct(f"PAs{n}", osT)
                block_direct(f"PBs{n}", osT[:, 4:6, :])
            pe.wait_ge(f_dve, F_MS)
            for c in range(KD):
                last = nc.tensor.transpose(ps[:, 7, 320 + NB * c:320 + NB * (c + 1)], yab[:, 0, c * P:(c + 1) * P],
                                           ident[0:NB, 0:NB])
            last.then_inc(f_pe, 1)
            pe.wait_ge(f_dve, F_MST)
            for n in range(2):
                block_direct(f"WOs{n}", msT)

        @block.vector
        def _(dve):
            v = nc.vector
            steps = [0]
            staged = [0]
            freed = [0]
            added = [0]
            miscs = [0]
            fcount = [0]

            def link(ins):
                steps[0] += 1
                ins.then_inc(dve_step, 1)
                dve.wait_ge(dve_step, steps[0])

            def rsqrt_seed(x, a, y, step):
                step(v.tensor_scalar(out=a.bitcast(I32), in0=x.bitcast(I32), scalar1=1, scalar2=None,
                                     op0=ALU.logical_shift_right))
                step(v.tensor_scalar(out=y.bitcast(I32), in0=a.bitcast(I32), scalar1=-1.0, scalar2=RSQRT_MAGIC,
                                     op0=ALU.mult, op1=ALU.add))

            def rsqrt_newton(x, a, y, step):
                step(v.tensor_tensor(out=a, in0=y, in1=y, op=ALU.mult))
                step(v.scalar_tensor_tensor(out=a, in0=a, scalar=-0.5, in1=x, op0=ALU.mult, op1=ALU.mult))
                step(v.scalar_tensor_tensor(out=y, in0=a, scalar=1.5, in1=y, op0=ALU.add, op1=ALU.mult))

            def rsqrt(x, a, y, step):
                rsqrt_seed(x, a, y, step)
                for _ in range(3):
                    rsqrt_newton(x, a, y, step)

            def inv_rms(cols_, *scales):
                w = cols_ // len(scales)
                for m, scale in enumerate(scales):
                    last = v.tensor_scalar(out=rsx[:, m * w:(m + 1) * w], in0=ms[:, m * w:(m + 1) * w], scalar1=scale,
                                           scalar2=EPS, op0=ALU.mult, op1=ALU.add)
                link(last)
                rsqrt(rsx[:, 0:cols_], rsa[:, 0:cols_], rsy[:, 0:cols_], link)

            def take(idx, n, w, small):
                wait_evac(dve, idx)
                z = stage[0:n, staged[0] % NSTAGE, 0:w]
                staged[0] += 1
                if small:
                    added[0] += 1
                    v.tensor_tensor(out=z, in0=z, in1=low_s[0:n, 0:w], op=ALU.add).then_inc(low_added, 1)
                    dve.wait_ge(low_added, added[0])
                return z

            def free_stage(ins):
                ins.then_inc(stage_free, 1)
                freed[0] += 1
                dve.wait_ge(stage_free, freed[0])

            def mean_square(z, w, col):
                n = z.shape[0]
                link(v.tensor_tensor_reduce(out=sqt[0:n, 0:w], in0=z, in1=z, scale=1.0 / w, scalar=0.0,
                                            op0=ALU.mult, op1=ALU.add, accum_out=ms[0:n, col:col + 1]))

            def rotate(x, out, sin_cos, heads):
                n = x.shape[0]
                a = pe1[0:n, 0:heads * ROPE].rearrange("p (h e) -> p h e", e=ROPE)
                b = pe2[0:n, 0:heads * ROPE].rearrange("p (h e) -> p h e", e=ROPE)
                v.tensor_tensor(out=a, in0=x, in1=rep(sin_cos[:, 0:32], 1, heads), op=ALU.mult)
                v.tensor_tensor(out=b[:, :, 0:16], in0=x[:, :, 16:32], in1=rep(sin_cos[:, 32:48], 1, heads), op=ALU.mult)
                link(v.tensor_tensor(out=b[:, :, 16:32], in0=x[:, :, 0:16], in1=rep(sin_cos[:, 48:64], 1, heads),
                                     op=ALU.mult))
                return v.tensor_tensor(out=out, in0=a, in1=b, op=ALU.add)

            def misc_wait():
                miscs[0] += 1
                dve.wait_ge(misc_done, miscs[0])

            def misc_read(ins):
                ins.then_inc(misc_free, 1)
                dve.wait_ge(misc_free, miscs[0])

            def split_small(src, dst, count, n=NB):
                link(v.tensor_copy(dst[:, 0:count, 0:n], src))
                return v.tensor_tensor(out=dst[:, 0:count, LO:LO + n], in0=src,
                                       in1=dst[:, 0:count, 0:n].bitcast(F32), op=ALU.subtract)

            def low_half(idx, out, hi, scale=None):
                dve.wait_ge(act_half, READER[idx][1])
                src = ps[:, idx % BANKS, :]
                if scale is None:
                    ins = v.tensor_tensor(out=out, in0=src, in1=hi.bitcast(F32), op=ALU.subtract)
                else:
                    ins = v.scalar_tensor_tensor(out=out, in0=src, scalar=scale, in1=hi.bitcast(F32), op0=ALU.mult,
                                                 op1=ALU.subtract)
                ins.then_inc(evac_d, 1)

            dve.wait_ge(sigm_c, 1)
            v.tensor_tensor(out=c9b[:, :], in0=c9[:, :], in1=c9b[:, :], op=ALU.mult).then_inc(csilu, 1)
            dve.wait_ge(zeroed, 2)
            misc_wait()
            misc_read(v.tensor_copy(cs[:, :, :], ps[:, 7, 0:72].rearrange("p (k n) -> p k n", n=9)))
            v.memset(flag[:, :], 0.0).then_inc(cs_ready, 1)
            dve.wait_ge(wuk_h, 1)
            v.tensor_tensor(out=wuk_lo, in0=wukr[:, :, :].rearrange("p c (f n) -> p c f n", f=2),
                            in1=wuk_hi.bitcast(F32), op=ALU.subtract)\
             .then_inc(wuk_split, 1)

            def ada_item(n):
                z = take(ITEM[f"ada{n}"], NB + 1, 512, False)
                if n == 0:
                    dve.wait_ge(bada_in, 16)
                free_stage(v.tensor_tensor(out=ada[:, n * 512:(n + 1) * 512], in0=z,
                                           in1=bada[:, n * 512:(n + 1) * 512], op=ALU.add))
                if n >= 4:
                    v.tensor_copy(gate_s[:, (n - 4) * 512:(n - 3) * 512], ada[0:NB, n * 512:(n + 1) * 512])\
                     .then_inc(ada_ready, 1)
                else:
                    v.memset(flag[:, :], 0.0).then_inc(ada_ready, 1)

            link(v.memset(ms[:, :], 1.0))
            for t in range(5):
                n = lanes(t)
                x = xs1[:, :] if t == TS else xt[:, t, :]
                dve.wait_ge(x_in[t], 16)
                link(v.tensor_tensor_reduce(out=xsq[0:n, :], in0=x, in1=x, scale=1.0 / D, scalar=0.0,
                                            op0=ALU.mult, op1=ALU.add, accum_out=ms[0:n, t:t + 1]))
            inv_rms(5, 1.0)
            for t in range(5):
                n = lanes(t)
                x = xs1[:, :] if t == TS else xt[:, t, :]
                v.tensor_scalar(out=x, in0=x, scalar1=rsy[0:n, t:t + 1], scalar2=None, op0=ALU.mult)\
                 .then_inc(xn_ready, 1)
            for n in range(2):
                ada_item(n)
            misc_wait()
            misc_read(v.tensor_copy(xTs[:, :], ps[:, 7, 0:64]))
            for n in range(2, 6):
                ada_item(n)
            misc_wait()
            adaT = ps[:, 7, 0:144].rearrange("p (k n) -> p k n", n=9)
            dve.wait_ge(tab_in, 32)
            dve.wait_ge(consts_in, 48)
            v.scalar_tensor_tensor(out=G1[:, :, :], in0=adaT[:, KD:2 * KD, :], scalar=1.0,
                                   in1=rep(colt[:, 0:KD], 2, 9), op0=ALU.add, op1=ALU.mult)
            misc_read(v.tensor_copy(SH[:, :, :], adaT[:, 0:KD, :]))
            xTs3 = xTs[:, :].rearrange("p (k n) -> p k n", n=NB)
            link(v.tensor_tensor(out=hs_f[:, :, :], in0=xTs3, in1=G1[:, :, 0:NB], op=ALU.mult))
            link(v.tensor_tensor(out=hs_f[:, :, :], in0=hs_f[:, :, :], in1=SH[:, :, 0:NB], op=ALU.add))
            split_small(hs_f[:, :, :], hTs, KD).then_inc(h_ready, 1)

            def low_h(k):
                dve.wait_ge(h_hi, k + 1)
                v.tensor_tensor(out=hTlo[:, k, :], in0=xT[:, k, :], in1=hThi[:, k, :].bitcast(F32), op=ALU.subtract)\
                 .then_inc(h_ready, 1)

            for k in range(KD):
                wait_evac(dve, ITEM["xT"] + k)
                v.tensor_scalar(out=xT[:, k, :], in0=xT[:, k, :], scalar1=G1[:, k, NB:NB + 1],
                                scalar2=SH[:, k, NB:NB + 1], op0=ALU.mult, op1=ALU.add).then_inc(h_f, 1)
                if k:
                    low_h(k - 1)
            low_h(KD - 1)
            v.tensor_tensor(out=g96[:, 0:NOPE], in0=gn[:, G_QN:G_QN + 64], in1=gn[:, G_KN:G_KN + 64], op=ALU.mult)
            link(v.tensor_copy(g96[:, NOPE:QK], gn[:, G_QR:G_QR + 32]))
            zs = []
            for t in range(5):
                zs.append(take(ITEM["Q"] + t, lanes(t), QR, t == TS))
                mean_square(zs[t], QR, t)
            inv_rms(5, 1.0)
            for t in range(5):
                n = lanes(t)
                free_stage(v.tensor_scalar(out=qan[0:n, t, :], in0=zs[t], scalar1=rsy[0:n, t:t + 1], scalar2=None,
                                           op0=ALU.mult))
            v.memset(flag[:, :], 0.0).then_inc(qan_ready, 1)
            for c in range(3):
                low_half(ITEM["Tq"] + c, qaTlo[:, c, :], qaThi[:, c, :], colt[:, KD + c:KD + c + 1])
            dve.wait_ge(zeroed, 4)
            misc_wait()
            qaf = pe1[:, 0:24].rearrange("p (k n) -> p k n", n=NB)
            misc_read(v.tensor_tensor(out=qaf, in0=ps[:, 7, 0:24].rearrange("p (k n) -> p k n", n=NB),
                                      in1=rep(colt[:, KD:KD + 3], 2, NB), op=ALU.mult))
            split_small(qaf, qaTs, 3).then_inc(smp_ready, 1)
            zs = []
            for t in range(5):
                zs.append(take(ITEM["KV"] + t, lanes(t), CW, t == TS))
                mean_square(zs[t][:, 0:KVR], KVR, t)
                mean_square(zs[t][:, KVR:CW], ROPE, 5 + t)
            inv_rms(10, 1.0)
            for t in range(5):
                n, z = lanes(t), zs[t]
                v.scalar_tensor_tensor(out=rows[0:n, t, 0:KVR], in0=z[:, 0:KVR], scalar=rsy[0:n, t:t + 1],
                                       in1=gn[0:n, G_KV:G_KV + KVR], op0=ALU.mult, op1=ALU.mult)
                free_stage(v.scalar_tensor_tensor(out=rows[0:n, t, KVR:CW], in0=z[:, KVR:CW],
                                                  scalar=rsy[0:n, 5 + t:6 + t], in1=gn[0:n, G_KR:G_KR + ROPE],
                                                  op0=ALU.mult, op1=ALU.mult))
                kp = rows[0:n, t, KVR:CW].unsqueeze(1)
                rotate(kp, kp, ropes[0:n, t, 128:192], 1).then_inc(rows_ready, 1)
                dve.wait_ge(rows_ready, t + 1)

            def q_squares(i, t):
                n = lanes(t)
                z = take(ITEM[f"QB{i}"] + t, n, 384, t == TS)
                z3 = z.rearrange("p (h e) -> p h e", e=QK)
                sq3 = sqt[0:n, 0:384].rearrange("p (h e) -> p h e", e=QK)
                link(v.tensor_tensor(out=sq3, in0=z3, in1=z3, op=ALU.mult))
                v.tensor_reduce(out=ms[0:n, 4 * t:4 * t + 4], in_=sq3[:, :, 0:NOPE], axis=AX, op=ALU.add)
                link(v.tensor_reduce(out=ms[0:n, 20 + 4 * t:24 + 4 * t], in_=sq3[:, :, NOPE:QK], axis=AX, op=ALU.add))
                return z3

            def q_item(i, t, z3):
                n = lanes(t)
                o3 = q_heads(i, t)
                v.tensor_tensor(out=o3[:, :, 0:NOPE], in0=z3[:, :, 0:NOPE], in1=rep(rsy[0:n, 4 * t:4 * t + 4], 2, NOPE),
                                op=ALU.mult)
                free_stage(v.tensor_tensor(out=o3[:, :, NOPE:QK], in0=z3[:, :, NOPE:QK],
                                           in1=rep(rsy[0:n, 20 + 4 * t:24 + 4 * t], 2, ROPE), op=ALU.mult))
                if i == 1:
                    link(v.tensor_tensor(out=o3, in0=o3, in1=rep(g96[0:n, :], 1, 4), op=ALU.mult))
                    if t == TS:
                        v.tensor_copy(qn_s[:, 256:512].rearrange("p (h e) -> p h e", e=NOPE), o3[:, :, 0:NOPE])
                    rotate(o3[:, :, NOPE:QK], o3[:, :, NOPE:QK], ropes[0:n, t, 128:192], 4).then_inc(qh1_ready, 1)
                    dve.wait_ge(qh1_ready, t + 1)

            def q_block(i):
                zs = [q_squares(i, t) for t in range(5)]
                inv_rms(40, 1.0 / NOPE, 1.0 / ROPE)
                for t in range(5):
                    q_item(i, t, zs[t])

            for c in range(2):
                low_half(ITEM["Tr"] + c, rTlo[:, c, :], rThi[:, c, :])
            misc_wait()
            rf = pe1[:, 0:16].rearrange("p (k n) -> p k n", n=NB)
            misc_read(v.tensor_copy(rf, ps[:, 7, 0:16].rearrange("p (k n) -> p k n", n=NB)))
            split_small(rf, rTs, 2).then_inc(smp_ready, 1)
            q_block(0)

            def head_squares(name, t):
                n = lanes(t)
                z = take(ITEM[name] + t, n, 512, t == TS)
                link(v.tensor_tensor(out=sqt[0:n, :], in0=z, in1=z, op=ALU.mult))
                link(v.tensor_reduce(out=ms[0:n, 8 * t:8 * t + 8], in_=sqt[0:n, :].rearrange("p (h e) -> p h e", e=64),
                                     axis=AX, op=ALU.add))
                return z.rearrange("p (h e) -> p h e", e=64)

            zs = [head_squares("K", t) for t in range(5)]
            inv_rms(40, 1.0 / NOPE)
            for t in range(5):
                n, z3 = lanes(t), zs[t]
                out = (k_s[:, :] if t == TS else kc[:, t, :]).rearrange("p (h e) -> p h e", e=QK)
                free_stage(v.tensor_tensor(out=out[:, :, 0:NOPE], in0=z3, in1=rep(rsy[0:n, 8 * t:8 * t + 8], 2, NOPE),
                                           op=ALU.mult))
                v.tensor_copy(out[:, :, NOPE:QK], rep(rows[0:n, t, KVR:CW], 1, HM)).then_inc(kc_ready, 1)
            q_block(1)
            misc_wait()
            v.tensor_copy(qsT[:, :], ps[:, 7, 0:32])
            link(v.memset(qpe[:, :], 0.0))
            for u in range(4):
                last = v.tensor_copy(qpe[32 * u:32 * u + 32, :].rearrange("p (b u h) -> p u h b", b=NB, u=4)[:, u],
                                     ps[0:ROPE, 7, 32:96].rearrange("p (h b) -> p h b", b=NB))
            misc_read(last)
            misc_wait()
            misc_read(v.tensor_copy(qabs[:, 0:NB * 16].rearrange("p (b c h) -> p c h b", c=2, b=NB),
                                    ps[:, 7, 0:128].rearrange("p (c h b) -> p c h b", c=2, b=NB)))
            link(v.memset(qabs[:, NB * 16:(NB + 1) * 16], 0.0))

            def set_q(b, p, step):
                q3 = qabs[:, bass.ds(16 * b, 16)].rearrange("p (c f h) -> p c f h", c=2, f=2)
                cols_ = slice(260 * p, 260 * p + 4)
                step(v.tensor_copy(wq_hi[:, :, :, cols_], q3))
                return v.tensor_tensor(out=wq_lo[:, :, :, cols_], in0=q3, in1=wq_hi[:, :, :, cols_].bitcast(F32),
                                       op=ALU.subtract)

            for b in range(2):
                link(set_q(b, b, link))
            dve.wait_ge(kc_ready, 5)
            own = tmp_t[0:NB, 1792:2560]
            link(v.tensor_tensor(out=own, in0=q_s[:, :], in1=k_s[:, :], op=ALU.mult))
            link(v.tensor_reduce(out=dns[:, :], in_=own.rearrange("p (h e) -> p h e", e=QK), axis=AX, op=ALU.add))
            link(v.tensor_tensor(out=snew[:, :].rearrange("p (b h) -> p b h", b=NB), in0=rep(dns[:, :], 1, NB),
                                 in1=rep(newmask, 2, HM), op=ALU.add))

            def attention(jobs, n0, c0, slots, ahead, mask, place, scale):
                def masks_max(n):
                    s = n % slots
                    dve.wait_ge(qk_done, n + 1)
                    if n - n0 >= slots:
                        dve.wait_ge(trp_done, CHUNK_END[n - slots])
                    a = amax[:, 4 * s:4 * s + 4]
                    parts = mask(jobs[n - n0], n, Pm[slots][:, s, :])
                    for m, (out, src, msk) in enumerate(parts):
                        link(v.tensor_tensor_reduce(out=out, in0=src, in1=msk, scale=1.0,
                                                    scalar=NEG if m == 0 else a[:, 0:1], op0=ALU.add, op1=ALU.max,
                                                    accum_out=a[:, m:m + 1]))
                    m = len(parts) - 1
                    v.tensor_scalar(out=a[:, 2:3], in0=a[:, m:m + 1], scalar1=-scale, scalar2=None, op0=ALU.mult)\
                     .then_inc(masked, 1)

                chunk = c0
                for n in range(n0, n0 + ahead):
                    masks_max(n)
                def finish(n):
                    s = n % 4
                    dve.wait_ge(exp_done, n + 1)
                    link(v.reciprocal(lsum[:, 4 + s:5 + s], lsum[:, s:s + 1]))
                    dve.wait_ge(pv_chunk, CHUNK_END[n])
                    out, src = place(jobs[n - n0], n)
                    v.tensor_scalar(out=out, in0=src, scalar1=lsum[:, 4 + s:5 + s], scalar2=None, op0=ALU.mult)\
                     .then_inc(o_done, 1)

                for n in range(n0, n0 + len(jobs)):
                    if n + ahead < n0 + len(jobs):
                        masks_max(n + ahead)
                    for m, w in enumerate(widths(jobs[n - n0][2])):
                        if chunk % 2 == 0:
                            pt_copy(dve, v.tensor_copy, chunk, w, pt_d, ())
                        chunk += 1
                        if m == 0 and n > n0:
                            finish(n - 1)
                finish(n0 + len(jobs) - 1)

            def mla_mask(job, n, p):
                w = job[2] * P
                return [(p[:, 0:w], ps[:, n % 4, 0:w], masks[:, M_R4 - w:M_R4])]

            def mla_place(job, n):
                i, h, nb = job
                return oN[:, i, h * 64:(h + 1) * 64], ps[:, 4 + n % 2, 0:64]

            dve.wait_ge(z_done, LAST_ITEM["TqM"] + 1)
            attention(MLA_JOBS, 0, 0, 4, 2, mla_mask, mla_place, MLA_SCALE)
            for g in range(ND):
                zs = [head_squares(f"D{g}QK", t) for t in range(5)]
                inv_rms(40, 1.0 / DH)
                for t in range(5):
                    c = 5 * g + t
                    n, z3 = lanes(t), zs[t]
                    y = tmp[0:n, c % 2, :]
                    if c >= 2:
                        dve.wait_ge(rope_done, c - 1)
                    free_stage(v.tensor_tensor(out=y.rearrange("p (h e) -> p h e", e=DH), in0=z3,
                                               in1=rep(rsy[0:n, 8 * t:8 * t + 8], 2, DH), op=ALU.mult))
                    for m, o in enumerate((G_DQ, G_DK)):
                        yh = y[:, m * BW:(m + 1) * BW].rearrange("p (h e) -> p h e", e=DH)
                        last = v.tensor_tensor(out=yh, in0=yh, in1=rep(gn[0:n, o + g * DH:o + (g + 1) * DH], 1, HD),
                                               op=ALU.mult)
                    last.then_inc(y_roped, 1)
                    dve.wait_ge(y_roped, 2 * c + 1)
                    if c >= 1:
                        dve.wait_ge(rope_done, c)
                    v.tensor_tensor(out=tmp[0:n, 2, :].rearrange("p (h e) -> p h e", e=DH),
                                    in0=y.rearrange("p (h e) -> p h e", e=DH),
                                    in1=rep(ropes[0:n, t, 0:64], 1, 2 * HD), op=ALU.mult).then_inc(y_roped, 1)
                wait_evac(dve, ITEM[f"D{g}V"] + TS)
                z = stage[0:NB, staged[0] % NSTAGE, 0:BW]
                staged[0] += 1
                free_stage(v.tensor_tensor(out=kv_s[:, g, BW:2 * BW], in0=z, in1=low_s[0:NB, 0:BW], op=ALU.add))
            dve.wait_ge(rope_done, 5 * ND)
            v.memset(flag[:, :], 0.0).then_inc(smp_ready, 1)

            def dil_mask(job, n, p):
                i = job[0]
                w0 = P if i == 0 else 2 * P
                w = (i + 1) * P
                both = masks[:, M_R4:M_R4 + 1024].rearrange("p (g c) -> p g c", g=2)[:, :, 512 - w:512]
                s = n % 2
                return [(p[:, 0:w0], ps[:, 4, 256 * s:256 * s + w0], masks[:, M_ALL - w0:M_ALL]),
                        (p[:, w0:w0 + 2 * w].rearrange("p (g c) -> p g c", g=2), ps[:, 2 * s:2 * s + 2, 0:w], both)]

            def dil_place(job, n):
                i, h, nb = job
                return oN[:, i, AW + h * 64:AW + (h + 1) * 64], ps[:, 5, 0:64]

            dve.wait_ge(z_done, LAST_ITEM["TD"] + 1)
            attention(DIL_JOBS, len(MLA_JOBS), N_MLA_CHUNKS, 2, 1, dil_mask, dil_place, DIL_SCALE)
            for name, c0, w in (("GA", 0, AW), ("GB", AW, BW)):
                for t in range(NT):
                    idx = ITEM[name] + t
                    dve.wait_ge(act_half, READER[idx][1])
                    sg = stage[:, staged[0] % NSTAGE, 0:w]
                    staged[0] += 1
                    v.tensor_tensor(out=sg, in0=sg, in1=ps[:, idx % BANKS, 0:w], op=ALU.mult).then_inc(evac_d, 1)
                    dve.wait_ge(evac_d, READER[idx][1])
                    free_stage(v.tensor_tensor(out=oN[:, t, c0:c0 + w], in0=oN[:, t, c0:c0 + w], in1=sg, op=ALU.mult))
                    v.memset(flag[:, :], 0.0).then_inc(gated, 1)
                wait_evac(dve, ITEM[name + "s"])
                z = stage[0:NB, staged[0] % NSTAGE, 0:w]
                staged[0] += 1
                free_stage(v.tensor_tensor(out=mix_s[:, c0:c0 + w], in0=z, in1=low_s[0:NB, 0:w], op=ALU.add))
            dve.wait_ge(win_out, 16 * 3)
            for c in range(6):
                low_half(ITEM["To"] + c, oTlo[:, c, :], oThi[:, c, :])
            for n in range(2):
                for b, y in (("A", ya), ("B", yb)):
                    for t in range(NT):
                        z = take(ITEM[f"M{b}{n}"] + t, P, 512, False)
                        yt = y[:, t, n * 512:(n + 1) * 512]
                        free_stage(v.tensor_tensor(out=yt, in0=yt, in1=z, op=ALU.mult))
                        if b == "B":
                            yt2 = ya[:, t, n * 512:(n + 1) * 512]
                            v.tensor_tensor(out=yt2, in0=yt2, in1=yt, op=ALU.add).then_inc(merged, 1)
                    idx = ITEM[f"M{b}{n}"] + TS
                    wait_evac(dve, idx)
                    z = stage[0:NB, staged[0] % NSTAGE, 0:512]
                    staged[0] += 1
                    c0 = (0 if b == "A" else D) + n * 512
                    free_stage(v.tensor_tensor(out=merge_s[:, c0:c0 + 512], in0=z, in1=low_s[0:NB, :], op=ALU.add))
            for k in range(KD):
                low_half(ITEM["Tm"] + k, hTlo[:, k, :], hThi[:, k, :])
            for n in range(2):
                dve.wait_ge(xr_in[n], 16)
                for t in range(NT):
                    z = take(ITEM[f"WO{n}"] + t, P, 512, False)
                    link(v.tensor_tensor(out=z, in0=z, in1=gate_bc[:, n * 512:(n + 1) * 512], op=ALU.mult))
                    free_stage(v.tensor_tensor(out=xr[n][:, t, :], in0=xr[n][:, t, :], in1=z, op=ALU.add))
                    v.memset(flag[:, :], 0.0).then_inc(y_rdy, 1)
            dve.wait_ge(z_done, LAST_ITEM["WO1"] + 1)
            dve.wait_ge(y_out[0], 16)
            v.memset(Sc[:, NPAGE, :], NEG)
            base = [0]
            within = [0]

            def lstep_link(ins):
                within[0] += 1
                ins.then_inc(lstep, 1)
                dve.wait_ge(lstep, base[0] + within[0])

            def lat_rows(G, q):
                dve.wait_ge(ct_hi, G + 1)
                v.tensor_tensor(out=cTlo[:, q % 2, :], in0=psw(0, 1024), in1=cThi[:, q % 2, :].bitcast(F32),
                                op=ALU.subtract)
                v.tensor_copy(kpT[:, q % 2, :], ps[:, 2, 0:P]).then_inc(ct_ready, 1)

            def half_scores(h, part):
                t0 = 16 * h
                if part == 0:
                    lstep_link(v.tensor_scalar(out=lx[:, :], in0=ssq[:, t0 * 8:t0 * 8 + 128], scalar1=1.0 / NOPE,
                                               scalar2=EPS, op0=ALU.mult, op1=ALU.add))
                    rsqrt_seed(lx[:, :], lax[:, :], ly[:, :], lstep_link)
                else:
                    rsqrt_newton(lx[:, :], lax[:, :], ly[:, :], lstep_link)
                if part < 3:
                    return
                s3 = Sc[:, t0:t0 + 16, :]
                lstep_link(v.tensor_tensor(out=s3, in0=Sq[:, t0:t0 + 16, :],
                                           in1=ly[:, :].rearrange("p (t h) -> p t h", h=8), op=ALU.mult))
                lstep_link(v.tensor_tensor(out=s3, in0=s3, in1=Sk[:, t0:t0 + 16, :], op=ALU.add))

            def softmax_diag(b):
                dve.wait_ge(pmT_done, b + 1)
                lstep_link(v.tensor_reduce(out=mx1[0:HM, :], in_=ps[0:HM, 7, 0:P], axis=AX, op=ALU.max))
                v.tensor_scalar(out=dgm[0:HM, 0:HM], in0=ident[0:HM, 0:HM], scalar1=mx1[0:HM, :], scalar2=None,
                                op0=ALU.mult).then_inc(dg_ready, 1)

            def softmax_shift(b):
                dve.wait_ge(mx_done, b + 1)
                v.tensor_tensor(out=Sc[:, :, :], in0=Sc[:, :, :], in1=rep(ps[:, 7, P:P + HM], 1, 33), op=ALU.subtract)\
                 .then_inc(sub_done, 1)

            def softmax_sum(b):
                dve.wait_ge(ex_done, b + 1)
                v.tensor_reduce(out=esm[:, :], in_=Ex[:, :, :].rearrange("p t h -> p h t"), axis=AX, op=ALU.add)\
                 .then_inc(es_ready, 1)

            def latent(b):
                dve.wait_ge(pv_done, b + 1)
                lstep_link(v.reciprocal(rdn[0:HM, 0:1], ps[0:HM, 7, P + 8:P + 9]))
                v.tensor_scalar(out=lat_h[:, bass.ds(KVR * b, KVR)], in0=ps[0:HM, 7, 256:512], scalar1=rdn[0:HM, 0:1],
                                scalar2=None, op0=ALU.mult).then_inc(lat_done, 1)

            def maxima(b):
                lstep_link(v.tensor_copy(Sc[0:NB, NPAGE, :], snew[:, bass.ds(8 * b, 8)]))
                v.tensor_reduce(out=pmx[:, :], in_=Sc[:, :, :].rearrange("p t h -> p h t"), axis=AX, op=ALU.max)\
                 .then_inc(pm_ready, 1)

            FIRST_HALF = ((4, 1), (5, 1), (6, 1), (7, 1))
            SECOND_HALF = ((0, 1), (1, 0), (1, 2), (2, 0))

            def batch(b, p, first, last):
                within[0] = 0
                base[0] = b * LSTEPS if first is False else 0
                for g in range(8):
                    if g == 0 and first:
                        lat_rows(8 * b, 0)
                    if not (last and g == 7):
                        lat_rows(8 * b + g + 1, g + 1)
                    if g == 0 and not first or g == 4:
                        dve.wait_ge(red_done, NPAGE * b + 4 * g)
                    for u in range(4):
                        if (g, u) in SECOND_HALF and not first:
                            half_scores(1, SECOND_HALF.index((g, u)))
                        if (g, u) == (2, 2) and not first:
                            maxima(b - 1)
                        if (g, u) == (3, 1) and not first:
                            softmax_diag(b - 1)
                        if (g, u) in FIRST_HALF:
                            half_scores(0, FIRST_HALF.index((g, u)))
                        if g == 4 and u == 2 and not first:
                            softmax_sum(b - 1)
                        if u == 3:
                            dve.wait_ge(s_done, 8 * b + g + 1)
                            v.tensor_copy(Sk[:, 4 * g:4 * g + 4, :],
                                          ps[:, 2, P:P + 32].rearrange("p (u n) -> p u n", u=4)).then_inc(s_read, 1)
                        dve.wait_ge(sq_done, NPAGE * b + 4 * g + u + 1)
                        v.tensor_reduce(out=ssq[:, (4 * g + u) * 8:(4 * g + u + 1) * 8],
                                        in_=sq4[:, u, :].rearrange("p (h e) -> p h e", e=NOPE), axis=AX, op=ALU.add)\
                         .then_inc(red_done, 1)
                    if not first:
                        if g == 3:
                            softmax_shift(b - 1)
                        elif g == 5:
                            latent(b - 1)
                if not last:
                    set_q(b + 2, p, lstep_link)
                return within[0]

            n0 = batch(0, 0, True, False)
            for _ in range(LSTEPS - n0):
                lstep_link(v.memset(flag[:, :], 0.0))
            with dve.Fori(0, (NB - 2) // 2) as i:
                assert batch(2 * i + 1, 1, False, False) == LSTEPS
                assert batch(2 * i + 2, 0, False, False) == LSTEPS
            batch(NB - 1, 1, False, True)
            dve.wait_ge(red_done, NPAGE * NB)
            for part in range(4):
                half_scores(1, part)
            maxima(NB - 1)
            softmax_diag(NB - 1)
            softmax_shift(NB - 1)
            softmax_sum(NB - 1)
            def signal(ins, want):
                fcount[0] += 1
                assert fcount[0] == want, (fcount[0], want)
                ins.then_inc(f_dve, 1)
                dve.wait_ge(f_dve, want)

            v.memset(SD_t[:, :], NEG)
            for b in range(NB):
                if b == 0:
                    dve.wait_ge(sdk_in[0], 48)
                if b == 6:
                    dve.wait_ge(sdk_in[1], 48)
                kv = (sdk0 if b < 6 else sdk1)[:, (b if b < 6 else b - 6) * ND:(b if b < 6 else b - 6) * ND + ND, 0:BW]
                dve.wait_ge(qb_done, b + 1)
                q0 = (1 + 2 * (b % 2)) * 512
                pr = prod[:, b % 2, :]
                v.tensor_tensor(out=pr.rearrange("p (g c) -> p g c", g=ND), in0=kv,
                                in1=psw(0, 4096)[:, q0:q0 + 768].rearrange("p (g c) -> p g c", g=ND), op=ALU.mult)\
                 .then_inc(qb_read, 1)
                dve.wait_ge(qb_read, b + 1)
                link(v.tensor_reduce(out=SD[:, b, 0:12], in_=pr.rearrange("p (n e) -> p n e", e=DH), axis=AX, op=ALU.add))
            latent(NB - 1)
            dve.wait_ge(lt_done, 1)
            v.tensor_copy(latT[:, :], ps[:, 7, 0:NB * 16]).then_inc(lt_ready, 1)
            pr = prod[0:NB, 0, :]
            link(v.tensor_tensor(out=pr.rearrange("p (g c) -> p g c", g=ND), in0=dq_s[:, :, :], in1=kv_s[:, :, 0:BW],
                                 op=ALU.mult))
            link(v.tensor_reduce(out=dn[:, 0:12], in_=pr.rearrange("p (n e) -> p n e", e=DH), axis=AX, op=ALU.add))
            link(v.tensor_tensor(out=SD[0:NB, :, 12:24], in0=rep(dn[:, 0:12], 1, NB), in1=rep(newmask, 2, 12), op=ALU.add))
            sd4 = SD_t[:, :].rearrange("p (b s h) -> p b h s", b=NB, h=HD)
            signal(v.tensor_reduce(out=dpm[:, :].rearrange("p (b h) -> p b h", b=NB), in_=sd4, axis=AX, op=ALU.max), F_MAX)
            dve.wait_ge(f_pe, 2)
            link(v.tensor_reduce(out=mx1[:, :], in_=ps[0:32, 5, 0:P], axis=AX, op=ALU.max))
            signal(v.tensor_scalar(out=dgm[:, :], in0=ident[0:32, 0:32], scalar1=mx1[:, :], scalar2=None, op0=ALU.mult),
                   F_DIAG)
            dve.wait_ge(f_pe, 3)
            signal(v.tensor_tensor(out=sd4, in0=sd4,
                                   in1=rep(ps[:, 5, 128:160].rearrange("p (b h) -> p b h", b=NB), 3, 6),
                                   op=ALU.subtract), F_SUB)
            dve.wait_ge(f_act, 1)
            ed4 = ED_t[:, :].rearrange("p (b s h) -> p b h s", b=NB, h=HD)
            link(v.memset(EZ_t[:, :], 0.0))
            ED4 = ED_t[:, :].rearrange("p (b s h) -> p b s h", b=NB, h=HD)
            v.tensor_copy(EZ_t[:, :].rearrange("p (b x) -> p b x", x=100)[:, :, 0:96]
                          .rearrange("p b (g x) -> p b g x", x=32)[:, :, :, 0:HD], ED4[:, :, 0:ND, :])
            v.tensor_copy(own_ed[:, :, :].rearrange("p g (b h) -> p b g h", h=HD), ED4[0:NB, :, ND:2 * ND, :])
            signal(v.tensor_reduce(out=dsm[:, :].rearrange("p (b h) -> p b h", b=NB), in_=ed4, axis=AX, op=ALU.add), F_SUM)
            dve.wait_ge(f_pe, 4)
            link(v.reciprocal(rl[0:32, 0:1], ps[0:32, 5, 160:161]))
            dve.wait_ge(f_pe, 5)
            signal(v.scalar_tensor_tensor(out=ob[:, :].rearrange("p (h e) -> p h e", h=HD),
                                          in0=ps[0:32, 6, 0:BW].rearrange("p (h e) -> p h e", h=HD),
                                          scalar=rl[0:32, 0:1], in1=rep(head_of, 2, DH), op0=ALU.mult, op1=ALU.mult),
                   F_OBT)
            dve.wait_ge(f_act, 2)
            link(v.tensor_tensor(out=sgm[:, :], in0=sgm[:, :], in1=mix_s[:, :], op=ALU.mult))
            v.tensor_tensor(out=og[:, 0:AW], in0=sgm[:, 0:AW], in1=ps[0:NB, 0, 0:AW], op=ALU.mult)
            dve.wait_ge(f_pe, 6)
            signal(v.tensor_tensor(out=og[:, AW:768], in0=sgm[:, AW:768], in1=ps[0:NB, 7, 0:BW], op=ALU.mult), F_OG)
            dve.wait_ge(f_pe, 7)
            signal(v.tensor_copy(osT[:, :, :], ps[:, 7, 256:304].rearrange("p (k n) -> p k n", n=NB)), F_OST)
            dve.wait_ge(f_act, 3)
            for n in range(2):
                for m, b in enumerate("AB"):
                    z = take(ITEM[f"P{b}s{n}"], NB, 512, False)
                    out = yab[:, m, n * 512:(n + 1) * 512]
                    free_stage(v.tensor_tensor(out=out, in0=z, in1=mgm[:, m * D + n * 512:m * D + (n + 1) * 512],
                                               op=ALU.mult))
            signal(v.tensor_tensor(out=yab[:, 0, :], in0=yab[:, 0, :], in1=yab[:, 1, :], op=ALU.add), F_MS)
            dve.wait_ge(f_pe, 8)
            signal(v.tensor_copy(msT[:, :, :], ps[:, 7, 320:384].rearrange("p (k n) -> p k n", n=NB)), F_MST)
            dve.wait_ge(late_in, 16)
            for n in range(2):
                z = take(ITEM[f"WOs{n}"], NB, 512, False)
                c = slice(n * 512, (n + 1) * 512)
                link(v.tensor_tensor(out=z, in0=z, in1=gate_s[:, c], op=ALU.mult))
                free_stage(v.tensor_tensor(out=xs2[:, c], in0=xs2[:, c], in1=z, op=ALU.add))
            signal(v.memset(flag[:, :], 0.0), F_Y)


def _tables():
    q, k = np.arange(P)[:, None], np.arange(P)[None, :]
    none = np.zeros((P, P), bool)
    parts = [none] * 3 + [k > q]
    for d in (4, 16):
        r = (q - k) % d != 0
        parts += [r] * 3 + [r | (k > q)]
    parts += [k < q, k > q]
    masks = np.where(np.concatenate(parts, 1), np.float32(NEG), np.float32(0))
    own = np.zeros((P, 8), np.float32)
    own[:NB] = np.where(np.eye(NB, dtype=bool), 0, np.float32(NEG))
    row = np.arange(P)[:, None]
    tab = np.concatenate([np.eye(P, dtype=np.float32), masks, own, row % HD == np.arange(HD),
                          row // HD == np.arange(NB)], 1).astype(np.float32)
    pos = np.concatenate([np.arange(S), np.full(NB, PAST)]).astype(np.float32)
    cols = []
    for half in (DH // 2, ROPE // 2):
        inv = (10000.0 ** (-np.arange(half, dtype=np.float64) / half)).astype(np.float32)
        ang = (pos[:, None] * inv[None, :]).astype(np.float32)
        c, s = np.cos(ang.astype(np.float64)), np.sin(ang.astype(np.float64))
        cols += [c, c, -s, s]
    return tab, np.concatenate(cols, 1).astype(np.float32)


def kernel(**a):
    import concourse.bacc as bacc
    from concourse.bass_utils import run_bass_kernel_spmd

    a = {k: np.asarray(v) for k, v in a.items()}
    nc = bacc.Bacc("TRN2", target_bir_lowering=False, num_devices=1)
    tab, rope = _tables()
    arrays = {
        "x_prompt": a["x_prompt"][0], "x_sample": a["x_sample"][:, 0], "cache_mla": a["cache_mla"][0],
        "cw0": a["cache_win0"][0].reshape(NB, -1, 2 * BW), "cw1": a["cache_win1"][0].reshape(NB, -1, 2 * BW),
        "cw2": a["cache_win2"][0].reshape(NB, -1, 2 * BW), "page_table": a["page_table"],
        "c_prompt": a["c_prompt"], "c_sample": a["c_sample"], "b_ada": a["b_ada"][0],
        "w_ada": a["w_ada"][0], "w_in": a["w_in"][0], "w_qb": a["w_qb"][0],
        "w_uk": a["w_uk"][0].reshape(KVR, -1), "w_uv": a["w_uv"][0].reshape(KVR, -1),
        "w_pa": a["w_pa"][0], "w_pb": a["w_pb"][0], "w_out": a["w_out"][0],
        "gains": np.concatenate([a[n][0].reshape(-1) for n in (
            "mla_kv_norm", "mla_kr_g", "mla_qn_g", "mla_kn_g", "mla_qr_g", "dil_q_g", "dil_k_g")]),
        "cols": np.concatenate([a["norm_w"][0].reshape(KD, P).T, a["mla_qa_norm"][0].reshape(3, P).T], 1),
        "tables": tab, "rope": rope,
    }
    outs = [("y_prompt", (S, D)), ("y_sample", (NB, D)), ("rows_p", (S, CW)), ("win0_p", (P, 512)),
            ("win1_p", (S, 512)), ("win2_p", (S, 512)), ("rows_s", (NB, CW)), ("win0_s", (NB, 512)),
            ("win1_s", (NB, 512)), ("win2_s", (NB, 512))]
    arrays = {f"in_{k}": np.ascontiguousarray(x) for k, x in arrays.items()}
    aps = [nc.dram_tensor(k, x.shape, mybir.dt.from_np(x.dtype), kind="ExternalInput").ap() for k, x in arrays.items()]
    aps += [nc.dram_tensor(f"out_{k}", s, F32, kind="ExternalOutput").ap() for k, s in outs]
    trunk_step(nc, *aps)
    got = run_bass_kernel_spmd(nc, [arrays], core_ids=[0]).results[0]
    o = {k: got[f"out_{k}"] for k, _ in outs}
    win = (2, HD, DH)
    return (o["y_prompt"].reshape(1, S, D), o["y_sample"].reshape(NB, 1, D), o["rows_p"].reshape(1, 1, S, CW),
            o["win0_p"].reshape(1, 1, P, *win), o["win1_p"].reshape(1, 1, S, *win), o["win2_p"].reshape(1, 1, S, *win),
            o["rows_s"].reshape(1, NB, 1, CW), o["win0_s"].reshape(1, NB, 1, *win),
            o["win1_s"].reshape(1, NB, 1, *win), o["win2_s"].reshape(1, NB, 1, *win))
```
